# Optimizing a Trainium2 kernel written in Bass

```python
import math
import jax, jax.numpy as jnp
from jax import lax
import numpy as np
import jax
import jax.numpy as jnp

D_MODEL = 1024
BATCH = 1
SEQ = 256
DEPTH = 2

HEAD_DIM = 64
N_HEADS = D_MODEL // HEAD_DIM
A_HEADS = N_HEADS // 2
A_BRANCHES = ((128, 1), (512, 4), (2048, 16))
B_HEADS = N_HEADS - A_HEADS
B_Q_RANK = D_MODEL // 4
IDX_HEADS = 8
IDX_DIM = 32
TOPK_MAX = 256
C_HEADS = N_HEADS
C_KV_HEADS = C_HEADS // 8
C_WINDOW = 128
D_FF = 2816
NUM_BUCKETS = 32
MAX_DISTANCE = 2048
BLOCK = 128
EPS = 1e-6
N_EVEN = (DEPTH + 1) // 2
N_ODD = DEPTH // 2
A_W = A_HEADS * HEAD_DIM
B_W = B_HEADS * HEAD_DIM
EVEN_SIZES = (A_W, A_W, A_W, B_Q_RANK, B_W, B_W, IDX_DIM, IDX_HEADS)
EVEN_IN = sum(EVEN_SIZES)
ODD_SIZES = (C_HEADS * HEAD_DIM, C_KV_HEADS * HEAD_DIM, C_KV_HEADS * HEAD_DIM)
ODD_IN = sum(ODD_SIZES)


F32 = jnp.float32

def _offsets(sizes):
    out, acc = [], 0
    for s in sizes[:-1]:
        acc += s
        out.append(acc)
    return out

def rmsnorm(x, g):
    xf = x.astype(F32)
    y = xf * lax.rsqrt(jnp.mean(xf * xf, axis=-1, keepdims=True) + EPS)
    return (y * g.astype(F32)).astype(x.dtype)

def swiglu(x, w1, w3, w2):
    return (jax.nn.silu(x @ w1) * (x @ w3)) @ w2

def t5_bucket(dist):
    dist = jnp.maximum(dist, 0)
    max_exact = NUM_BUCKETS // 2
    d_f = jnp.maximum(dist, 1).astype(F32)
    large = max_exact + (jnp.log(d_f / max_exact) / math.log(MAX_DISTANCE / max_exact)
                         * (NUM_BUCKETS - max_exact)).astype(jnp.int32)
    large = jnp.minimum(large, NUM_BUCKETS - 1)
    return jnp.where(dist < max_exact, dist, large)

def rel_bias(table, dist):
    return table.astype(F32)[t5_bucket(dist)]

def local_dist():
    return jnp.arange(BLOCK)[:, None] + BLOCK - jnp.arange(2 * BLOCK)[None, :]

def banded_attention(q, k, v, bias, max_dist):
    n, L, H, dh = q.shape
    hk = k.shape[2]
    g = H // hk
    nb = -(-L // BLOCK)
    lp = nb * BLOCK
    pad = lp - L
    qb = jnp.pad(q, ((0, 0), (0, pad), (0, 0), (0, 0))).reshape(n, nb, BLOCK, hk, g, dh)

    def windows(t):
        tp = jnp.pad(t, ((0, 0), (BLOCK, pad), (0, 0), (0, 0))).reshape(n, nb + 1, BLOCK, hk, dh)
        return jnp.concatenate([tp[:, :-1], tp[:, 1:]], axis=2)

    kw, vw = windows(k), windows(v)
    s = jnp.einsum('nbqhgd,nbshd->nbhgqs', qb, kw, preferred_element_type=F32) * (dh ** -0.5)
    s = s + bias.reshape(hk, g, BLOCK, 2 * BLOCK)[None, None]
    loc = local_dist()
    key_abs = jnp.arange(nb)[:, None, None] * BLOCK + jnp.arange(2 * BLOCK)[None, None, :] - BLOCK
    mask = (loc >= 0)[None] & (loc <= max_dist)[None] & (key_abs >= 0)
    s = jnp.where(mask[None, :, None, None], s, -jnp.inf)
    m = jnp.max(s, axis=-1, keepdims=True)
    p = jnp.exp(s - m)
    den = jnp.sum(p, axis=-1)
    o = jnp.einsum('nbhgqs,nbshd->nbqhgd', p, vw.astype(F32))
    o = o / jnp.transpose(den, (0, 1, 4, 2, 3))[..., None]
    lse = jnp.transpose(m[..., 0] + jnp.log(den), (0, 1, 4, 2, 3))
    o = o.reshape(n, lp, H, dh)[:, :L]
    lse = lse.reshape(n, lp, H)[:, :L]
    return o, lse

def dilated_mixture(q, k, v, table):
    bn, S, H, dh = q.shape
    outs, lses = [], []
    for window, dil in A_BRANCHES:
        ls = S // dil

        def fold(t):
            return t.reshape(bn, ls, dil, H, dh).transpose(0, 2, 1, 3, 4).reshape(bn * dil, ls, H, dh)

        bias = jnp.moveaxis(rel_bias(table, dil * local_dist()), -1, 0)
        o, lse = banded_attention(fold(q), fold(k), fold(v), bias, window // dil)
        outs.append(o.reshape(bn, dil, ls, H, dh).transpose(0, 2, 1, 3, 4).reshape(bn, S, H, dh))
        lses.append(lse.reshape(bn, dil, ls, H).transpose(0, 2, 1, 3).reshape(bn, S, H))
    wts = jax.nn.softmax(jnp.stack(lses), axis=0)
    return jnp.einsum('rbsh,rbshd->bshd', wts, jnp.stack(outs))

def dsa_attention(q, k, v, q_idx, k_idx, w_idx, table, topk):
    bn, S, H, dh = q.shape
    nb = S // BLOCK
    idx_scale = (IDX_DIM ** -0.5) * (IDX_HEADS ** -0.5)
    spos = jnp.arange(S)

    def to_blocks(t):
        return jnp.swapaxes(t.reshape((bn, nb, BLOCK) + t.shape[2:]), 0, 1)

    def one_block(args):
        qb, qib, wb, t0 = args
        tpos = t0 + jnp.arange(BLOCK)
        sc = jax.nn.relu(jnp.einsum('bqhd,bsd->bqhs', qib, k_idx, preferred_element_type=F32))
        score = jnp.einsum('bqhs,bqh->bqs', sc, wb.astype(F32)) * idx_scale
        score = jnp.where((spos[None, :] <= tpos[:, None])[None], score, -jnp.inf)
        _, idx = lax.top_k(score, topk)
        ks = jax.vmap(lambda kk, ii: kk[ii])(k, idx)
        vs = jax.vmap(lambda vv, ii: vv[ii])(v, idx)
        dist = tpos[None, :, None] - idx
        logits = jnp.einsum('bqhd,bqkhd->bqhk', qb, ks, preferred_element_type=F32) * (dh ** -0.5)
        logits = logits + jnp.moveaxis(rel_bias(table, dist), -1, 2)
        logits = jnp.where((dist >= 0)[:, :, None, :], logits, -jnp.inf)
        p = jax.nn.softmax(logits, axis=-1)
        return jnp.einsum('bqhk,bqkhd->bqhd', p, vs.astype(F32))

    t0s = jnp.arange(nb, dtype=jnp.int32) * BLOCK
    out = lax.map(one_block, (to_blocks(q), to_blocks(q_idx), to_blocks(w_idx), t0s))
    return jnp.swapaxes(out, 0, 1).reshape(bn, S, H, dh)

def hybrid_ab_mixer(u, table, w_in, cq_g, wq_b, wq_idx, w_out):
    bn, S, _ = u.shape
    proj = u @ w_in
    qa, ka, va, cq, kb, vb, k_idx, w_idx = jnp.split(proj, _offsets(EVEN_SIZES), axis=-1)
    hs = (bn, S, A_HEADS, HEAD_DIM)
    o_a = dilated_mixture(qa.reshape(hs), ka.reshape(hs), va.reshape(hs), table[:, :A_HEADS])
    cq = rmsnorm(cq, cq_g)
    hb = (bn, S, B_HEADS, HEAD_DIM)
    qb = (cq @ wq_b).reshape(hb)
    q_idx = (cq @ wq_idx).reshape(bn, S, IDX_HEADS, IDX_DIM)
    topk = min(TOPK_MAX, S // 4)
    o_b = dsa_attention(qb, kb.reshape(hb), vb.reshape(hb), q_idx, k_idx, w_idx,
                        table[:, A_HEADS:], topk)
    o = jnp.concatenate([o_a.reshape(bn, S, A_W), o_b.reshape(bn, S, B_W)], axis=-1)
    return o.astype(u.dtype) @ w_out

def swa_sink_mixer(u, table, w_in, sinks, w_out):
    bn, S, _ = u.shape
    q, k, v = jnp.split(u @ w_in, _offsets(ODD_SIZES), axis=-1)
    q = q.reshape(bn, S, C_HEADS, HEAD_DIM)
    k = k.reshape(bn, S, C_KV_HEADS, HEAD_DIM)
    v = v.reshape(bn, S, C_KV_HEADS, HEAD_DIM)
    bias = jnp.moveaxis(rel_bias(table, local_dist()), -1, 0)
    o, lse = banded_attention(q, k, v, bias, C_WINDOW - 1)
    o = o * jax.nn.sigmoid(lse - sinks.astype(F32))[..., None]
    return o.reshape(bn, S, C_HEADS * HEAD_DIM).astype(u.dtype) @ w_out

def first_inputs(seed: int = 0) -> dict:
    key = jax.random.key(seed)
    ks = jax.random.split(key, 20)
    nrm = lambda k, shape, scale: jax.random.normal(k, shape, F32) * scale
    return {
        "x": nrm(ks[0], (BATCH, SEQ, D_MODEL), 1.0),
        "norm_g": 1.0 + nrm(ks[1], (DEPTH, 3, D_MODEL), 0.02),
        "final_g": 1.0 + nrm(ks[2], (D_MODEL,), 0.02),
        "rel_bias_table": nrm(ks[3], (NUM_BUCKETS, N_HEADS), 0.2),
        "ffn_w1": nrm(ks[4], (DEPTH, 2, D_MODEL, D_FF), D_MODEL ** -0.5),
        "ffn_w3": nrm(ks[5], (DEPTH, 2, D_MODEL, D_FF), D_MODEL ** -0.5),
        "ffn_w2": nrm(ks[6], (DEPTH, 2, D_FF, D_MODEL), D_FF ** -0.5),
        "hyb_w_in": nrm(ks[7], (N_EVEN, D_MODEL, EVEN_IN), D_MODEL ** -0.5),
        "hyb_cq_g": 1.0 + nrm(ks[8], (N_EVEN, B_Q_RANK), 0.02),
        "hyb_wq_b": nrm(ks[9], (N_EVEN, B_Q_RANK, B_W), B_Q_RANK ** -0.5),
        "hyb_wq_idx": nrm(ks[10], (N_EVEN, B_Q_RANK, IDX_HEADS * IDX_DIM), B_Q_RANK ** -0.5),
        "hyb_w_out": nrm(ks[11], (N_EVEN, A_W + B_W, D_MODEL), (A_W + B_W) ** -0.5),
        "swa_w_in": nrm(ks[12], (N_ODD, D_MODEL, ODD_IN), D_MODEL ** -0.5),
        "swa_sinks": nrm(ks[13], (N_ODD, C_HEADS), 1.0),
        "swa_w_out": nrm(ks[14], (N_ODD, C_HEADS * HEAD_DIM, D_MODEL), (C_HEADS * HEAD_DIM) ** -0.5),
    }

def first_block(x, norm_g, final_g, rel_bias_table, ffn_w1, ffn_w3, ffn_w2, hyb_w_in, hyb_cq_g,
              hyb_wq_b, hyb_wq_idx, hyb_w_out, swa_w_in, swa_sinks, swa_w_out):
    h = x
    for layer in range(DEPTH):
        g = norm_g[layer]
        h = h + 0.5 * swiglu(rmsnorm(h, g[0]), ffn_w1[layer, 0], ffn_w3[layer, 0], ffn_w2[layer, 0])
        u = rmsnorm(h, g[1])
        i = layer // 2
        if layer % 2 == 0:
            mix = hybrid_ab_mixer(u, rel_bias_table, hyb_w_in[i], hyb_cq_g[i], hyb_wq_b[i],
                                  hyb_wq_idx[i], hyb_w_out[i])
        else:
            mix = swa_sink_mixer(u, rel_bias_table, swa_w_in[i], swa_sinks[i], swa_w_out[i])
        h = h + mix
        h = h + 0.5 * swiglu(rmsnorm(h, g[2]), ffn_w1[layer, 1], ffn_w3[layer, 1], ffn_w2[layer, 1])
    return rmsnorm(h, final_g)


GRID_W = 64
CTX_LEN = 256
NA_HEADS = 6
NA_WIN_R = 8
NA_WIN_C = 16
SG_GROUPS = 4
SG_CHUNK = 128
GQA_Q_HEADS = 6
GQA_KV_HEADS = 2
Q_BLOCK = 128
ROPE_THETA = 10000.0

D_A = NA_HEADS * HEAD_DIM
D_B = SG_GROUPS * HEAD_DIM
D_C = GQA_Q_HEADS * HEAD_DIM
D_MIX = D_A + D_B + D_C
D_KV_C = GQA_KV_HEADS * HEAD_DIM
IN_SIZES = (D_A, D_A, D_A, 2 * D_B, D_C, D_KV_C, D_KV_C)
D_IN = 3 * D_A + 2 * D_B + D_C + 2 * D_KV_C
D_FF_2 = int(math.ceil(8 * D_MODEL / 3 / 256)) * 256
N_MOD = 6
ALPHA = (2 * DEPTH) ** 0.25
BETA = (8 * DEPTH) ** -0.25
LN_EPS = 1e-6


def layer_norm(x):
    xf = x.astype(jnp.float32)
    mu = jnp.mean(xf, -1, keepdims=True)
    var = jnp.mean(jnp.square(xf - mu), -1, keepdims=True)
    return ((xf - mu) * lax.rsqrt(var + LN_EPS)).astype(x.dtype)

def rms_norm(x, g):
    xf = x.astype(jnp.float32)
    y = xf * lax.rsqrt(jnp.mean(xf * xf, -1, keepdims=True) + LN_EPS)
    return y.astype(x.dtype) * g

def modulate(x, shift, scale):
    return layer_norm(x) * (1 + scale) + shift

def split_cols(p, sizes):
    out, off = [], 0
    for s in sizes:
        out.append(p[..., off:off + s])
        off += s
    return out

def heads(t, n):
    return t.reshape(t.shape[0], t.shape[1], n, HEAD_DIM)

def axial_rope_tables(n_tokens, dtype):
    t = jnp.arange(n_tokens, dtype=jnp.int32)
    row = (t // GRID_W).astype(jnp.float32)
    col = (t % GRID_W).astype(jnp.float32)
    n_freq = HEAD_DIM // 4
    inv = 1.0 / (ROPE_THETA ** (jnp.arange(n_freq, dtype=jnp.float32) / n_freq))
    ang = jnp.stack([row[:, None] * inv, col[:, None] * inv], axis=1)
    return jnp.cos(ang).astype(dtype), jnp.sin(ang).astype(dtype)

def apply_axial_rope(x, cos, sin):
    n_freq = HEAD_DIM // 4
    xr = x.reshape(*x.shape[:-1], 2, 2, n_freq)
    x1, x2 = xr[..., 0, :], xr[..., 1, :]
    c, s = cos[:, None], sin[:, None]
    out = jnp.stack([x1 * c - x2 * s, x2 * c + x1 * s], axis=-2)
    return out.reshape(x.shape)

def attend(q, k, v):
    scale = q.shape[-1] ** -0.5
    s = jnp.einsum('bqkgd,bskd->bkgqs', q, k) * scale
    p = jax.nn.softmax(s.astype(jnp.float32), axis=-1).astype(v.dtype)
    return jnp.einsum('bkgqs,bskd->bqkgd', p, v)

def neighbourhood_attention(q, k, v, k_ctx, v_ctx, rpb):
    B, S, H, Dh = q.shape
    rows = S // GRID_W
    kr = min(NA_WIN_R, rows)
    kcw = NA_WIN_C
    scale = Dh ** -0.5
    qg = q.reshape(B, rows, GRID_W, H, Dh)
    kg = k.reshape(B, rows, GRID_W, H, Dh)
    vg = v.reshape(B, rows, GRID_W, H, Dh)
    r_idx = jnp.arange(rows, dtype=jnp.int32)
    row_start = jnp.clip(r_idx - kr // 2, 0, rows - kr)
    c_idx = jnp.arange(GRID_W, dtype=jnp.int32)
    col_start = jnp.clip(c_idx - kcw // 2, 0, GRID_W - kcw)
    col_win = col_start[:, None] + jnp.arange(kcw, dtype=jnp.int32)[None, :]
    dc = col_win - c_idx[:, None] + (NA_WIN_C - 1)
    n_loc = kr * kcw

    def one_row(args):
        q_row, rs, r = args
        k_rows = lax.dynamic_slice_in_dim(kg, rs, kr, axis=1)
        v_rows = lax.dynamic_slice_in_dim(vg, rs, kr, axis=1)
        k_win = k_rows[:, :, col_win]
        v_win = v_rows[:, :, col_win]
        s_loc = jnp.einsum('bqhd,brqchd->bhqrc', q_row, k_win) * scale
        dr = rs + jnp.arange(kr, dtype=jnp.int32) - r + (NA_WIN_R - 1)
        bias = rpb[:, dr][:, :, dc]
        s_loc = s_loc + jnp.transpose(bias, (0, 2, 1, 3))[None]
        s_ctx = jnp.einsum('bqhd,blhd->bhql', q_row, k_ctx) * scale
        s = jnp.concatenate([s_loc.reshape(B, H, GRID_W, n_loc), s_ctx], axis=-1)
        p = jax.nn.softmax(s.astype(jnp.float32), axis=-1).astype(v.dtype)
        p_loc = p[..., :n_loc].reshape(B, H, GRID_W, kr, kcw)
        p_ctx = p[..., n_loc:]
        return (jnp.einsum('bhqrc,brqchd->bqhd', p_loc, v_win)
                + jnp.einsum('bhql,blhd->bqhd', p_ctx, v_ctx))

    out = lax.map(one_row, (jnp.transpose(qg, (1, 0, 2, 3, 4)), row_start, r_idx))
    return jnp.transpose(out, (1, 0, 2, 3, 4)).reshape(B, S, H, Dh)

def gqa_latent(q, k, v, k_ctx, v_ctx):
    B, S, Hq, Dh = q.shape
    G = Hq // GQA_KV_HEADS
    nb = S // Q_BLOCK
    qb = jnp.transpose(q.reshape(B, nb, Q_BLOCK, GQA_KV_HEADS, G, Dh), (1, 0, 2, 3, 4, 5))
    k_all = jnp.concatenate([k, k_ctx], axis=1)
    v_all = jnp.concatenate([v, v_ctx], axis=1)
    out = lax.map(lambda qblk: attend(qblk, k_all, v_all), qb)
    return jnp.transpose(out, (1, 0, 2, 3, 4, 5)).reshape(B, S, Hq, Dh)

def spatial_gating(z, w_s, b_s, g_sgu):
    B, N, _ = z.shape
    u, v = z[..., :D_B], z[..., D_B:]
    v = layer_norm(v) * g_sgu
    vc = v.reshape(B, N // SG_CHUNK, SG_CHUNK, SG_GROUPS, HEAD_DIM)
    mixed = jnp.einsum('gpq,bnqgc->bnpgc', w_s, vc) + jnp.transpose(b_s)[None, None, :, :, None]
    return u * mixed.reshape(B, N, D_B)

def merge_groups(o_a, o_b, o_c, g_out):
    B, N = o_b.shape[0], o_b.shape[1]
    return jnp.concatenate([
        rms_norm(o_a.reshape(B, N, D_A), g_out[:D_A]),
        rms_norm(o_b, g_out[D_A:D_A + D_B]),
        rms_norm(o_c.reshape(B, N, D_C), g_out[D_A + D_B:]),
    ], axis=-1)

def mixing_sublayer(h, hc, w_in, rpb, w_s, b_s, g_sgu, g_q, g_k, g_out, w_o, need_ctx_out):
    B, S, _ = h.shape
    qa, ka, va, zb, qc, kc, vc = split_cols(h @ w_in, IN_SIZES)
    qa_x, ka_x, va_x, zb_x, qc_x, kc_x, vc_x = split_cols(hc @ w_in, IN_SIZES)
    cos, sin = axial_rope_tables(S, h.dtype)
    ka_x, va_x = heads(ka_x, NA_HEADS), heads(va_x, NA_HEADS)
    kc_x = rms_norm(heads(kc_x, GQA_KV_HEADS), g_k)
    vc_x = heads(vc_x, GQA_KV_HEADS)
    o_a = neighbourhood_attention(heads(qa, NA_HEADS), heads(ka, NA_HEADS), heads(va, NA_HEADS),
                                  ka_x, va_x, rpb)
    o_b = spatial_gating(jax.nn.gelu(zb), w_s, b_s, g_sgu)
    q_c = apply_axial_rope(rms_norm(heads(qc, GQA_Q_HEADS), g_q), cos, sin)
    k_c = apply_axial_rope(rms_norm(heads(kc, GQA_KV_HEADS), g_k), cos, sin)
    o_c = gqa_latent(q_c, k_c, heads(vc, GQA_KV_HEADS), kc_x, vc_x)
    y = merge_groups(o_a, o_b, o_c, g_out) @ w_o
    if not need_ctx_out:
        return y, None
    L = hc.shape[1]
    o_ax = attend(heads(qa_x, NA_HEADS)[:, :, :, None], ka_x, va_x)
    o_bx = spatial_gating(jax.nn.gelu(zb_x), w_s, b_s, g_sgu)
    q_cx = rms_norm(heads(qc_x, GQA_Q_HEADS), g_q).reshape(
        B, L, GQA_KV_HEADS, GQA_Q_HEADS // GQA_KV_HEADS, HEAD_DIM)
    o_cx = attend(q_cx, kc_x, vc_x)
    yc = merge_groups(o_ax, o_bx, o_cx, g_out) @ w_o
    return y, yc

def swiglu_2(h, w_in, w_out):
    a, b = h @ w_in[:, :D_FF_2], h @ w_in[:, D_FF_2:]
    return (jax.nn.silu(a) * b) @ w_out

def second_inputs(seed: int = 0) -> dict:
    key = jax.random.key(seed)
    ks = jax.random.split(key, 24)
    n = jax.random.normal
    f = jnp.float32
    return {
        "x": n(ks[0], (BATCH, SEQ, D_MODEL), f),
        "c": n(ks[1], (BATCH, D_MODEL), f),
        "ctx": n(ks[2], (BATCH, CTX_LEN, D_MODEL), f),
        "c_ctx": n(ks[3], (D_MODEL,), f),
        "w_mod": n(ks[4], (DEPTH, D_MODEL, N_MOD * D_MODEL), f) * (0.5 * D_MODEL ** -0.5),
        "b_mod": n(ks[5], (DEPTH, N_MOD * D_MODEL), f) * 0.02,
        "w_in": n(ks[6], (DEPTH, D_MODEL, D_IN), f) * D_MODEL ** -0.5,
        "rpb": n(ks[7], (DEPTH, NA_HEADS, 2 * NA_WIN_R - 1, 2 * NA_WIN_C - 1), f) * 0.02,
        "w_s": n(ks[8], (DEPTH, SG_GROUPS, SG_CHUNK, SG_CHUNK), f) * SG_CHUNK ** -0.5,
        "b_s": n(ks[9], (DEPTH, SG_GROUPS, SG_CHUNK), f) * 0.02,
        "g_sgu": 1.0 + 0.02 * n(ks[10], (DEPTH, D_B), f),
        "g_q": 1.0 + 0.02 * n(ks[11], (DEPTH, HEAD_DIM), f),
        "g_k": 1.0 + 0.02 * n(ks[12], (DEPTH, HEAD_DIM), f),
        "g_out": 1.0 + 0.02 * n(ks[13], (DEPTH, D_MIX), f),
        "w_o": n(ks[14], (DEPTH, D_MIX, D_MODEL), f) * (D_MIX ** -0.5 * BETA),
        "ln1_g": 1.0 + 0.02 * n(ks[15], (DEPTH, D_MODEL), f),
        "ln1_b": 0.02 * n(ks[16], (DEPTH, D_MODEL), f),
        "w_ffn_in": n(ks[17], (DEPTH, D_MODEL, 2 * D_FF_2), f) * D_MODEL ** -0.5,
        "w_ffn_out": n(ks[18], (DEPTH, D_FF_2, D_MODEL), f) * (D_FF_2 ** -0.5 * BETA),
        "ln2_g": 1.0 + 0.02 * n(ks[19], (DEPTH, D_MODEL), f),
        "ln2_b": 0.02 * n(ks[20], (DEPTH, D_MODEL), f),
    }

def second_block(x, c, ctx, c_ctx, w_mod, b_mod, w_in, rpb, w_s, b_s, g_sgu, g_q, g_k, g_out, w_o,
              ln1_g, ln1_b, w_ffn_in, w_ffn_out, ln2_g, ln2_b):
    sc = jax.nn.silu(c)
    sc_ctx = jax.nn.silu(c_ctx)
    for l in range(DEPTH):
        need_ctx_out = l < DEPTH - 1
        mod = split_cols((sc @ w_mod[l] + b_mod[l])[:, None, :], (D_MODEL,) * N_MOD)
        mod_x = split_cols(sc_ctx @ w_mod[l] + b_mod[l], (D_MODEL,) * N_MOD)
        sh1, sc1, g1, sh2, sc2, g2 = mod
        sh1x, sc1x, g1x, sh2x, sc2x, g2x = mod_x
        h = modulate(x, sh1, sc1)
        hc = modulate(ctx, sh1x, sc1x)
        y, yc = mixing_sublayer(h, hc, w_in[l], rpb[l], w_s[l], b_s[l], g_sgu[l], g_q[l], g_k[l],
                                g_out[l], w_o[l], need_ctx_out)
        x = layer_norm(ALPHA * x + g1 * y) * ln1_g[l] + ln1_b[l]
        x = layer_norm(ALPHA * x + g2 * swiglu_2(modulate(x, sh2, sc2), w_ffn_in[l], w_ffn_out[l])) \
            * ln2_g[l] + ln2_b[l]
        if need_ctx_out:
            ctx = layer_norm(ALPHA * ctx + g1x * yc) * ln1_g[l] + ln1_b[l]
            ctx = layer_norm(ALPHA * ctx + g2x * swiglu_2(modulate(ctx, sh2x, sc2x), w_ffn_in[l],
                                                         w_ffn_out[l])) * ln2_g[l] + ln2_b[l]
    return x


def setup_inputs(seed=0):
    out = dict(first_inputs(seed))
    for name, value in second_inputs(seed + 1).items():
        if name != "x":
            out[name + "_2"] = value
    return out


def reference(
    x, norm_g, final_g, rel_bias_table, ffn_w1, ffn_w3, ffn_w2, hyb_w_in, hyb_cq_g, hyb_wq_b,
    hyb_wq_idx, hyb_w_out, swa_w_in, swa_sinks, swa_w_out, c_2, ctx_2, c_ctx_2, w_mod_2,
    b_mod_2, w_in_2, rpb_2, w_s_2, b_s_2, g_sgu_2, g_q_2, g_k_2, g_out_2, w_o_2, ln1_g_2,
    ln1_b_2, w_ffn_in_2, w_ffn_out_2, ln2_g_2, ln2_b_2,
):
    x = first_block(
        x, norm_g, final_g, rel_bias_table, ffn_w1, ffn_w3, ffn_w2, hyb_w_in, hyb_cq_g,
        hyb_wq_b, hyb_wq_idx, hyb_w_out, swa_w_in, swa_sinks, swa_w_out,
    )
    return second_block(
        x, c_2, ctx_2, c_ctx_2, w_mod_2, b_mod_2, w_in_2, rpb_2, w_s_2, b_s_2, g_sgu_2, g_q_2,
        g_k_2, g_out_2, w_o_2, ln1_g_2, ln1_b_2, w_ffn_in_2, w_ffn_out_2, ln2_g_2, ln2_b_2,
    )


_drawn_inputs = setup_inputs


def setup_inputs(seed=0):
    import zlib

    import numpy as np

    out = dict(_drawn_inputs(seed))
    spreads = {}
    factors = {'final_g': 2.779,
     'hyb_cq_g': 3.558,
     'swa_sinks': 4.459,
     'b_mod_2': 3.31,
     'rpb_2': 8.0,
     'b_s_2': 8.0,
     'g_sgu_2': 8.0,
     'g_q_2': 8.0,
     'g_k_2': 8.0,
     'g_out_2': 8.0}
    for name, (base, spread) in spreads.items():
        noise = np.random.default_rng([zlib.crc32(name.encode()), seed]).standard_normal(out[name].shape)
        drawn = base * np.exp(spread * noise) if base else spread * noise
        out[name] = jnp.asarray(drawn.astype(out[name].dtype))
    for name, factor in factors.items():
        out[name] = (out[name] * factor).astype(out[name].dtype)
    return out
```

```python
import math
from contextlib import ExitStack

import numpy as np

import concourse.bass as bass
from concourse import mybir

F32 = mybir.dt.float32
ALU = mybir.AluOpType
ACT = mybir.ActivationFunctionType
AX = mybir.AxisListType

P = 128
D = 1024
KT = D // P
S = 256
FF = 2816
FB = FF // P
HD = 64
EPS = 1e-6
ALPHA = 4.0 ** 0.25
QSCALE = HD ** -0.5
NEG = -1.0e30
TAKEN = -3.0e38
TOPK = 64
UC = 384
UNIT = KT * UC
RING = 4
IDX_SCALE = (32 ** -0.5) * (8 ** -0.5)
GELU_C = 2.0 * math.sqrt(2.0 / math.pi)

VEC_PARTS = [("norm_g", 48), ("final_g", 8), ("cq_g", 2), ("b_mod", 96), ("g_sgu", 4), ("g_q", 2), ("g_k", 2),
             ("g_out", 16), ("ln1_g", 16), ("ln1_b", 16), ("ln2_g", 16), ("ln2_b", 16), ("cond", 16)]
VEC = {}
_at = 0
for _name, _n in VEC_PARTS:
    VEC[_name] = _at
    _at += _n
NVEC = _at
CONST_PARTS = [("ident", 128), ("ones", 128), ("halves", 128), ("swap", 128), ("mask_mix", 256),
               ("mask_causal", 256), ("mask_swa", 256), ("mask_na", 64), ("cos", 256), ("sin", 256)]
CONST = {}
_at = 0
for _name, _n in CONST_PARTS:
    CONST[_name] = _at
    _at += _n
NCONST = _at


def constants():
    c = np.zeros((P, NCONST), np.float32)

    def put(name, a):
        c[:, CONST[name]:CONST[name] + a.shape[1]] = a

    put("ident", np.eye(P, dtype=np.float32))
    put("ones", np.ones((P, P), np.float32))
    half = np.arange(P) // HD
    put("halves", (half[:, None] == half[None, :]).astype(np.float32))
    swap = np.zeros((P, P), np.float32)
    for m in range(P):
        if m % 32 < 16:
            swap[m + 16, m] = -1.0
        else:
            swap[m - 16, m] = 1.0
    put("swap", swap)
    dist = 255 - np.arange(P)[:, None] - np.arange(S)[None, :]
    count = (dist <= 128).astype(int) + (dist % 4 == 0) + (dist % 16 == 0)
    ok = (dist >= 0) & (count > 0)
    put("mask_mix", np.where(ok, np.log(np.maximum(count, 1).astype(np.float64)), NEG).astype(np.float32))
    put("mask_causal", np.where(dist >= 0, 0.0, NEG).astype(np.float32))
    put("mask_swa", np.where((dist >= 0) & (dist <= 127), 0.0, NEG).astype(np.float32))
    col = 63 - np.arange(P) % 64
    start = np.clip(col - 8, 0, 48)
    key = np.arange(64)[None, :]
    put("mask_na", np.where((key >= start[:, None]) & (key < start[:, None] + 16), 0.0, NEG).astype(np.float32))
    t = np.arange(S)
    inv = (1.0 / (np.float32(10000.0) ** (np.arange(16, dtype=np.float32) / np.float32(16)))).astype(np.float32)
    pos = np.stack([t // 64, t % 64]).astype(np.float32)
    feature = np.arange(P) % HD
    ang = pos[feature // 32] * inv[feature % 16][:, None]
    put("cos", np.cos(ang.astype(np.float32)).astype(np.float32))
    put("sin", np.sin(ang.astype(np.float32)).astype(np.float32))
    return c


def bucket_rows():
    d = np.maximum(255 - np.arange(384), 0)
    f = np.maximum(d, 1).astype(np.float32)
    large = 16 + (np.log(f / np.float32(16)) / np.float32(math.log(2048 / 16)) * np.float32(16)).astype(np.int32)
    b = np.where(d < 16, d, np.minimum(large, 31))
    return (np.arange(32)[:, None] == b[None, :]).astype(np.float32)


class Count:

    def __init__(self):
        self.n = {}

    def take(self, name, n):
        base = self.n.get(name, 0)
        self.n[name] = base + n
        return base


def tiles_cols(n):
    return -(-n // UC)


def build_program(nc, a):
    with ExitStack() as ctx:
        def sb(name, shape):
            return ctx.enter_context(nc.sbuf_tensor(name, shape, F32))

        def bank(name):
            return ctx.enter_context(nc.psum_tensor(name, [P, 512], F32))

        sems = {}

        def sem(name):
            if name not in sems:
                sems[name] = ctx.enter_context(nc.semaphore(name))
            return sems[name]

        X = sb("resid", [P, KT, 2 * S])
        N = sb("normed", [P, KT, 2 * S])
        ring = [sb(f"unit{i}", [P, UNIT]) for i in range(RING)]
        SQ = sb("squares", [P, KT, S])
        RS = sb("rstd", [P, 3, S])
        SC = sb("scratch", [P, 6144])
        PJ = sb("proj", [P, 12, 2 * S])
        VT = sb("values", [P, 4, 512])
        ZV = sb("gate_v", [P, 4, 256])
        BT = sb("bias", [P, 16, 256])
        vec = sb("vec", [P, NVEC])
        con = sb("con", [P, NCONST])
        WS = sb("gate_w", [P, 2, 4, P])
        BS = sb("gate_b", [P, 2, 2, P])
        MOD = sb("mod", [P, 2, 48, 2])
        small = sb("small", [P, 256])
        OH = SC[0:32, 0:384]
        TB = SC[0:32, 384:400]
        ROW = SC[0:16, 512:896]

        acc = [bank(f"acc{i}") for i in range(4)]
        up = [bank(f"up{i}") for i in range(2)]
        stat = [bank(f"stat{i}") for i in range(2)]

        mean_bank = up[0]
        sum_bank = [stat[0], stat[1], up[1]]
        head_bank = [up[0], up[1], stat[0], stat[1]]

        def cst(name, n=None):
            return con[:, CONST[name]:CONST[name] + (n or dict(CONST_PARTS)[name])]

        def v(name, i):
            return vec[:, VEC[name] + i:VEC[name] + i + 1]

        ident, ones = cst("ident"), cst("ones")
        eps = small[:, 0:1]
        sinks = small[:, 16:32]
        GQ = small[:, 32:34]
        WX = small[:, 40:56].rearrange("p (i h) -> p i h", i=2)
        CS = small[:, 64:80].rearrange("p (s k) -> p k s", s=2)
        CTMP = small[:, 80:96]
        ATT = small[:, 96:96 + 24].rearrange("p (b n) -> p b n", b=3)
        LNS = small[:, 128:160].rearrange("p (t n) -> p t n", t=4)

        fE = [SC[:, i * 256:(i + 1) * 256] for i in range(2)]
        fG = [SC[:, 512 + i * 256:768 + i * 256] for i in range(2)]
        fT = [SC[:, 1024 + i * 256:1280 + i * 256] for i in range(2)]
        aS = [SC[:, i * 512:(i + 1) * 512] for i in range(3)]
        aP = [SC[:, 1536 + i * 512:2048 + i * 512] for i in range(3)]
        aT = [SC[:, 3072 + i * 1024:4096 + i * 1024].rearrange("p (s t) -> p s t", s=4) for i in range(2)]
        SEL = SC[:, 5120:5632].rearrange("p (i s) -> p i s", i=2)
        SCORE = SC[:, 5632:6144].rearrange("p (i s) -> p i s", i=2)
        RELU = [SC[:, i * 256:(i + 1) * 256] for i in range(2)]
        QI = SQ
        PJE = PJ[:, :, :].rearrange("p b (u t) -> p (b u) t", u=2)
        VTE = VT[:, :, :].rearrange("p (i u) n -> p i (u n)", u=2)
        NAB = BT[:, 0:12, :].rearrange("p (i h) s -> p i h s", i=2)

        scratch_rows = nc.dram_tensor("bias_rows", (16, 384), F32).ap()

        def rev(ap):
            return ap[:, ::-1]

        cnt = Count()
        stages = []
        loads = []

        def add_units(name, start, n):
            loads.append((a[name], start, n))
            return cnt.take("unit", n)

        def src_wait(*pairs):
            return list(pairs)

        def norm(kind, groups, src, dst, gain, shift, ready, centred=None):
            nb = sum(len(g) for g in groups)
            st = dict(kind="norm", ln=kind == "ln", groups=groups, src=src, dst=dst, gain=gain, shift=shift,
                      ready=ready, centred=centred, nb=nb, sq=cnt.take("sq", nb), ss=cnt.take("ss", len(groups)),
                      rstd=cnt.take("rstd", len(groups)))
            if st["ln"]:
                st["mean"] = cnt.take("mean", 1)
                st["cen"] = cnt.take("cen", nb)
                st["scaled"] = cnt.take("scaled", nb)
            st["out_sem"] = "ln_out" if st["ln"] else "rms_out"
            st["out"] = cnt.take(st["out_sem"], nb)
            st["rstd_free"] = cnt.n["rms_out"] - (0 if st["ln"] else nb) if "rms_out" in cnt.n else 0
            stages.append(st)
            return (st["out_sem"], st["out"] + nb)

        def ffn(units, tok, ready, resid):
            st = dict(kind="ffn", tok=tok, ready=ready, resid=resid, unit=add_units(*units, FB),
                      up=cnt.take("up", FB), exp=cnt.take("ffn_exp", FB), gated=cnt.take("gated", FB),
                      scaled=cnt.take("alpha", KT if resid else 0), res=cnt.take("resid", 8))
            stages.append(st)
            return ("resid", st["res"] + 8)

        def proj(jobs, units, ready):
            base = add_units(*units)
            last = {}
            for j, job in enumerate(jobs):
                last[job["unit"]] = j
            for j, job in enumerate(jobs):
                job["slot"] = base + job["unit"]
                job["last"] = last[job["unit"]] == j
                job["done"] = ("unit_used", base + job["unit"] + 1) if job["last"] else \
                    ("proj", cnt.take("proj", 1) + 1)
                e = job["evac"]
                name = "resid" if e[0] == "resid" else {"act": "evac_act", "dve": "evac_dve"}[job["eng"]]
                job["out"] = (name, cnt.take(name, 1) + 1)
                if e[0] == "resid" and e[1] is not None:
                    job["scaled"] = cnt.take("alpha", 1) + 1
            st = dict(kind="proj", jobs=jobs, ready=ready)
            stages.append(st)
            return [(n, max(j["out"][1] for j in jobs if j["out"][0] == n)) for n in {j["out"][0] for j in jobs}]

        def other(kind, sizes, **kw):
            st = dict(kind=kind, **kw)
            for name, n in sizes.items():
                st[name] = cnt.take(name, n)
            stages.append(st)
            return st

        def alternate(jobs):
            for j, job in enumerate(jobs):
                job.setdefault("eng", "act" if j % 2 == 0 else "dve")
            return jobs

        def in_block(b, tok=0, n=S):
            return lambda b_, t=tok: X[:, b_, t:t + n]

        def xs(tok):
            return lambda b: X[:, b, tok:tok + S]

        def ns(tok):
            return lambda b: N[:, b, tok:tok + S]

        def feature_job(unit, off, m, dst, q, n=S, tok=0, src=None, kts=KT, kstep=UC):
            return dict(unit=unit, off=off, m=m, kts=kts, kstep=kstep, tm=False, n=n, dst=dst,
                        src=src or (lambda k: N[:, k, tok:tok + n]), evac=("q" if q else "copy",))

        def token_job(unit, off, n, tile, dst):
            return dict(unit=unit, off=off, m=P, kts=KT, kstep=UC, tm=True, n=n, dst=dst,
                        src=lambda k: N[:, k, tile * P:(tile + 1) * P], evac=("copy",))

        def out_jobs(toks, gain):
            jobs = []
            for b in range(KT):
                for t in toks:
                    jobs.append(dict(unit=b // 3, off=(b % 3) * P, m=P, kts=KT, kstep=UC, tm=False, n=S,
                                     dst=X[:, b, t:t + S], src=lambda k, t=t: N[:, k, t:t + S],
                                     evac=("resid", gain(b, t)), eng="dve"))
            return jobs

        def attention(pairs, **kw):
            tiles = []
            for n, pr in enumerate(pairs):
                for h in range(2):
                    for i in range(2):
                        tiles.append((n, h, i))
            return other("attn", dict(att_s=len(tiles), att_m=len(tiles), att_e=len(tiles), att_n=len(tiles),
                                      att_t=len(tiles), att_c=len(tiles), att_o=2 * len(pairs),
                                      att_out=len(pairs), att_add=len(tiles)),
                         pairs=pairs, tiles=tiles, **kw)

        x_ready = [("load_x", 16), ("load_con", 32)]
        for layer in range(2):
            ng = lambda j, layer=layer: (lambda b: v("norm_g", (layer * 3 + j) * 8 + b))
            r = norm("rms", [range(KT)], xs(0), ns(0), ng(0), None, x_ready if layer == 0 else [r])
            r = ffn(("ffn_units", (2 * layer) * FB), 0, [r], None)
            r = norm("rms", [range(KT)], xs(0), ns(0), ng(1), None, [r])
            if layer == 0:
                jobs = []
                for b in range(8):
                    jobs.append(feature_job(b // 3, (b % 3) * P, P, PJE[:, b, :], b < 4))
                for i in range(2):
                    jobs.append(token_job(2, 256, 128, i, VTE[:, i, 0:128]))
                for i in range(2):
                    jobs.append(token_job(3, 0, 384, i, VTE[:, i, 128:512]))
                for b in range(2):
                    jobs.append(feature_job(4, b * P, P, PJE[:, 16 + b, :], False))
                for b in range(4):
                    jobs.append(feature_job(4 + (b + 2) // 3, ((b + 2) % 3) * P, P, PJE[:, 8 + b, :], False))
                for i in range(2):
                    jobs.append(token_job(6, 0, 384, i, VTE[:, i, 512:896]))
                for i in range(2):
                    jobs.append(token_job(7, 0, 128, i, VTE[:, i, 896:1024]))
                jobs.append(feature_job(7, 128, 32, PJE[0:32, 20, :], False))
                wx = feature_job(7, 160, 8, PJE[0:8, 21, :], False)
                wx["evac"] = ("reverse", IDX_SCALE)
                jobs.append(wx)
                w = proj(alternate(jobs), ("even_units", 0, 8), [r])
                r = norm("rms", [range(2)], lambda b: PJE[:, 16 + b, :], lambda b: PJE[:, 18 + b, :],
                         lambda b: v("cq_g", b), None, w)
                cq = lambda k: PJE[:, 18 + k, :]
                jobs = [feature_job(0, b * P, P, PJE[:, 12 + b, :], True, src=cq, kts=2, kstep=512)
                        for b in range(4)]
                for h in range(8):
                    j = feature_job(0, 1024 + h * 32, 32, QI[0:32, h, :], False, src=cq, kts=2, kstep=256)
                    j["evac"] = ("reverse", 1.0)
                    jobs.append(j)
                w = proj(alternate(jobs), ("even_units", 8, 1), [r])
                st = other("index", dict(wx_t=2, wx=2, ix_s=16, ix_r=16, ix_a=16, top=1), ready=w)
                pairs = []
                for j in range(8):
                    mix = j < 4
                    pairs.append(dict(q=(lambda i, j=j: PJE[:, (j if j < 4 else 8 + j), i * P:(i + 1) * P]),
                                      k=(lambda h, i, j=j: PJE[:, 4 + j, 0:(i + 1) * P]),
                                      v=(lambda h, s, j=j: VTE[:, s, (2 * j + h) * HD:(2 * j + h + 1) * HD]),
                                      bias=(lambda h, i, j=j: BT[:, 2 * j + h, (1 - i) * P:2 * P]),
                                      keys=lambda i: i + 1, sel=not mix, sink=None, dst=N[:, j, 0:S]))
                at = attention(pairs, ready=[("top", st["top"] + 1)] + w, bias_ready=("bias0", 1))
                r = proj(out_jobs([0], lambda b, t: None), ("even_units", 9, 3), [("att_out", at["att_out"] + 8)])[0]
            else:
                jobs = []
                for b in range(8):
                    jobs.append(feature_job(b // 3, (b % 3) * P, P, PJE[:, b, :], True))
                jobs.append(feature_job(2, 256, P, PJE[:, 8, :], False))
                for i in range(2):
                    jobs.append(token_job(3, 0, 128, i, VTE[:, i, 0:128]))
                w = proj(alternate(jobs), ("swa_units", 0, 4), [r])
                pairs = []
                for j in range(8):
                    pairs.append(dict(q=(lambda i, j=j: PJE[:, j, i * P:(i + 1) * P]),
                                      k=(lambda h, i: PJE[:, 8, 0:(i + 1) * P]),
                                      v=(lambda h, s: VTE[:, s, h * HD:(h + 1) * HD]),
                                      bias=(lambda h, i, j=j: BT[:, 8 * h + j, (1 - i) * P:2 * P]),
                                      keys=lambda i: i + 1, sel=False,
                                      sink=(lambda h, j=j: sinks[:, 8 * h + j:8 * h + j + 1]), dst=N[:, j, 0:S]))
                at = attention(pairs, ready=w, bias_ready=("bias1", 1))
                r = proj(out_jobs([0], lambda b, t: None), ("swa_units", 4, 3), [("att_out", at["att_out"] + 8)])[0]
            first_att = at if layer == 0 else first_att
            second_att = at
            r = norm("rms", [range(KT)], xs(0), ns(0), ng(2), None, [r])
            r = ffn(("ffn_units", (2 * layer + 1) * FB), 0, [r], None)
        r = norm("rms", [range(KT)], xs(0), xs(0), lambda b: v("final_g", b), None, [r])

        mod_unit = add_units("mod_units", 0, 32)
        md = other("mod", dict(mod=2, cond=1), unit=mod_unit)
        x_now, c_now = r, ("load_ctx", 16)

        def modv(layer, which, stream):
            return lambda b: MOD[:, layer, which * 8 + b, stream:stream + 1]

        na_att = []
        for layer in range(2):
            both = layer == 0
            toks = [0, S] if both else [0]
            T = len(toks) * S
            rx = norm("ln", [range(KT)], xs(0), ns(0), modv(layer, 1, 0), modv(layer, 0, 0),
                      [x_now, ("mod", 2)], ns(0))
            rc = norm("ln", [range(KT)], xs(S), ns(S), modv(layer, 1, 1), modv(layer, 0, 1), [c_now], ns(S))
            jobs = []

            def feats(unit, off, blk, q, streams):
                n = len(streams) * S
                tok = streams[0] * S
                jobs.append(feature_job(unit, off, P, PJ[:, blk, tok:tok + n], q, n=n, tok=tok))

            mine, all_ = (([0, 1], [0, 1]) if both else ([0], [0, 1]))
            for b in range(3):
                feats(0, b * P, b, True, mine)
            for b in range(3):
                feats(1, b * P, 3 + b, False, all_)
            for i in range(4):
                jobs.append(token_job(2, 0, 384, i, VT[:, i, 0:384]))
            for b in range(2):
                feats(3, b * P, 6 + b, False, mine)
            for i in range(T // P):
                jobs.append(token_job(3, 256, 128, i, ZV[:, i, 0:128]))
            for i in range(T // P):
                jobs.append(token_job(4, 0, 128, i, ZV[:, i, 128:256]))
            for b in range(2):
                feats(4, (1 + b) * P, 8 + b, False, mine)
            feats(5, 0, 10, False, mine)
            feats(5, P, 11, False, all_)
            for i in range(4):
                jobs.append(token_job(5, 256, 128, i, VT[:, i, 384:512]))
            w = proj(alternate(jobs), ("mix2_units", layer * 9, 6), [rx, rc])
            nchunk = T // S * 2
            gt = other("gate", dict(g_sq=nchunk, g_w=nchunk, g_e=nchunk, g_z=nchunk, zc=T // P, zr=T // P, zn=T // P,
                                    g_mm=T // P, g_out=2 * (T // P)), layer=layer, T=T, ready=w)
            items = [(8 + b, 0) for b in range(4)] + ([(8 + b, 1) for b in range(4)] if both else [(11, 1)])
            rp = other("rope", dict(r_sq=len(items), r_ss=len(items), r_rs=len(items), r_y=len(items) - 1, r_rot=4,
                                    r_out=len(items)), layer=layer, items=items, ready=w)
            pairs = []
            for j in range(3):
                pairs.append(dict(q=(lambda i, j=j: PJ[:, j, i * P:(i + 1) * P]),
                                  k=(lambda h, i, j=j: PJ[:, 3 + j, 0:512]),
                                  v=(lambda h, s, j=j: VT[:, s, (2 * j + h) * HD:(2 * j + h + 1) * HD]),
                                  bias=(lambda h, i, j=j: NAB[:, i, 2 * j + h, :]),
                                  keys=lambda i: 4, sel=False, sink=None, dst=N[:, j, 0:S]))
            for j in range(3):
                pairs.append(dict(q=(lambda i, j=j: PJ[:, 8 + j, i * P:(i + 1) * P]),
                                  k=(lambda h, i: PJ[:, 11, 0:512]),
                                  v=(lambda h, s: VT[:, s, 384 + h * HD:384 + (h + 1) * HD]),
                                  bias=None, keys=lambda i: 4, sel=False, sink=None, dst=N[:, 5 + j, 0:S]))
            if both:
                for j in range(3):
                    pairs.append(dict(q=(lambda i, j=j: PJ[:, j, S + i * P:S + (i + 1) * P]),
                                      k=(lambda h, i, j=j: PJ[:, 3 + j, S:2 * S]),
                                      v=(lambda h, s, j=j: VT[:, 2 + s, (2 * j + h) * HD:(2 * j + h + 1) * HD]),
                                      bias=None, keys=lambda i: 2, sel=False, sink=None, dst=N[:, j, S:2 * S]))
                for j in range(3):
                    pairs.append(dict(q=(lambda i, j=j: PJ[:, 8 + j, S + i * P:S + (i + 1) * P]),
                                      k=(lambda h, i: PJ[:, 11, S:2 * S]),
                                      v=(lambda h, s: VT[:, 2 + s, 384 + h * HD:384 + (h + 1) * HD]),
                                      bias=None, keys=lambda i: 2, sel=False, sink=None, dst=N[:, 5 + j, S:2 * S]))
            at = attention(pairs, ready=[("r_out", rp["r_out"] + len(items))], bias_ready=(f"bias{2 + layer}", 1))
            na_att.append(at)
            done = [("att_out", at["att_out"] + len(pairs)), ("g_out", gt["g_out"] + 2 * (T // P))]
            merged = []
            for t in toks:
                merged.append(norm("rms", [range(3), range(3, 5), range(5, 8)], ns(t), ns(t),
                                   lambda b, layer=layer: v("g_out", layer * 8 + b), None, done))
            r = proj(out_jobs(toks, lambda b, t, layer=layer: modv(layer, 2, t // S)(b)),
                     ("mix2_units", layer * 9 + 6, 3), merged)[0]
            for which, t in enumerate(toks):
                ln = lambda name, layer=layer: (lambda b: v(name, layer * 8 + b))
                q = norm("ln", [range(KT)], xs(t), xs(t), ln("ln1_g"), ln("ln1_b"), [r], ns(t))
                q = norm("ln", [range(KT)], xs(t), ns(t), modv(layer, 4, which), modv(layer, 3, which), [q],
                         ns(t))
                q = ffn(("ffn2_units", layer * FB), t, [q], modv(layer, 5, which))
                q = norm("ln", [range(KT)], xs(t), xs(t), ln("ln2_g"), ln("ln2_b"), [q], ns(t))
                if which == 0:
                    x_now = q
                else:
                    c_now = q
        total_units = cnt.n["unit"]
        landed = [sem(f"unit_landed{i}") for i in range(RING)]

        def unit_slot(n):
            return ring[n % RING]

        def wait_all(eng, pairs):
            for name, value in pairs:
                eng.wait_ge(sem(name), value)

        for name in list(cnt.n) + ["load_x", "load_con", "load_ctx", "load_oh", "load_misc", "rows", "rows_sb",
                                   "rows_dram", "bt0", "bt1", "nab0", "nab1", "bias0", "bias1", "bias2",
                                   "bias3", "store", "dve_step", "act_step", "unit_used", "setup", "cond_exp"]:
            sem(name)

        def evacuate(eng, j, job, copy):
            bank_ = acc[j % 4]
            m, n = job["m"], job["n"]
            kind = job["evac"][0]
            if kind == "copy":
                return copy(job["dst"], bank_[0:m, 0:n], 1.0)
            factor = QSCALE if kind == "q" else job["evac"][1]
            return copy(job["dst"].rearrange("p (i t) -> p i t", t=P)[:, :, ::-1],
                        bank_[0:m, 0:n].rearrange("p (i t) -> p i t", t=P), factor)

        def gate_chunks(st):
            if st["T"] == 2 * S:
                return [PJ[:, b, :].rearrange("p (i t) -> p i t", i=2) for b in (6, 7)] + [
                    ZV[:, 0:2, :], ZV[:, 2:4, :]]
            return [PJ[:, 6:8, 0:S], ZV[:, 0:2, :]]

        def gate_tmp(c):
            t = SC[:, (c % 2) * 512:(c % 2 + 1) * 512]
            return t.rearrange("p (i t) -> p i t", i=2)

        block = ctx.enter_context(nc.Block())

        @block.sync
        def _(sp):
            n = 0
            for src, start, count in loads:
                def load(slot, unit, used):
                    if used is not None:
                        sp.wait_ge(sem("unit_used"), used)
                    sp.dma_start(ring[slot][:, :], src[unit]).then_inc(landed[slot], 16)

                head = min(count, max(0, RING - n)) if n < RING else 0
                for j in range(head):
                    load((n + j) % RING, start + j, None)
                left = count - head
                trips = left // RING
                if trips > 1:
                    with sp.Fori(0, trips) as i:
                        for j in range(RING):
                            m = n + head + j
                            sp.wait_ge(sem("unit_used"), i * RING + (m - RING + 1))
                            sp.dma_start(ring[m % RING][:, :],
                                         src[bass.ds(i * RING + (start + head + j), 1), :, :].rearrange(
                                             "o p c -> (o p) c")).then_inc(landed[m % RING], 16)
                    done = head + trips * RING
                else:
                    done = head
                for j in range(done, count):
                    load((n + j) % RING, start + j, n + j - RING + 1)
                n += count
            sp.wait_ge(sem(x_now[0]), x_now[1])
            sp.dma_start(a["out"], X[:, :, 0:S]).then_inc(sem("store"), 16)
            sp.wait_ge(sem("store"), 16)

        @block.gpsimd
        def _(pool):
            pool.dma_start(X[:, :, 0:S], a["x"]).then_inc(sem("load_x"), 16)
            pool.dma_start(con[:, :], a["con"]).then_inc(sem("load_con"), 16)
            pool.dma_start(vec[:, :], a["vec"]).then_inc(sem("load_con"), 16)
            pool.dma_start(OH, a["onehot"]).then_inc(sem("load_oh"), 16)
            pool.dma_start(TB, a["table"]).then_inc(sem("load_oh"), 16)
            pool.dma_start(X[:, :, S:2 * S], a["ctx"]).then_inc(sem("load_ctx"), 16)
            pool.dma_start(sinks, bass.AP(a["sinks"].tensor, 0, [[0, P], [1, 16]])).then_inc(sem("load_misc"), 16)
            pool.dma_start(WS[:, :, :, :], a["w_s"]).then_inc(sem("load_misc"), 16)
            for half in range(2):
                for layer in range(2):
                    src = bass.AP(a["b_s"].tensor, layer * 4 * P + half * P, [[0, HD], [2 * P, 2], [1, P]])
                    pool.dma_start(BS[half * HD:(half + 1) * HD, layer, :, :], src).then_inc(sem("load_misc"), 16)
            pool.wait_ge(sem("rows_sb"), 1)
            pool.dma_start(scratch_rows, ROW).then_inc(sem("rows_dram"), 16)
            pool.wait_ge(sem("rows_dram"), 16)
            diagonal = bass.AP(scratch_rows.tensor, 0, [[1, P], [384, 16], [1, 256]])

            def add_mask(region, mask, shape, done):
                pool.tensor_tensor(region, region, mask.unsqueeze(1).to_broadcast(shape), ALU.add).then_inc(
                    sem(done), 1)

            pool.dma_start(BT[:, :, :], diagonal).then_inc(sem("bt0"), 16)
            pool.wait_ge(sem("bt0"), 16)
            pool.wait_ge(sem("load_con"), 32)
            pool.tensor_tensor(BT[:, 0:8, :], BT[:, 0:8, :],
                               cst("mask_mix").unsqueeze(1).to_broadcast([P, 8, 256]), ALU.add)
            add_mask(BT[:, 8:16, :], cst("mask_causal"), [P, 8, 256], "bias0")
            pool.wait_ge(sem("att_m"), first_att["att_m"] + len(first_att["tiles"]))
            pool.dma_start(BT[:, :, :], diagonal).then_inc(sem("bt1"), 16)
            pool.wait_ge(sem("bt1"), 16)
            add_mask(BT[:, :, :], cst("mask_swa"), [P, 16, 256], "bias1")
            for layer in range(2):
                before = second_att if layer == 0 else na_att[0]
                pool.wait_ge(sem("att_m"), before["att_m"] + len(before["tiles"]))
                nd = 0
                for r_ in range(4):
                    part = 0 if r_ % 2 else HD
                    for h in range(6):
                        src = bass.AP(a["rpb"].tensor, ((layer * 6 + h) * 7 + 3 - r_) * 128,
                                      [[1, HD], [128, 4], [1, 64]])
                        dst = NAB[part:part + HD, r_ // 2, h, :].rearrange("p (k c) -> p k c", k=4)
                        pool.dma_start(dst, src).then_inc(sem(f"nab{layer}"), 16)
                        nd += 16
                pool.wait_ge(sem(f"nab{layer}"), nd)
                add_mask(BT[:, 0:12, :].rearrange("p h (k c) -> p (h k) c", c=64), cst("mask_na"),
                         [P, 48, 64], f"bias{2 + layer}")

        @block.tensor
        def _(pe):
            mm = nc.tensor.matmul

            def norm_stage(st):
                if st["ln"]:
                    wait_all(pe, st["ready"])
                    for j in range(st["nb"]):
                        last = mm(mean_bank[:, 0:S], ones, st["src"](j), start=j == 0, stop=j == st["nb"] - 1)
                    last.then_inc(sem("mean"), 1)
                n = 0
                for g, blocks in enumerate(st["groups"]):
                    for j, b in enumerate(blocks):
                        pe.wait_ge(sem("sq"), st["sq"] + n + 1)
                        last = mm(sum_bank[g][:, 0:S], ones, SQ[:, n, :],
                                  start=j == 0, stop=j == len(blocks) - 1, skip_group_check=True)
                        n += 1
                    last.then_inc(sem("ss"), 1)

            def ffn_stage(st):
                nb, tok = st["unit"], st["tok"]

                def ffn_up(w, bank_, rest):
                    for half in range(2):
                        for k in range(KT):
                            last = mm(bank_[:, half * S:(half + 1) * S],
                                      w[:, half * D + k * P:half * D + (k + 1) * P],
                                      N[:, k, tok:tok + S], start=k == 0 and half == 0, stop=k == KT - 1,
                                      skip_group_check=True)
                    last.then_inc(sem("up"), 1)

                def ffn_down(w, g, first):
                    for b in range(KT):
                        last = mm(acc[b // 2][:, (b % 2) * S:(b % 2 + 1) * S],
                                  w[:, 2 * D + b * P:2 * D + (b + 1) * P], g,
                                  start=first and b % 2 == 0, stop=True, skip_group_check=True)
                    last.then_inc(sem("unit_used"), 1)

                def one(u, d):
                    if u is not None:
                        pe.wait_ge(landed[(nb + u) % RING], 16 * ((nb + u) // RING + 1))
                        if u >= 2:
                            pe.wait_ge(sem("gated"), st["gated"] + u - 1)
                        ffn_up(unit_slot(nb + u), up[u % 2], None)
                    if d is not None:
                        pe.wait_ge(sem("gated"), st["gated"] + d + 1)
                        ffn_down(unit_slot(nb + d), fG[d % 2], d == 0)

                wait_all(pe, st["ready"])
                one(0, None)
                one(1, 0)
                trips = (FB - 2) // RING
                with pe.Fori(0, trips) as i:
                    for j in range(RING):
                        u, d = 2 + j, 1 + j
                        pe.wait_ge(landed[(nb + u) % RING], i * 16 + 16 * ((nb + u) // RING + 1))
                        pe.wait_ge(sem("gated"), i * RING + (st["gated"] + u - 1))
                        ffn_up(unit_slot(nb + u), up[u % 2], None)
                        pe.wait_ge(sem("gated"), i * RING + (st["gated"] + d + 1))
                        ffn_down(unit_slot(nb + d), fG[d % 2], False)
                for d in range(1 + trips * RING, FB):
                    one(d + 1 if d + 1 < FB else None, d)

            def proj_stage(st):
                wait_all(pe, st["ready"])
                jobs = st["jobs"]
                seen = set()
                for j, job in enumerate(jobs):
                    if job["slot"] not in seen:
                        seen.add(job["slot"])
                        pe.wait_ge(landed[job["slot"] % RING], 16 * (job["slot"] // RING + 1))
                    if j >= 4:
                        pe.wait_ge(sem(jobs[j - 4]["out"][0]), jobs[j - 4]["out"][1])
                    w = unit_slot(job["slot"])
                    for k in range(job["kts"]):
                        cols = w[:, k * job["kstep"] + job["off"]:k * job["kstep"] + job["off"] +
                                 (job["n"] if job["tm"] else job["m"])] if job["off"] < 1024 or job["kts"] == KT \
                            else w[:, 1024 + k * 256 + job["off"] - 1024:1024 + k * 256 + job["off"] - 1024 + job["m"]]
                        lhs, rhs = (job["src"](k), cols) if job["tm"] else (cols, job["src"](k))
                        last = mm(acc[j % 4][0:job["m"], 0:job["n"]], lhs, rhs, start=k == 0,
                                  stop=k == job["kts"] - 1, skip_group_check=True)
                    last.then_inc(sem("unit_used" if job["last"] else "proj"), 1)

            def index_stage(st):
                wait_all(pe, st["ready"])
                for i in range(2):
                    nc.tensor.transpose(acc[2 + i][:, 0:8], PJE[0:8, 21, i * P:(i + 1) * P],
                                        ident[0:8, 0:8]).then_inc(sem("wx_t"), 1)
                for n in range(16):
                    i, h = n // 8, n % 8
                    if n >= 2:
                        pe.wait_ge(sem("ix_r"), st["ix_r"] + n - 1)
                    mm(acc[n % 2][:, 0:(i + 1) * P], QI[0:32, h, i * P:(i + 1) * P], PJE[0:32, 20, 0:(i + 1) * P],
                       start=True, stop=True).then_inc(sem("ix_s"), 1)

            def attn_stage(st):
                pairs, tiles = st["pairs"], st["tiles"]
                wait_all(pe, st["ready"])
                nt = len(tiles)

                def scores(t):
                    n, h, i = tiles[t]
                    pr = pairs[n]
                    if t >= 3:
                        pe.wait_ge(sem("att_e"), st["att_e"] + t - 2)
                    lo = h * HD
                    mm(acc[t % 3][:, 0:pr["keys"](i) * P], pr["q"](i)[lo:lo + HD], pr["k"](h, i)[lo:lo + HD],
                       start=True, stop=True).then_inc(sem("att_s"), 1)

                def turn(t):
                    n, h, i = tiles[t]
                    pe.wait_ge(sem("att_n"), st["att_n"] + t + 1)
                    if t >= 2:
                        pe.wait_ge(sem("att_c"), st["att_c"] + t - 1)
                    for s in range(pairs[n]["keys"](i)):
                        last = nc.tensor.transpose(up[t % 2][:, s * P:(s + 1) * P], aP[t % 3][:, s * P:(s + 1) * P],
                                                   ident)
                    last.then_inc(sem("att_t"), 1)

                def values(t):
                    n, h, i = tiles[t]
                    pr = pairs[n]
                    pe.wait_ge(sem("att_c"), st["att_c"] + t + 1)
                    if h == 0 and n >= 2:
                        pe.wait_ge(sem("att_out"), st["att_out"] + n - 1)
                    o = stat[n % 2][h * HD:(h + 1) * HD]
                    pT = aT[(2 * n + h) % 2]
                    ks = pr["keys"](1)
                    for s in range(ks):
                        t0 = P if s >= pr["keys"](0) else 0
                        last = mm(o[:, t0:S], pr["v"](h, s), pT[:, s, t0:S], start=s == 0, stop=s == ks - 1,
                                  skip_group_check=True)
                    last.then_inc(sem("att_o"), 1)

                for t in range(nt + 3):
                    if t < nt:
                        scores(t)
                    if 0 <= t - 2 < nt:
                        turn(t - 2)
                    if 0 <= t - 3 < nt and tiles[t - 3][2] == 1:
                        values(t - 3)

            def gate_stage(st):
                T, layer = st["T"], st["layer"]
                pe.wait_ge(sem("load_misc"), 16 * 6)
                for tb in range(T // P):
                    pe.wait_ge(sem("zn"), st["zn"] + tb + 1)
                    for g in range(4):
                        h = g % 2
                        last = mm(acc[tb][h * HD:(h + 1) * HD, (g // 2) * P:(g // 2 + 1) * P],
                                  ZV[:, tb, g * HD:(g + 1) * HD], WS[:, layer, g, :], start=True, stop=True,
                                  skip_group_check=True)
                    last.then_inc(sem("g_mm"), 1)

            def rope_stage(st):
                for n, (b, s) in enumerate(st["items"]):
                    pe.wait_ge(sem("r_sq"), st["r_sq"] + n + 1)
                    if n >= 4:
                        pe.wait_ge(sem("r_rs"), st["r_rs"] + n - 3)
                    mm(head_bank[n % 4][:, 0:S], cst("halves"), SQ[:, n, :], start=True,
                       stop=True, skip_group_check=True).then_inc(sem("r_ss"), 1)
                for n in range(4):
                    pe.wait_ge(sem("r_y"), st["r_y"] + n + 1)
                    mm(acc[n][:, 0:S], cst("swap"), SC[:, n * S:(n + 1) * S],
                       start=True, stop=True, skip_group_check=True).then_inc(sem("r_rot"), 1)

            def mod_stage(st):
                pe.wait_ge(sem("cond"), st["cond"] + 1)
                for u in range(32):
                    n = st["unit"] + u
                    pe.wait_ge(landed[n % RING], 16 * (n // RING + 1))
                    for b in range(3):
                        col = ((u % 16) * 3 + b) * 2
                        for k in range(KT):
                            last = mm(acc[u // 16][:, col:col + 2], unit_slot(n)[:, k * UC + b * P:k * UC + (b + 1) * P],
                                      CS[:, k, :], start=k == 0, stop=k == KT - 1, skip_group_check=True)
                    last.then_inc(sem("unit_used"), 1)

            pe.wait_ge(sem("load_oh"), 32)
            mm(stat[1][0:16, 0:384], TB, OH, start=True, stop=True).then_inc(sem("rows"), 1)
            pe.wait_ge(sem("rows_sb"), 1)
            run = dict(norm=norm_stage, ffn=ffn_stage, proj=proj_stage, index=index_stage, attn=attn_stage,
                       gate=gate_stage, rope=rope_stage, mod=mod_stage)
            for st in stages:
                run[st["kind"]](st)

        @block.scalar
        def _(act):
            fn = nc.scalar.activation
            steps = [0]

            def link(ins):
                steps[0] += 1
                ins.then_inc(sem("act_step"), 1)
                act.wait_ge(sem("act_step"), steps[0])

            def norm_stage(st):
                wait_all(act, st["ready"])
                n = 0
                for g, blocks in enumerate(st["groups"]):
                    for b in blocks:
                        if st["ln"]:
                            act.wait_ge(sem("cen"), st["cen"] + n + 1)
                            src = st["centred"](b)
                        else:
                            src = st["src"](b)
                        fn(SQ[:, n, :], src, ACT.Square).then_inc(sem("sq"), 1)
                        n += 1
                for g, blocks in enumerate(st["groups"]):
                    act.wait_ge(sem("ss"), st["ss"] + g + 1)
                    if g == 0 and st["rstd_free"] > 0:
                        act.wait_ge(sem("rms_out"), st["rstd_free"])
                    link(fn(RS[:, g, :], sum_bank[g][:, 0:S], ACT.Ln,
                            bias=eps, scale=1.0 / (len(blocks) * P)))
                    fn(RS[:, g, :], RS[:, g, :], ACT.Exp, scale=-0.5).then_inc(sem("rstd"), 1)
                if st["ln"]:
                    for b in range(st["nb"]):
                        act.wait_ge(sem("scaled"), st["scaled"] + b + 1)
                        fn(st["dst"](b), st["centred"](b), ACT.Identity,
                           bias=st["shift"](b)).then_inc(sem("ln_out"), 1)

            def ffn_stage(st):
                for p in range(2):
                    act.wait_ge(sem("up"), st["up"] + p + 1)
                    fn(fE[p % 2], up[p % 2][:, 0:S], ACT.Exp, scale=-1.0).then_inc(sem("ffn_exp"), 1)
                with act.Fori(0, (FB - 2) // 2) as i:
                    for p in range(2):
                        act.wait_ge(sem("up"), i * 2 + (st["up"] + p + 3))
                        act.wait_ge(sem("gated"), i * 2 + (st["gated"] + p + 1))
                        fn(fE[p % 2], up[p % 2][:, 0:S], ACT.Exp, scale=-1.0).then_inc(sem("ffn_exp"), 1)

            def proj_stage(st):
                for j, job in enumerate(st["jobs"]):
                    if job["eng"] == "act":
                        act.wait_ge(sem(job["done"][0]), job["done"][1])
                        evacuate(act, j, job, lambda d, s, f: fn(d, s, ACT.Copy, scale=f)).then_inc(
                            sem("evac_act"), 1)

            def index_stage(st):
                for n in range(16):
                    i = n // 8
                    act.wait_ge(sem("ix_s"), st["ix_s"] + n + 1)
                    if n >= 2:
                        act.wait_ge(sem("ix_a"), st["ix_a"] + n - 1)
                    fn(RELU[n % 2][:, 0:(i + 1) * P], acc[n % 2][:, 0:(i + 1) * P], ACT.Relu).then_inc(
                        sem("ix_r"), 1)

            def attn_stage(st):
                pairs, tiles = st["pairs"], st["tiles"]

                def exps(t):
                    n, h, i = tiles[t]
                    pr = pairs[n]
                    w = pr["keys"](i) * P
                    act.wait_ge(sem("att_m"), st["att_m"] + t + 1)
                    if t >= 3:
                        act.wait_ge(sem("att_t"), st["att_t"] + t - 2)
                    m = ATT[:, t % 3]
                    nm = m[:, 0:1]
                    if pr["bias"] is None:
                        last = fn(aP[t % 3][:, 0:w], acc[t % 3][:, 0:w], ACT.Exp, bias=nm, accum_out=m[:, 2:3])
                    else:
                        wb = min(w, 256)
                        last = fn(aP[t % 3][:, 0:wb], aS[t % 3][:, 0:wb], ACT.Exp, bias=nm, scale=-1.0,
                                  accum_out=m[:, 2:3])
                        if w > wb:
                            last = fn(aP[t % 3][:, wb:w], acc[t % 3][:, wb:w], ACT.Exp, bias=nm,
                                      accum_out=m[:, 3:4])
                    if pr["sink"] is not None:
                        last = fn(m[:, 3:4], pr["sink"](h), ACT.Exp, bias=nm)
                    last.then_inc(sem("att_e"), 1)

                def copies(t):
                    n, h, i = tiles[t]
                    ks = pairs[n]["keys"](i)
                    b = 2 * n + h
                    act.wait_ge(sem("att_t"), st["att_t"] + t + 1)
                    if b >= 2 and i == 0:
                        act.wait_ge(sem("att_o"), st["att_o"] + b - 1)
                    fn(aT[b % 2][:, 0:ks, i * P:(i + 1) * P][:, :, ::-1],
                       up[t % 2][:, 0:ks * P].rearrange("p (s t) -> p s t", t=P), ACT.Copy).then_inc(sem("att_c"), 1)

                nt = len(tiles)
                for t in range(nt + 2):
                    if t < nt:
                        exps(t)
                    if 0 <= t - 2 < nt:
                        copies(t - 2)

            def gate_stage(st):
                T = st["T"]
                wait_all(act, st["ready"])
                chunks = gate_chunks(st)
                for c, z in enumerate(chunks):
                    if c >= 2:
                        act.wait_ge(sem("g_z"), st["g_z"] + c - 1)
                    fn(gate_tmp(c), z, ACT.Square).then_inc(sem("g_sq"), 1)
                    act.wait_ge(sem("g_w"), st["g_w"] + c + 1)
                    fn(gate_tmp(c), gate_tmp(c), ACT.Exp, scale=-GELU_C).then_inc(sem("g_e"), 1)
                for tb in range(T // P):
                    act.wait_ge(sem("zc"), st["zc"] + tb + 1)
                    link(fn(SC[:, 2048 + tb * 256:2304 + tb * 256], ZV[:, tb, :], ACT.Square, accum_out=LNS[:, tb, 2:3]))
                    link(fn(LNS[:, tb, 3:4], LNS[:, tb, 2:3], ACT.Ln, bias=eps, scale=1.0 / 256))
                    fn(LNS[:, tb, 4:5], LNS[:, tb, 3:4], ACT.Exp, scale=-0.5).then_inc(sem("zr"), 1)

            def rope_stage(st):
                for n, (b, s) in enumerate(st["items"]):
                    fn(SQ[:, n, :], PJ[:, b, s * S:(s + 1) * S], ACT.Square).then_inc(sem("r_sq"), 1)
                for n, (b, s) in enumerate(st["items"]):
                    act.wait_ge(sem("r_ss"), st["r_ss"] + n + 1)
                    link(fn(SQ[:, n, :], head_bank[n % 4][:, 0:S], ACT.Ln, bias=eps,
                            scale=1.0 / HD))
                    fn(SQ[:, n, :], SQ[:, n, :], ACT.Exp, scale=-0.5).then_inc(sem("r_rs"), 1)

            def mod_stage(st):
                fn(CTMP, vec[:, VEC["cond"]:VEC["cond"] + 16], ACT.Exp, scale=-1.0).then_inc(sem("cond_exp"), 1)

            nc.scalar.preload_act_table_set("natural_log_exp_and_others")
            act.wait_ge(sem("setup"), 1)
            run = dict(norm=norm_stage, ffn=ffn_stage, proj=proj_stage, index=index_stage, attn=attn_stage,
                       gate=gate_stage, rope=rope_stage, mod=mod_stage)
            for st in stages:
                run[st["kind"]](st)

        @block.vector
        def _(dve):
            ve = nc.vector
            steps = [0]

            def link(ins):
                steps[0] += 1
                ins.then_inc(sem("dve_step"), 1)
                dve.wait_ge(sem("dve_step"), steps[0])

            def norm_stage(st):
                if st["ln"]:
                    wait_all(dve, st["ready"])
                    dve.wait_ge(sem("mean"), st["mean"] + 1)
                    for b in range(st["nb"]):
                        ve.scalar_tensor_tensor(out=st["centred"](b), in0=mean_bank[:, 0:S], scalar=-1.0 / (st["nb"] * P),
                                                in1=st["src"](b), op0=ALU.mult, op1=ALU.add).then_inc(sem("cen"), 1)
                n = 0
                for g, blocks in enumerate(st["groups"]):
                    dve.wait_ge(sem("rstd"), st["rstd"] + g + 1)
                    for b in blocks:
                        src = st["centred"](b) if st["ln"] else st["src"](b)
                        dst = st["centred"](b) if st["ln"] else st["dst"](b)
                        ve.scalar_tensor_tensor(out=dst, in0=src, scalar=st["gain"](b), in1=RS[:, g, :],
                                                op0=ALU.mult, op1=ALU.mult).then_inc(
                            sem("scaled" if st["ln"] else "rms_out"), 1)
                        n += 1

            def ffn_stage(st):
                tok = st["tok"]

                def gate(p, value, wait_used):
                    e, t, u = fE[p % 2], fT[p % 2], up[p % 2]
                    dve.wait_ge(sem("ffn_exp"), value(st["exp"] + p + 1))
                    ve.tensor_scalar(e, e, 1.0, None, ALU.add).then_inc(sem("dve_step"), 1)
                    dve.wait_ge(sem("dve_step"), value3(value, steps[0] + 3 * p + 1))
                    ve.reciprocal(e, e).then_inc(sem("dve_step"), 1)
                    dve.wait_ge(sem("dve_step"), value3(value, steps[0] + 3 * p + 2))
                    ve.tensor_tensor(t, e, u[:, 0:S], ALU.mult).then_inc(sem("dve_step"), 1)
                    dve.wait_ge(sem("dve_step"), value3(value, steps[0] + 3 * p + 3))
                    if wait_used:
                        dve.wait_ge(sem("unit_used"), value(st["unit"] + p - 1))
                    ve.tensor_tensor(fG[p % 2], t, u[:, S:2 * S], ALU.mult).then_inc(sem("gated"), 1)

                def value3(value, const):
                    return value(const, 3)

                for p in range(2):
                    gate(p, lambda c, per=1: c, False)
                with dve.Fori(0, (FB - 2) // 2) as i:
                    for p in range(2, 4):
                        gate(p, lambda c, per=1: i * (2 * per) + c, True)
                steps[0] += 3 * FB
                dve.wait_ge(sem("unit_used"), st["unit"] + FB)
                for b in range(KT):
                    x = X[:, b, tok:tok + S]
                    residual(x, acc[b // 2][:, (b % 2) * S:(b % 2 + 1) * S],
                             st["resid"](b) if st["resid"] else 0.5, st["resid"] is not None, st["scaled"] + b + 1)

            def residual(x, y, gain, post, value):
                if post:
                    ve.tensor_scalar(x, x, ALPHA, None, ALU.mult).then_inc(sem("alpha"), 1)
                    dve.wait_ge(sem("alpha"), value)
                ve.scalar_tensor_tensor(out=x, in0=y, scalar=gain, in1=x, op0=ALU.mult, op1=ALU.add).then_inc(
                    sem("resid"), 1)

            def proj_stage(st):
                for j, job in enumerate(st["jobs"]):
                    if job["eng"] != "dve":
                        continue
                    dve.wait_ge(sem(job["done"][0]), job["done"][1])
                    if job["evac"][0] == "resid":
                        gain = job["evac"][1]
                        residual(job["dst"], acc[j % 4][:, 0:S], 1.0 if gain is None else gain, gain is not None,
                                 job.get("scaled"))
                    else:
                        evacuate(dve, j, job, lambda d, s, f: ve.tensor_scalar(d, s, f, None, ALU.mult)).then_inc(
                            sem("evac_dve"), 1)

            def index_stage(st):
                wait_all(dve, st["ready"])
                for i in range(2):
                    dve.wait_ge(sem("wx_t"), st["wx_t"] + i + 1)
                    ve.tensor_copy(WX[:, i, :], acc[2 + i][:, 0:8]).then_inc(sem("wx"), 1)
                    dve.wait_ge(sem("wx"), st["wx"] + i + 1)
                for n in range(16):
                    i, h = n // 8, n % 8
                    w = (i + 1) * P
                    dve.wait_ge(sem("ix_r"), st["ix_r"] + n + 1)
                    if h > 0:
                        dve.wait_ge(sem("ix_a"), st["ix_a"] + n)
                    before = SCORE[:, i, 0:w] if h else cst("mask_causal")[:, (1 - i) * P:2 * P]
                    ve.scalar_tensor_tensor(out=SCORE[:, i, 0:w], in0=RELU[n % 2][:, 0:w], scalar=WX[:, i, h:h + 1],
                                            in1=before, op0=ALU.mult, op1=ALU.add).then_inc(sem("ix_a"), 1)
                dve.wait_ge(sem("ix_a"), st["ix_a"] + 16)
                for i in range(2):
                    w = (i + 1) * P
                    for r_ in range(TOPK // 8):
                        top8 = small[:, 160 + 8 * i:168 + 8 * i]
                        link(ve.max(top8, SCORE[:, i, 0:w]))
                        link(ve.match_replace(SCORE[:, i, 0:w], top8, SCORE[:, i, 0:w], TAKEN))
                for i in range(2):
                    w = (i + 1) * P
                    last = ve.tensor_scalar(SEL[:, i, 0:w], SCORE[:, i, 0:w], TAKEN / 2, NEG, ALU.is_gt, ALU.mult)
                last.then_inc(sem("top"), 1)

            def attn_stage(st):
                pairs, tiles = st["pairs"], st["tiles"]
                wait_all(dve, st["ready"])
                dve.wait_ge(sem(st["bias_ready"][0]), st["bias_ready"][1])

                def maxima(t):
                    n, h, i = tiles[t]
                    pr = pairs[n]
                    w = pr["keys"](i) * P
                    m = ATT[:, t % 3]
                    s = acc[t % 3]
                    dve.wait_ge(sem("att_s"), st["att_s"] + t + 1)
                    if t >= 3:
                        dve.wait_ge(sem("att_n"), st["att_n"] + t - 2)
                    if pr["bias"] is None:
                        ve.tensor_reduce(m[:, 0:1], s[:, 0:w], AX.X, ALU.max, negate=True).then_inc(sem("att_m"), 1)
                        return
                    wb = min(w, 256)
                    bias = pr["bias"](h, i)
                    src = s[:, 0:wb]
                    if pr["sel"]:
                        link(ve.tensor_tensor(aS[t % 3][:, 0:wb], src, bias, ALU.add))
                        src, bias = aS[t % 3][:, 0:wb], SEL[:, i, 0:wb]
                    if w == wb:
                        ve.tensor_tensor_reduce(aS[t % 3][:, 0:wb], src, bias, -1.0, -NEG, ALU.add, ALU.min,
                                                m[:, 0:1]).then_inc(sem("att_m"), 1)
                        return
                    ve.tensor_tensor_reduce(aS[t % 3][:, 0:wb], src, bias, -1.0, -NEG, ALU.add, ALU.min, m[:, 4:5])
                    link(ve.tensor_reduce(m[:, 5:6], s[:, wb:w], AX.X, ALU.max, negate=True))
                    ve.tensor_tensor(m[:, 0:1], m[:, 4:5], m[:, 5:6], ALU.min).then_inc(sem("att_m"), 1)

                def scale(t):
                    n, h, i = tiles[t]
                    pr = pairs[n]
                    w = pr["keys"](i) * P
                    m = ATT[:, t % 3]
                    dve.wait_ge(sem("att_e"), st["att_e"] + t + 1)
                    den = m[:, 2:3]
                    if pr["sink"] is not None or (pr["bias"] is not None and w > 256):
                        link(ve.tensor_tensor(m[:, 6:7], m[:, 2:3], m[:, 3:4], ALU.add))
                        den = m[:, 6:7]
                    link(ve.reciprocal(m[:, 7:8], den))
                    ve.tensor_scalar(aP[t % 3][:, 0:w], aP[t % 3][:, 0:w], m[:, 7:8], None, ALU.mult).then_inc(
                        sem("att_n"), 1)

                def outputs(n):
                    dve.wait_ge(sem("att_o"), st["att_o"] + 2 * n + 2)
                    ve.tensor_copy(pairs[n]["dst"], stat[n % 2][:, 0:S]).then_inc(sem("att_out"), 1)

                nt = len(tiles)
                for t in range(nt + 5):
                    if t < nt:
                        maxima(t)
                    if 0 <= t - 1 < nt:
                        scale(t - 1)
                    if t >= 8 and t % 4 == 0 and t // 4 - 2 < len(pairs):
                        outputs(t // 4 - 2)

            def gate_stage(st):
                T, layer = st["T"], st["layer"]
                wait_all(dve, st["ready"])
                dve.wait_ge(sem("load_misc"), 16 * 6)
                for c, z in enumerate(gate_chunks(st)):
                    t = gate_tmp(c)
                    dve.wait_ge(sem("g_sq"), st["g_sq"] + c + 1)
                    link(ve.tensor_scalar(t, t, 0.044715, 1.0, ALU.mult, ALU.add))
                    ve.tensor_tensor(t, t, z, ALU.mult).then_inc(sem("g_w"), 1)
                    dve.wait_ge(sem("g_e"), st["g_e"] + c + 1)
                    link(ve.tensor_scalar(t, t, 1.0, None, ALU.add))
                    link(ve.reciprocal(t, t))
                    ve.tensor_tensor(z, z, t, ALU.mult).then_inc(sem("g_z"), 1)
                    dve.wait_ge(sem("g_z"), st["g_z"] + c + 1)
                for tb in range(T // P):
                    z = ZV[:, tb, :]
                    link(ve.tensor_reduce(LNS[:, tb, 0:1], z, AX.X, ALU.add))
                    link(ve.tensor_scalar(LNS[:, tb, 1:2], LNS[:, tb, 0:1], -1.0 / 256, None, ALU.mult))
                    ve.tensor_scalar(z, z, LNS[:, tb, 1:2], None, ALU.add).then_inc(sem("zc"), 1)
                for tb in range(T // P):
                    dve.wait_ge(sem("zr"), st["zr"] + tb + 1)
                    ve.tensor_scalar(ZV[:, tb, :], ZV[:, tb, :], LNS[:, tb, 4:5], None, ALU.mult).then_inc(
                        sem("zn"), 1)
                for tb in range(T // P):
                    dve.wait_ge(sem("g_mm"), st["g_mm"] + tb + 1)
                    for j in range(2):
                        t = SC[:, 3072 + (2 * tb + j) * P:3072 + (2 * tb + j + 1) * P]
                        link(ve.scalar_tensor_tensor(out=t, in0=acc[tb][:, j * P:(j + 1) * P],
                                                     scalar=v("g_sgu", layer * 2 + j), in1=BS[:, layer, j, :],
                                                     op0=ALU.mult, op1=ALU.add))
                        ve.tensor_tensor(N[:, 3 + j, tb * P:(tb + 1) * P], t, PJ[:, 6 + j, tb * P:(tb + 1) * P],
                                         ALU.mult).then_inc(sem("g_out"), 1)

            def rope_stage(st):
                layer = st["layer"]

                def tiles3(ap):
                    return ap.rearrange("p (i t) -> p i t", t=P)

                for n, (b, s) in enumerate(st["items"]):
                    g = GQ[:, layer:layer + 1] if b < 11 else v("g_k", layer)
                    z = PJ[:, b, s * S:(s + 1) * S]
                    dve.wait_ge(sem("r_rs"), st["r_rs"] + n + 1)
                    if s == 0:
                        ve.scalar_tensor_tensor(out=SC[:, n * S:(n + 1) * S], in0=z, scalar=g, in1=SQ[:, n, :],
                                                op0=ALU.mult, op1=ALU.mult).then_inc(sem("r_y"), 1)
                    elif b == 11:
                        ve.scalar_tensor_tensor(out=z, in0=z, scalar=g, in1=SQ[:, n, :], op0=ALU.mult,
                                                op1=ALU.mult).then_inc(sem("r_out"), 1)
                    else:
                        ve.scalar_tensor_tensor(out=SQ[:, n, :], in0=z, scalar=g, in1=SQ[:, n, :], op0=ALU.mult,
                                                op1=ALU.mult).then_inc(sem("r_y"), 1)
                for n, (b, s) in enumerate(st["items"][:-1]):
                    z = PJ[:, b, s * S:(s + 1) * S]
                    dve.wait_ge(sem("r_y"), st["r_y"] + n + 1)
                    if s == 0:
                        dve.wait_ge(sem("r_rot"), st["r_rot"] + n + 1)
                        y, r_ = SC[:, n * S:(n + 1) * S], SC[:, (4 + n) * S:(5 + n) * S]
                        ve.tensor_tensor(SQ[:, n, :], y, cst("cos"), ALU.mult)
                        link(ve.tensor_tensor(r_, acc[n][:, 0:S], cst("sin"), ALU.mult))
                        out = z if b == 11 else tiles3(z)[:, :, ::-1]
                        p, q = (SQ[:, n, :], r_) if b == 11 else (tiles3(SQ[:, n, :]), tiles3(r_))
                        ve.tensor_tensor(out, p, q, ALU.add).then_inc(sem("r_out"), 1)
                    else:
                        ve.tensor_copy(tiles3(z)[:, :, ::-1], tiles3(SQ[:, n, :])).then_inc(sem("r_out"), 1)

            def mod_stage(st):
                dve.wait_ge(sem("cond_exp"), 1)
                link(ve.tensor_scalar(CTMP, CTMP, 1.0, None, ALU.add))
                link(ve.reciprocal(CTMP, CTMP))
                ve.tensor_tensor(small[:, 64:80], CTMP, vec[:, VEC["cond"]:VEC["cond"] + 16], ALU.mult).then_inc(
                    sem("cond"), 1)
                for layer in range(2):
                    dve.wait_ge(sem("unit_used"), st["unit"] + 16 * (layer + 1))
                    b = vec[:, VEC["b_mod"] + layer * 48:VEC["b_mod"] + (layer + 1) * 48]
                    link(ve.tensor_tensor(MOD[:, layer, :, :], acc[layer][:, 0:96].rearrange("p (n s) -> p n s", s=2),
                                          b.unsqueeze(2).to_broadcast([P, 48, 2]), ALU.add))
                    link(ve.tensor_scalar(MOD[:, layer, 8:16, :], MOD[:, layer, 8:16, :], 1.0, None, ALU.add))
                    ve.tensor_scalar(MOD[:, layer, 32:40, :], MOD[:, layer, 32:40, :], 1.0, None,
                                     ALU.add).then_inc(sem("mod"), 1)

            ve.memset(eps, EPS).then_inc(sem("setup"), 1)
            dve.wait_ge(sem("load_con"), 32)
            ve.tensor_scalar(GQ, vec[:, VEC["g_q"]:VEC["g_q"] + 2], QSCALE, None, ALU.mult)
            dve.wait_ge(sem("rows"), 1)
            ve.tensor_copy(ROW, stat[1][0:16, 0:384]).then_inc(sem("rows_sb"), 1)
            dve.wait_ge(sem("rows_dram"), 16)
            run = dict(norm=norm_stage, ffn=ffn_stage, proj=proj_stage, index=index_stage, attn=attn_stage,
                       gate=gate_stage, rope=rope_stage, mod=mod_stage)
            for st in stages:
                run[st["kind"]](st)


def column_units(w):
    n = w.shape[1]
    u = tiles_cols(n)
    w = np.pad(w, ((0, 0), (0, u * UC - n)))
    return w.reshape(KT, P, u, UC).transpose(2, 1, 0, 3).reshape(u, P, UNIT)


def hidden_units(w1, w3, w2):
    def cols(w):
        return w.reshape(KT, P, FB, P).transpose(2, 1, 0, 3).reshape(FB, P, D)

    return np.concatenate([cols(w1), cols(w3), w2.reshape(FB, P, D)], axis=2)


def columns(v):
    return np.asarray(v).reshape(-1, P).T


def kernel(x, norm_g, final_g, rel_bias_table, ffn_w1, ffn_w3, ffn_w2, hyb_w_in, hyb_cq_g, hyb_wq_b, hyb_wq_idx,
           hyb_w_out, swa_w_in, swa_sinks, swa_w_out, c_2, ctx_2, c_ctx_2, w_mod_2, b_mod_2, w_in_2, rpb_2, w_s_2,
           b_s_2, g_sgu_2, g_q_2, g_k_2, g_out_2, w_o_2, ln1_g_2, ln1_b_2, w_ffn_in_2, w_ffn_out_2, ln2_g_2,
           ln2_b_2):
    import concourse.bacc as bacc
    from concourse.bass_utils import run_bass_kernel_spmd

    swa_cols = np.concatenate([np.r_[j * HD:(j + 1) * HD, (8 + j) * HD:(9 + j) * HD] for j in range(8)])
    gqa_cols = np.concatenate([np.r_[j * HD:(j + 1) * HD, (3 + j) * HD:(4 + j) * HD] for j in range(3)])
    swa_in = np.concatenate([swa_w_in[0][:, swa_cols], swa_w_in[0][:, 1024:]], axis=1)
    in2_cols = np.r_[0:1664, 1664 + gqa_cols, 2048:2304]
    out2_rows = np.r_[0:640, 640 + gqa_cols]

    def feature_major(t):
        return t[0].T.reshape(KT, P, S).transpose(1, 0, 2)

    cq_unit = np.zeros((1, P, UNIT), np.float32)
    cq_unit[0, :, 0:1024] = hyb_wq_b[0].reshape(2, P, 512).transpose(1, 0, 2).reshape(P, 1024)
    cq_unit[0, :, 1024:1536] = hyb_wq_idx[0].reshape(2, P, 256).transpose(1, 0, 2).reshape(P, 512)
    arrays = {
        "x": feature_major(x), "ctx": feature_major(ctx_2),
        "con": constants(), "onehot": bucket_rows(), "table": rel_bias_table,
        "vec": np.concatenate([columns(norm_g), columns(final_g), columns(hyb_cq_g), columns(b_mod_2),
                               columns(g_sgu_2), columns(np.tile(g_q_2, (1, 2))), columns(np.tile(g_k_2, (1, 2))),
                               columns(g_out_2[:, out2_rows]), columns(ln1_g_2), columns(ln1_b_2),
                               columns(ln2_g_2), columns(ln2_b_2), columns(c_2), columns(c_ctx_2)], axis=1),
        "sinks": swa_sinks, "b_s": b_s_2, "w_s": w_s_2.transpose(3, 0, 1, 2),
        "rpb": np.pad(rpb_2[:, :, 4:11, :], ((0, 0), (0, 0), (0, 0), (48, 49))),
        "ffn_units": np.concatenate([hidden_units(ffn_w1[l, f], ffn_w3[l, f], ffn_w2[l, f])
                                     for l in range(2) for f in range(2)]),
        "even_units": np.concatenate([column_units(hyb_w_in[0]), cq_unit, column_units(hyb_w_out[0])]),
        "swa_units": np.concatenate([column_units(swa_in), column_units(swa_w_out[0][swa_cols])]),
        "mod_units": np.concatenate([column_units(w_mod_2[l]) for l in range(2)]),
        "mix2_units": np.concatenate([column_units(w) for l in range(2)
                                      for w in (w_in_2[l][:, in2_cols], w_o_2[l][out2_rows])]),
        "ffn2_units": np.concatenate([hidden_units(w_ffn_in_2[l][:, :FF], w_ffn_in_2[l][:, FF:], w_ffn_out_2[l])
                                      for l in range(2)]),
    }
    nc = bacc.Bacc("TRN2", target_bir_lowering=False, num_devices=1)
    inputs, aps = {}, {}
    for name, value in arrays.items():
        value = np.ascontiguousarray(value)
        inputs[f"in_{name}"] = value
        aps[name] = nc.dram_tensor(f"in_{name}", value.shape, mybir.dt.from_np(value.dtype),
                                   kind="ExternalInput").ap()
    aps["out"] = nc.dram_tensor("out_x", (P, KT, S), F32, kind="ExternalOutput").ap()
    build_program(nc, aps)
    r = run_bass_kernel_spmd(nc, [inputs], core_ids=[0])
    out = r.results[0]["out_x"]
    return out.transpose(1, 0, 2).reshape(1, D, S).transpose(0, 2, 1)
```

```python
import math
from contextlib import ExitStack

import numpy as np

import concourse.bass as bass
from concourse import mybir

F32 = mybir.dt.float32
F32R = mybir.dt.float32r
ALU = mybir.AluOpType
ACT = mybir.ActivationFunctionType
AX = mybir.AxisListType

P = 128
D = 1024
KT = D // P
S = 256
FF = 2816
FB = FF // P
HD = 64
EPS = 1e-6
ALPHA = 4.0 ** 0.25
QSCALE = HD ** -0.5
NEG = -1.0e30
TAKEN = -3.0e38
TOPK = 64
UC = 384
UNIT = KT * UC
RING = 4
SPLIT = 4
CHUNKS = 3 * FB
IDX_SCALE = (32 ** -0.5) * (8 ** -0.5)
GELU_C = 2.0 * math.sqrt(2.0 / math.pi)

VEC_PARTS = [("norm_g", 48), ("final_g", 8), ("cq_g", 2), ("b_mod", 96), ("g_sgu", 4), ("g_q", 2), ("g_k", 2),
             ("g_out", 16), ("ln1_g", 16), ("ln1_b", 16), ("ln2_g", 16), ("ln2_b", 16), ("cond", 16)]
VEC = {}
_at = 0
for _name, _n in VEC_PARTS:
    VEC[_name] = _at
    _at += _n
NVEC = _at
CONST_PARTS = [("ident", 128), ("ones", 128), ("halves", 128), ("swap", 128), ("mask_mix", 256),
               ("mask_causal", 256), ("mask_swa", 256), ("mask_na", 64), ("cos", 256), ("sin", 256)]
CONST = {}
_at = 0
for _name, _n in CONST_PARTS:
    CONST[_name] = _at
    _at += _n
NCONST = _at


def constants():
    c = np.zeros((P, NCONST), np.float32)

    def put(name, a):
        c[:, CONST[name]:CONST[name] + a.shape[1]] = a

    put("ident", np.eye(P, dtype=np.float32))
    put("ones", np.ones((P, P), np.float32))
    half = np.arange(P) // HD
    put("halves", (half[:, None] == half[None, :]).astype(np.float32))
    swap = np.zeros((P, P), np.float32)
    for m in range(P):
        if m % 32 < 16:
            swap[m + 16, m] = -1.0
        else:
            swap[m - 16, m] = 1.0
    put("swap", swap)
    dist = 255 - np.arange(P)[:, None] - np.arange(S)[None, :]
    count = (dist <= 128).astype(int) + (dist % 4 == 0) + (dist % 16 == 0)
    ok = (dist >= 0) & (count > 0)
    put("mask_mix", np.where(ok, np.log(np.maximum(count, 1).astype(np.float64)), NEG).astype(np.float32))
    put("mask_causal", np.where(dist >= 0, 0.0, NEG).astype(np.float32))
    put("mask_swa", np.where((dist >= 0) & (dist <= 127), 0.0, NEG).astype(np.float32))
    col = 63 - np.arange(P) % 64
    start = np.clip(col - 8, 0, 48)
    key = np.arange(64)[None, :]
    put("mask_na", np.where((key >= start[:, None]) & (key < start[:, None] + 16), 0.0, NEG).astype(np.float32))
    t = np.arange(S)
    inv = (1.0 / (np.float32(10000.0) ** (np.arange(16, dtype=np.float32) / np.float32(16)))).astype(np.float32)
    pos = np.stack([t // 64, t % 64]).astype(np.float32)
    feature = np.arange(P) % HD
    ang = pos[feature // 32] * inv[feature % 16][:, None]
    put("cos", np.cos(ang.astype(np.float32)).astype(np.float32))
    put("sin", np.sin(ang.astype(np.float32)).astype(np.float32))
    return c


def bucket_rows():
    d = np.maximum(255 - np.arange(384), 0)
    f = np.maximum(d, 1).astype(np.float32)
    large = 16 + (np.log(f / np.float32(16)) / np.float32(math.log(2048 / 16)) * np.float32(16)).astype(np.int32)
    b = np.where(d < 16, d, np.minimum(large, 31))
    return (np.arange(32)[:, None] == b[None, :]).astype(np.float32)


class Count:

    def __init__(self):
        self.n = {}

    def take(self, name, n):
        base = self.n.get(name, 0)
        self.n[name] = base + n
        return base


def tiles_cols(n):
    return -(-n // UC)


def build_program(nc, a):
    with ExitStack() as ctx:
        def sb(name, shape):
            return ctx.enter_context(nc.sbuf_tensor(name, shape, F32))

        def sb_r(name, shape):
            return ctx.enter_context(nc.sbuf_tensor(name, shape, F32R))

        def bank(name):
            return ctx.enter_context(nc.psum_tensor(name, [P, 512], F32))

        sems = {}

        def sem(name):
            if name not in sems:
                sems[name] = ctx.enter_context(nc.semaphore(name))
            return sems[name]

        X = sb("resid", [P, KT, 2 * S])
        N = sb("normed", [P, KT, 2 * S])
        ring = [sb(f"unit{i}", [P, UNIT]) for i in range(RING)]
        SQ = sb("squares", [P, KT, S])
        RS = sb("rstd", [P, 3, S])
        BT = sb("bias", [P, 16, 256])
        vec = sb("vec", [P, NVEC])
        con = sb("con", [P, NCONST])
        WS = sb("gate_w", [P, 2, 4, P])
        BS = sb("gate_b", [P, 2, 2, P])
        MOD = sb("mod", [P, 2, 2, 48])
        ROWS = sb("mod_rows", [2, 2, UC])
        MROW = sb("mod_blocks", [48, 4, P])
        small = sb("small", [P, 256])
        with ExitStack() as mixers:
            def mixer_sb(name, shape):
                return mixers.enter_context(nc.sbuf_tensor(name, shape, F32))

            SC = mixer_sb("scratch", [P, 6144])
            PJ = mixer_sb("proj", [P, 12, 2 * S])
            VT = mixer_sb("values", [P, 4, 512])
            ZV = mixer_sb("gate_v", [P, 4, 256])
        WHI = [sb_r(f"w_hi{i}", [P, D]) for i in range(SPLIT)]
        WLO = [sb_r(f"w_lo{i}", [P, D]) for i in range(SPLIT)]
        NHI = sb_r("normed_hi", [P, KT, S])
        NLO = sb_r("normed_lo", [P, KT, S])
        GHI = [sb_r(f"hidden_hi{i}", [P, S]) for i in range(2)]
        GLO = [sb_r(f"hidden_lo{i}", [P, S]) for i in range(2)]
        fE = [sb(f"silu{i}", [P, S]) for i in range(2)]
        fG = [sb(f"hidden{i}", [P, S]) for i in range(2)]
        flat = BT[:, :, :].rearrange("p h s -> p (h s)")
        OH = flat[0:32, 0:384]
        TB = flat[0:32, 384:400]
        ROW = flat[0:16, 512:896]

        acc = [bank(f"acc{i}") for i in range(4)]
        up = [bank(f"up{i}") for i in range(2)]
        stat = [bank(f"stat{i}") for i in range(2)]

        mean_bank = up[0]
        sum_bank = [stat[0], stat[1], up[1]]
        head_bank = [up[0], up[1], stat[0], stat[1]]

        def cst(name, n=None):
            return con[:, CONST[name]:CONST[name] + (n or dict(CONST_PARTS)[name])]

        def v(name, i):
            return vec[:, VEC[name] + i:VEC[name] + i + 1]

        ident, ones = cst("ident"), cst("ones")
        eps = small[:, 0:1]
        sinks = small[:, 16:32]
        GQ = small[:, 32:34]
        WX = small[:, 40:56].rearrange("p (i h) -> p i h", i=2)
        CS = small[:, 64:80].rearrange("p (s k) -> p k s", s=2)
        CTMP = small[:, 80:96]
        ATT = small[:, 96:96 + 24].rearrange("p (b n) -> p b n", b=3)
        LNS = small[:, 128:160].rearrange("p (t n) -> p t n", t=4)

        aS = [SC[:, i * 512:(i + 1) * 512] for i in range(3)]
        aP = [SC[:, 1536 + i * 512:2048 + i * 512] for i in range(3)]
        aT = [SC[:, 3072 + i * 1024:4096 + i * 1024].rearrange("p (s t) -> p s t", s=4) for i in range(2)]
        SEL = SC[:, 5120:5632].rearrange("p (i s) -> p i s", i=2)
        SCORE = SC[:, 5632:6144].rearrange("p (i s) -> p i s", i=2)
        RELU = [SC[:, i * 256:(i + 1) * 256] for i in range(2)]
        QI = SQ
        PJE = PJ[:, :, :].rearrange("p b (u t) -> p (b u) t", u=2)
        VTE = VT[:, :, :].rearrange("p (i u) n -> p i (u n)", u=2)
        NAB = BT[:, 0:12, :].rearrange("p (i h) s -> p i h s", i=2)

        scratch_rows = nc.dram_tensor("bias_rows", (16, 384), F32).ap()
        scratch_mod = nc.dram_tensor("mod_rows_dram", (2, 2, 6 * D), F32).ap()

        def rev(ap):
            return ap[:, ::-1]

        def at_up(u, half):
            return half if u == 0 else 3 * u - 1 + half

        def at_down(d):
            return min(4 + 3 * d, CHUNKS - 1)

        cnt = Count()
        stages = []
        loads = []
        free = []

        def add_units(name, start, n):
            loads.append((a[name], start, n))
            return cnt.take("unit", n)

        def by_tensor(n):
            base = cnt.take("unit_used", n)
            free.extend(("unit_used", base + j + 1) for j in range(n))
            return base

        def src_wait(*pairs):
            return list(pairs)

        def norm(kind, groups, src, dst, gain, shift, ready, centred=None):
            nb = sum(len(g) for g in groups)
            st = dict(kind="norm", ln=kind == "ln", groups=groups, src=src, dst=dst, gain=gain, shift=shift,
                      ready=ready, centred=centred, nb=nb, sq=cnt.take("sq", nb), ss=cnt.take("ss", len(groups)),
                      rstd=cnt.take("rstd", len(groups)))
            if st["ln"]:
                st["mean"] = cnt.take("mean", 1)
                st["cen"] = cnt.take("cen", nb)
                st["scaled"] = cnt.take("scaled", nb)
            st["out_sem"] = "ln_out" if st["ln"] else "rms_out"
            st["out"] = cnt.take(st["out_sem"], nb)
            st["rstd_free"] = cnt.n["rms_out"] - (0 if st["ln"] else nb) if "rms_out" in cnt.n else 0
            stages.append(st)
            return (st["out_sem"], st["out"] + nb)

        def ffn(units, tok, ready, resid):
            st = dict(kind="ffn", tok=tok, ready=ready, resid=resid, unit=add_units(*units, FB),
                      chunk=cnt.take("chunk_used", CHUNKS), hi=cnt.take("w_hi", CHUNKS),
                      split=cnt.take("w_split", CHUNKS), n_hi=cnt.take("n_hi", KT), n_split=cnt.take("n_split", KT),
                      act=cnt.take("hidden", FB), g_hi=cnt.take("hidden_hi", FB), exp=cnt.take("ffn_exp", FB), gated=cnt.take("gated", FB),
                      scaled=cnt.take("alpha", KT if resid else 0), res=cnt.take("resid", 8))
            free.extend(("w_split", st["split"] + at_down(d) + 1) for d in range(FB))
            stages[-1]["next_ffn"] = st
            stages.append(st)
            return ("resid", st["res"] + 8)

        def proj(jobs, units, ready):
            base = add_units(*units)
            used = by_tensor(units[2])
            last = {}
            for j, job in enumerate(jobs):
                last[job["unit"]] = j
            for j, job in enumerate(jobs):
                job["slot"] = base + job["unit"]
                job["last"] = last[job["unit"]] == j
                job["done"] = ("unit_used", used + job["unit"] + 1) if job["last"] else \
                    ("proj", cnt.take("proj", 1) + 1)
                e = job["evac"]
                name = "resid" if e[0] == "resid" else {"act": "evac_act", "dve": "evac_dve"}[job["eng"]]
                job["out"] = (name, cnt.take(name, 1) + 1)
                if e[0] == "resid" and e[1] is not None:
                    job["scaled"] = cnt.take("alpha", 1) + 1
            st = dict(kind="proj", jobs=jobs, ready=ready)
            stages.append(st)
            return [(n, max(j["out"][1] for j in jobs if j["out"][0] == n)) for n in {j["out"][0] for j in jobs}]

        def other(kind, sizes, **kw):
            st = dict(kind=kind, **kw)
            for name, n in sizes.items():
                st[name] = cnt.take(name, n)
            stages.append(st)
            return st

        def alternate(jobs):
            for j, job in enumerate(jobs):
                job.setdefault("eng", "act" if j % 2 == 0 else "dve")
            return jobs

        def in_block(b, tok=0, n=S):
            return lambda b_, t=tok: X[:, b_, t:t + n]

        def xs(tok):
            return lambda b: X[:, b, tok:tok + S]

        def ns(tok):
            return lambda b: N[:, b, tok:tok + S]

        def feature_job(unit, off, m, dst, q, n=S, tok=0, src=None, kts=KT, kstep=UC):
            return dict(unit=unit, off=off, m=m, kts=kts, kstep=kstep, tm=False, n=n, dst=dst,
                        src=src or (lambda k: N[:, k, tok:tok + n]), evac=("q" if q else "copy",))

        def token_job(unit, off, n, tile, dst):
            return dict(unit=unit, off=off, m=P, kts=KT, kstep=UC, tm=True, n=n, dst=dst,
                        src=lambda k: N[:, k, tile * P:(tile + 1) * P], evac=("copy",))

        def out_jobs(toks, gain):
            jobs = []
            for b in range(KT):
                for t in toks:
                    jobs.append(dict(unit=b // 3, off=(b % 3) * P, m=P, kts=KT, kstep=UC, tm=False, n=S,
                                     dst=X[:, b, t:t + S], src=lambda k, t=t: N[:, k, t:t + S],
                                     evac=("resid", gain(b, t)), eng="dve"))
            return jobs

        def attention(pairs, mods=None, **kw):
            if mods is not None:
                kw.update(mods=mods, mod_unit=add_units("mod_units", 16 * mods, 16), mod_used=by_tensor(16),
                          mod_row=cnt.take("mod_row", 16))
            else:
                kw.update(mods=None)
            tiles = []
            for n, pr in enumerate(pairs):
                for h in range(2):
                    for i in range(2):
                        tiles.append((n, h, i))
            return other("attn", dict(att_s=len(tiles), att_m=len(tiles), att_e=len(tiles), att_n=len(tiles),
                                      att_t=len(tiles), att_c=len(tiles), att_o=2 * len(pairs),
                                      att_out=len(pairs), att_add=len(tiles)),
                         pairs=pairs, tiles=tiles, **kw)

        x_ready = [("load_x", 16), ("load_con", 32)]
        for layer in range(2):
            ng = lambda j, layer=layer: (lambda b: v("norm_g", (layer * 3 + j) * 8 + b))
            r = norm("rms", [range(KT)], xs(0), ns(0), ng(0), None, x_ready if layer == 0 else [r])
            r = ffn(("ffn_units", (2 * layer) * FB), 0, [r], None)
            r = norm("rms", [range(KT)], xs(0), ns(0), ng(1), None, [r])
            if layer == 0:
                jobs = []
                for b in range(8):
                    jobs.append(feature_job(b // 3, (b % 3) * P, P, PJE[:, b, :], b < 4))
                for i in range(2):
                    jobs.append(token_job(2, 256, 128, i, VTE[:, i, 0:128]))
                for i in range(2):
                    jobs.append(token_job(3, 0, 384, i, VTE[:, i, 128:512]))
                for b in range(2):
                    jobs.append(feature_job(4, b * P, P, PJE[:, 16 + b, :], False))
                for b in range(4):
                    jobs.append(feature_job(4 + (b + 2) // 3, ((b + 2) % 3) * P, P, PJE[:, 8 + b, :], False))
                for i in range(2):
                    jobs.append(token_job(6, 0, 384, i, VTE[:, i, 512:896]))
                for i in range(2):
                    jobs.append(token_job(7, 0, 128, i, VTE[:, i, 896:1024]))
                jobs.append(feature_job(7, 128, 32, PJE[0:32, 20, :], False))
                wx = feature_job(7, 160, 8, PJE[0:8, 21, :], False)
                wx["evac"] = ("reverse", IDX_SCALE)
                jobs.append(wx)
                w = proj(alternate(jobs), ("even_units", 0, 8), [r])
                r = norm("rms", [range(2)], lambda b: PJE[:, 16 + b, :], lambda b: PJE[:, 18 + b, :],
                         lambda b: v("cq_g", b), None, w)
                cq = lambda k: PJE[:, 18 + k, :]
                jobs = [feature_job(0, b * P, P, PJE[:, 12 + b, :], True, src=cq, kts=2, kstep=512)
                        for b in range(4)]
                for h in range(8):
                    j = feature_job(0, 1024 + h * 32, 32, QI[0:32, h, :], False, src=cq, kts=2, kstep=256)
                    j["evac"] = ("reverse", 1.0)
                    jobs.append(j)
                w = proj(alternate(jobs), ("even_units", 8, 1), [r])
                st = other("index", dict(wx_t=2, wx=2, ix_s=16, ix_r=16, ix_a=16, top=1), ready=w)
                pairs = []
                for j in range(8):
                    mix = j < 4
                    pairs.append(dict(q=(lambda i, j=j: PJE[:, (j if j < 4 else 8 + j), i * P:(i + 1) * P]),
                                      k=(lambda h, i, j=j: PJE[:, 4 + j, 0:(i + 1) * P]),
                                      v=(lambda h, s, j=j: VTE[:, s, (2 * j + h) * HD:(2 * j + h + 1) * HD]),
                                      bias=(lambda h, i, j=j: BT[:, 2 * j + h, (1 - i) * P:2 * P]),
                                      keys=lambda i: i + 1, sel=not mix, sink=None, dst=N[:, j, 0:S]))
                at = attention(pairs, mods=0, ready=[("top", st["top"] + 1)] + w, bias_ready=("bias0", 1))
                r = proj(out_jobs([0], lambda b, t: None), ("even_units", 9, 3), [("att_out", at["att_out"] + 8)])[0]
            else:
                jobs = []
                for b in range(8):
                    jobs.append(feature_job(b // 3, (b % 3) * P, P, PJE[:, b, :], True))
                jobs.append(feature_job(2, 256, P, PJE[:, 8, :], False))
                for i in range(2):
                    jobs.append(token_job(3, 0, 128, i, VTE[:, i, 0:128]))
                w = proj(alternate(jobs), ("swa_units", 0, 4), [r])
                pairs = []
                for j in range(8):
                    pairs.append(dict(q=(lambda i, j=j: PJE[:, j, i * P:(i + 1) * P]),
                                      k=(lambda h, i: PJE[:, 8, 0:(i + 1) * P]),
                                      v=(lambda h, s: VTE[:, s, h * HD:(h + 1) * HD]),
                                      bias=(lambda h, i, j=j: BT[:, 8 * h + j, (1 - i) * P:2 * P]),
                                      keys=lambda i: i + 1, sel=False,
                                      sink=(lambda h, j=j: sinks[:, 8 * h + j:8 * h + j + 1]), dst=N[:, j, 0:S]))
                at = attention(pairs, mods=1, ready=w, bias_ready=("bias1", 1))
                r = proj(out_jobs([0], lambda b, t: None), ("swa_units", 4, 3), [("att_out", at["att_out"] + 8)])[0]
            first_att = at if layer == 0 else first_att
            second_att = at
            r = norm("rms", [range(KT)], xs(0), ns(0), ng(2), None, [r])
            r = ffn(("ffn_units", (2 * layer + 1) * FB), 0, [r], None)
        r = norm("rms", [range(KT)], xs(0), xs(0), lambda b: v("final_g", b), None, [r])

        other("mod", dict(mod=2, mod_t=1))
        x_now, c_now = r, ("load_ctx", 16)

        def modv(layer, which, stream):
            return lambda b: MOD[:, layer, stream, which * 8 + b:which * 8 + b + 1]

        na_att = []
        for layer in range(2):
            both = layer == 0
            toks = [0, S] if both else [0]
            T = len(toks) * S
            rx = norm("ln", [range(KT)], xs(0), ns(0), modv(layer, 1, 0), modv(layer, 0, 0),
                      [x_now, ("mod", 2)], ns(0))
            rc = norm("ln", [range(KT)], xs(S), ns(S), modv(layer, 1, 1), modv(layer, 0, 1), [c_now], ns(S))
            jobs = []

            def feats(unit, off, blk, q, streams):
                n = len(streams) * S
                tok = streams[0] * S
                jobs.append(feature_job(unit, off, P, PJ[:, blk, tok:tok + n], q, n=n, tok=tok))

            mine, all_ = (([0, 1], [0, 1]) if both else ([0], [0, 1]))
            for b in range(3):
                feats(0, b * P, b, True, mine)
            for b in range(3):
                feats(1, b * P, 3 + b, False, all_)
            for i in range(4):
                jobs.append(token_job(2, 0, 384, i, VT[:, i, 0:384]))
            for b in range(2):
                feats(3, b * P, 6 + b, False, mine)
            for i in range(T // P):
                jobs.append(token_job(3, 256, 128, i, ZV[:, i, 0:128]))
            for i in range(T // P):
                jobs.append(token_job(4, 0, 128, i, ZV[:, i, 128:256]))
            for b in range(2):
                feats(4, (1 + b) * P, 8 + b, False, mine)
            feats(5, 0, 10, False, mine)
            feats(5, P, 11, False, all_)
            for i in range(4):
                jobs.append(token_job(5, 256, 128, i, VT[:, i, 384:512]))
            w = proj(alternate(jobs), ("mix2_units", layer * 9, 6), [rx, rc])
            nchunk = T // S * 2
            gt = other("gate", dict(g_sq=nchunk, g_w=nchunk, g_e=nchunk, g_z=nchunk, zc=T // P, zr=T // P, zn=T // P,
                                    g_mm=T // P, g_out=2 * (T // P)), layer=layer, T=T, ready=w)
            items = [(8 + b, 0) for b in range(4)] + ([(8 + b, 1) for b in range(4)] if both else [(11, 1)])
            rp = other("rope", dict(r_sq=len(items), r_ss=len(items), r_rs=len(items), r_y=len(items) - 1, r_rot=4,
                                    r_out=len(items)), layer=layer, items=items, ready=w)
            pairs = []
            for j in range(3):
                pairs.append(dict(q=(lambda i, j=j: PJ[:, j, i * P:(i + 1) * P]),
                                  k=(lambda h, i, j=j: PJ[:, 3 + j, 0:512]),
                                  v=(lambda h, s, j=j: VT[:, s, (2 * j + h) * HD:(2 * j + h + 1) * HD]),
                                  bias=(lambda h, i, j=j: NAB[:, i, 2 * j + h, :]),
                                  keys=lambda i: 4, sel=False, sink=None, dst=N[:, j, 0:S]))
            for j in range(3):
                pairs.append(dict(q=(lambda i, j=j: PJ[:, 8 + j, i * P:(i + 1) * P]),
                                  k=(lambda h, i: PJ[:, 11, 0:512]),
                                  v=(lambda h, s: VT[:, s, 384 + h * HD:384 + (h + 1) * HD]),
                                  bias=None, keys=lambda i: 4, sel=False, sink=None, dst=N[:, 5 + j, 0:S]))
            if both:
                for j in range(3):
                    pairs.append(dict(q=(lambda i, j=j: PJ[:, j, S + i * P:S + (i + 1) * P]),
                                      k=(lambda h, i, j=j: PJ[:, 3 + j, S:2 * S]),
                                      v=(lambda h, s, j=j: VT[:, 2 + s, (2 * j + h) * HD:(2 * j + h + 1) * HD]),
                                      bias=None, keys=lambda i: 2, sel=False, sink=None, dst=N[:, j, S:2 * S]))
                for j in range(3):
                    pairs.append(dict(q=(lambda i, j=j: PJ[:, 8 + j, S + i * P:S + (i + 1) * P]),
                                      k=(lambda h, i: PJ[:, 11, S:2 * S]),
                                      v=(lambda h, s: VT[:, 2 + s, 384 + h * HD:384 + (h + 1) * HD]),
                                      bias=None, keys=lambda i: 2, sel=False, sink=None, dst=N[:, 5 + j, S:2 * S]))
            at = attention(pairs, ready=[("r_out", rp["r_out"] + len(items))], bias_ready=(f"bias{2 + layer}", 1))
            na_att.append(at)
            done = [("att_out", at["att_out"] + len(pairs)), ("g_out", gt["g_out"] + 2 * (T // P))]
            merged = []
            for t in toks:
                merged.append(norm("rms", [range(3), range(3, 5), range(5, 8)], ns(t), ns(t),
                                   lambda b, layer=layer: v("g_out", layer * 8 + b), None, done))
            r = proj(out_jobs(toks, lambda b, t, layer=layer: modv(layer, 2, t // S)(b)),
                     ("mix2_units", layer * 9 + 6, 3), merged)[0]
            for which, t in enumerate(toks):
                ln = lambda name, layer=layer: (lambda b: v(name, layer * 8 + b))
                q = norm("ln", [range(KT)], xs(t), xs(t), ln("ln1_g"), ln("ln1_b"), [r], ns(t))
                q = norm("ln", [range(KT)], xs(t), ns(t), modv(layer, 4, which), modv(layer, 3, which), [q],
                         ns(t))
                q = ffn(("ffn2_units", layer * FB), t, [q], modv(layer, 5, which))
                q = norm("ln", [range(KT)], xs(t), xs(t), ln("ln2_g"), ln("ln2_b"), [q], ns(t))
                if which == 0:
                    x_now = q
                else:
                    c_now = q
        total_units = cnt.n["unit"]
        landed = [sem(f"unit_landed{i}") for i in range(RING)]

        def unit_slot(n):
            return ring[n % RING]

        def wait_all(eng, pairs):
            for name, value in pairs:
                eng.wait_ge(sem(name), value)

        for name in list(cnt.n) + ["load_x", "load_con", "load_ctx", "load_oh", "load_misc", "rows", "rows_sb",
                                   "rows_dram", "bt0", "bt1", "nab0", "nab1", "bias0", "bias1", "bias2",
                                   "bias3", "store", "dve_step", "act_step", "unit_used", "setup", "cond_exp", "cond",
                                   "mod_stored0", "mod_stored1", "mod_read"]:
            sem(name)

        def evacuate(eng, j, job, copy):
            bank_ = acc[j % 4]
            m, n = job["m"], job["n"]
            kind = job["evac"][0]
            if kind == "copy":
                return copy(job["dst"], bank_[0:m, 0:n], 1.0)
            factor = QSCALE if kind == "q" else job["evac"][1]
            return copy(job["dst"].rearrange("p (i t) -> p i t", t=P)[:, :, ::-1],
                        bank_[0:m, 0:n].rearrange("p (i t) -> p i t", t=P), factor)

        def gate_chunks(st):
            if st["T"] == 2 * S:
                return [PJ[:, b, :].rearrange("p (i t) -> p i t", i=2) for b in (6, 7)] + [
                    ZV[:, 0:2, :], ZV[:, 2:4, :]]
            return [PJ[:, 6:8, 0:S], ZV[:, 0:2, :]]

        def gate_tmp(c):
            t = SC[:, (c % 2) * 512:(c % 2 + 1) * 512]
            return t.rearrange("p (i t) -> p i t", i=2)

        block = ctx.enter_context(nc.Block())

        @block.sync
        def _(sp):
            def steady(n, trips):
                if n < RING:
                    return False
                step = free[n][1] - free[n - RING][1]
                return all(free[n - RING + RING * t + j] == (free[n - RING][0], free[n - RING + j][1] + step * t)
                           for t in range(trips) for j in range(RING))

            n = 0
            for src, start, count in loads:
                at = 0
                while at < count:
                    m = n + at
                    trips = (count - at) // RING
                    while trips > 1 and not steady(m, trips):
                        trips -= 1
                    if trips > 1:
                        name = free[m - RING][0]
                        step = free[m][1] - free[m - RING][1]
                        with sp.Fori(0, trips) as i:
                            for j in range(RING):
                                sp.wait_ge(sem(name), i * step + free[m - RING + j][1])
                                sp.dma_start(ring[(m + j) % RING][:, :],
                                             src[bass.ds(i * RING + (start + at + j), 1), :, :].rearrange(
                                                 "o p c -> (o p) c")).then_inc(landed[(m + j) % RING], 16)
                        at += trips * RING
                    else:
                        if m >= RING:
                            sp.wait_ge(sem(free[m - RING][0]), free[m - RING][1])
                        sp.dma_start(ring[m % RING][:, :], src[start + at]).then_inc(landed[m % RING], 16)
                        at += 1
                n += count
            sp.wait_ge(sem(x_now[0]), x_now[1])
            sp.dma_start(a["out"], X[:, :, 0:S]).then_inc(sem("store"), 16)
            sp.wait_ge(sem("store"), 16)

        @block.gpsimd
        def _(pool):
            pool.dma_start(X[:, :, 0:S], a["x"]).then_inc(sem("load_x"), 16)
            pool.dma_start(con[:, :], a["con"]).then_inc(sem("load_con"), 16)
            pool.dma_start(vec[:, :], a["vec"]).then_inc(sem("load_con"), 16)
            pool.dma_start(OH, a["onehot"]).then_inc(sem("load_oh"), 16)
            pool.dma_start(TB, a["table"]).then_inc(sem("load_oh"), 16)
            pool.dma_start(X[:, :, S:2 * S], a["ctx"]).then_inc(sem("load_ctx"), 16)
            pool.dma_start(sinks, bass.AP(a["sinks"].tensor, 0, [[0, P], [1, 16]])).then_inc(sem("load_misc"), 16)
            pool.dma_start(WS[:, :, :, :], a["w_s"]).then_inc(sem("load_misc"), 16)
            for half in range(2):
                for layer in range(2):
                    src = bass.AP(a["b_s"].tensor, layer * 4 * P + half * P, [[0, HD], [2 * P, 2], [1, P]])
                    pool.dma_start(BS[half * HD:(half + 1) * HD, layer, :, :], src).then_inc(sem("load_misc"), 16)
            pool.wait_ge(sem("rows_sb"), 1)
            pool.dma_start(scratch_rows, ROW).then_inc(sem("rows_dram"), 16)
            pool.wait_ge(sem("rows_dram"), 16)
            diagonal = bass.AP(scratch_rows.tensor, 0, [[1, P], [384, 16], [1, 256]])

            def add_mask(region, mask, shape, done):
                pool.tensor_tensor(region, region, mask.unsqueeze(1).to_broadcast(shape), ALU.add).then_inc(
                    sem(done), 1)

            pool.dma_start(BT[:, :, :], diagonal).then_inc(sem("bt0"), 16)
            pool.wait_ge(sem("bt0"), 16)
            pool.wait_ge(sem("load_con"), 32)
            pool.tensor_tensor(BT[:, 0:8, :], BT[:, 0:8, :],
                               cst("mask_mix").unsqueeze(1).to_broadcast([P, 8, 256]), ALU.add)
            add_mask(BT[:, 8:16, :], cst("mask_causal"), [P, 8, 256], "bias0")
            def mod_rows(st):
                for u in range(16):
                    pool.wait_ge(sem("mod_row"), st["mod_row"] + u + 1)
                    pool.dma_start(scratch_mod[st["mods"], :, u * UC:(u + 1) * UC], ROWS[:, u % 2, :]).then_inc(
                        sem(f"mod_stored{u % 2}"), 16)

            mod_rows(first_att)
            pool.wait_ge(sem("att_m"), first_att["att_m"] + len(first_att["tiles"]))
            pool.dma_start(BT[:, :, :], diagonal).then_inc(sem("bt1"), 16)
            pool.wait_ge(sem("bt1"), 16)
            add_mask(BT[:, :, :], cst("mask_swa"), [P, 16, 256], "bias1")
            mod_rows(second_att)
            for half in range(2):
                pool.wait_ge(sem(f"mod_stored{half}"), 16 * 16)
            pool.dma_start(MROW[:, :, :], bass.AP(scratch_mod.tensor, 0, [[P, 48], [6 * D, 4], [1, P]])).then_inc(
                sem("mod_read"), 16)
            for layer in range(2):
                before = second_att if layer == 0 else na_att[0]
                pool.wait_ge(sem("att_m"), before["att_m"] + len(before["tiles"]))
                nd = 0
                for r_ in range(4):
                    part = 0 if r_ % 2 else HD
                    for h in range(6):
                        src = bass.AP(a["rpb"].tensor, ((layer * 6 + h) * 7 + 3 - r_) * 128,
                                      [[1, HD], [128, 4], [1, 64]])
                        dst = NAB[part:part + HD, r_ // 2, h, :].rearrange("p (k c) -> p k c", k=4)
                        pool.dma_start(dst, src).then_inc(sem(f"nab{layer}"), 16)
                        nd += 16
                pool.wait_ge(sem(f"nab{layer}"), nd)
                add_mask(BT[:, 0:12, :].rearrange("p h (k c) -> p (h k) c", c=64), cst("mask_na"),
                         [P, 48, 64], f"bias{2 + layer}")

        @block.tensor
        def _(pe):
            mm = nc.tensor.matmul

            def norm_stage(st):
                if st["ln"]:
                    wait_all(pe, st["ready"])
                    for j in range(st["nb"]):
                        last = mm(mean_bank[:, 0:S], ones, st["src"](j), start=j == 0, stop=j == st["nb"] - 1)
                    last.then_inc(sem("mean"), 1)
                n = 0
                for g, blocks in enumerate(st["groups"]):
                    for j, b in enumerate(blocks):
                        pe.wait_ge(sem("sq"), st["sq"] + n + 1)
                        last = mm(sum_bank[g][:, 0:S], ones, SQ[:, n, :],
                                  start=j == 0, stop=j == len(blocks) - 1, skip_group_check=True)
                        n += 1
                    last.then_inc(sem("ss"), 1)

            def ffn_stage(st):
                def parts(out, w, k, hi, lo, first, last):
                    cols = slice(k * P, (k + 1) * P)
                    mm(out, WHI[w][:, cols], hi, start=first, stop=False, skip_group_check=True)
                    mm(out, WHI[w][:, cols], lo, start=False, stop=False, skip_group_check=True)
                    return mm(out, WLO[w][:, cols], hi, start=False, stop=last, skip_group_check=True)

                def ffn_up(at, u, half, wait):
                    pe.wait_ge(sem("w_split"), wait(st["split"] + at + 1, 3))
                    for k in range(KT):
                        if u == 0 and half == 0:
                            pe.wait_ge(sem("n_split"), st["n_split"] + k + 1)
                        last = parts(up[u % 2][:, half * S:(half + 1) * S], at % SPLIT, k, NHI[:, k, :],
                                     NLO[:, k, :], k == 0 and half == 0, k == KT - 1)
                    last.then_inc(sem("chunk_used"), 1)

                def ffn_down(at, d, first, wait):
                    pe.wait_ge(sem("w_split"), wait(st["split"] + at + 1, 3))
                    pe.wait_ge(sem("gated"), wait(st["gated"] + d + 1, 1))
                    for b in range(KT):
                        last = parts(acc[b // 2][:, (b % 2) * S:(b % 2 + 1) * S], at % SPLIT, b, GHI[d % 2][:, :],
                                     GLO[d % 2][:, :], first and b % 2 == 0, True)
                    last.then_inc(sem("chunk_used"), 1)

                def both(u, wait):
                    if u >= 2:
                        pe.wait_ge(sem("hidden"), wait(st["act"] + u - 1, 1))
                    ffn_up(at_up(u, 0), u, 0, wait)
                    ffn_up(at_up(u, 1), u, 1, wait)

                def fixed(value, per):
                    return value

                both(0, fixed)
                both(1, fixed)
                ffn_down(at_down(0), 0, True, fixed)
                trips = (FB - 2) // RING
                with pe.Fori(0, trips) as i:
                    def turning(value, per):
                        return i * (RING * per) + value

                    for j in range(RING):
                        both(2 + j, turning)
                        ffn_down(at_down(1 + j), 1 + j, False, turning)
                ffn_down(at_down(FB - 1), FB - 1, False, fixed)

            def proj_stage(st):
                wait_all(pe, st["ready"])
                jobs = st["jobs"]
                seen = set()
                for j, job in enumerate(jobs):
                    if job["slot"] not in seen:
                        seen.add(job["slot"])
                        pe.wait_ge(landed[job["slot"] % RING], 16 * (job["slot"] // RING + 1))
                    if j >= 4:
                        pe.wait_ge(sem(jobs[j - 4]["out"][0]), jobs[j - 4]["out"][1])
                    w = unit_slot(job["slot"])
                    for k in range(job["kts"]):
                        cols = w[:, k * job["kstep"] + job["off"]:k * job["kstep"] + job["off"] +
                                 (job["n"] if job["tm"] else job["m"])] if job["off"] < 1024 or job["kts"] == KT \
                            else w[:, 1024 + k * 256 + job["off"] - 1024:1024 + k * 256 + job["off"] - 1024 + job["m"]]
                        lhs, rhs = (job["src"](k), cols) if job["tm"] else (cols, job["src"](k))
                        last = mm(acc[j % 4][0:job["m"], 0:job["n"]], lhs, rhs, start=k == 0,
                                  stop=k == job["kts"] - 1, skip_group_check=True)
                    last.then_inc(sem("unit_used" if job["last"] else "proj"), 1)

            def index_stage(st):
                wait_all(pe, st["ready"])
                for i in range(2):
                    nc.tensor.transpose(acc[2 + i][:, 0:8], PJE[0:8, 21, i * P:(i + 1) * P],
                                        ident[0:8, 0:8]).then_inc(sem("wx_t"), 1)
                for n in range(16):
                    i, h = n // 8, n % 8
                    if n >= 2:
                        pe.wait_ge(sem("ix_r"), st["ix_r"] + n - 1)
                    mm(acc[n % 2][:, 0:(i + 1) * P], QI[0:32, h, i * P:(i + 1) * P], PJE[0:32, 20, 0:(i + 1) * P],
                       start=True, stop=True).then_inc(sem("ix_s"), 1)

            def attn_stage(st):
                pairs, tiles = st["pairs"], st["tiles"]
                wait_all(pe, st["ready"])
                nt = len(tiles)

                def scores(t):
                    n, h, i = tiles[t]
                    pr = pairs[n]
                    if t >= 3:
                        pe.wait_ge(sem("att_e"), st["att_e"] + t - 2)
                    lo = h * HD
                    mm(acc[t % 3][:, 0:pr["keys"](i) * P], pr["q"](i)[lo:lo + HD], pr["k"](h, i)[lo:lo + HD],
                       start=True, stop=True).then_inc(sem("att_s"), 1)

                def turn(t):
                    n, h, i = tiles[t]
                    pe.wait_ge(sem("att_n"), st["att_n"] + t + 1)
                    if t >= 2:
                        pe.wait_ge(sem("att_c"), st["att_c"] + t - 1)
                    for s in range(pairs[n]["keys"](i)):
                        last = nc.tensor.transpose(up[t % 2][:, s * P:(s + 1) * P], aP[t % 3][:, s * P:(s + 1) * P],
                                                   ident)
                    last.then_inc(sem("att_t"), 1)

                def values(t):
                    n, h, i = tiles[t]
                    pr = pairs[n]
                    pe.wait_ge(sem("att_c"), st["att_c"] + t + 1)
                    if h == 0 and n >= 2:
                        pe.wait_ge(sem("att_out"), st["att_out"] + n - 1)
                    o = stat[n % 2][h * HD:(h + 1) * HD]
                    pT = aT[(2 * n + h) % 2]
                    ks = pr["keys"](1)
                    for s in range(ks):
                        t0 = P if s >= pr["keys"](0) else 0
                        last = mm(o[:, t0:S], pr["v"](h, s), pT[:, s, t0:S], start=s == 0, stop=s == ks - 1,
                                  skip_group_check=True)
                    last.then_inc(sem("att_o"), 1)

                def modulation(t):
                    u, half = t // 2, t % 2
                    n = st["mod_unit"] + u
                    if half == 0:
                        pe.wait_ge(landed[n % RING], 16 * (n // RING + 1))
                        if u:
                            pe.wait_ge(sem("mod_row"), st["mod_row"] + u)
                    for k in range(4 * half, 4 * half + 4):
                        last = mm(acc[3][0:2, 0:UC], CS[:, k, :], unit_slot(n)[:, k * UC:(k + 1) * UC],
                                  start=k == 0, stop=k == KT - 1, skip_group_check=True)
                    if half:
                        last.then_inc(sem("unit_used"), 1)

                if st["mods"] is not None:
                    pe.wait_ge(sem("cond"), 1)
                for t in range(nt + 3):
                    if t < nt:
                        scores(t)
                    if 0 <= t - 2 < nt:
                        turn(t - 2)
                    if 0 <= t - 3 < nt and tiles[t - 3][2] == 1:
                        values(t - 3)
                    if st["mods"] is not None and t < nt:
                        modulation(t)

            def gate_stage(st):
                T, layer = st["T"], st["layer"]
                pe.wait_ge(sem("load_misc"), 16 * 6)
                for tb in range(T // P):
                    pe.wait_ge(sem("zn"), st["zn"] + tb + 1)
                    for g in range(4):
                        h = g % 2
                        last = mm(acc[tb][h * HD:(h + 1) * HD, (g // 2) * P:(g // 2 + 1) * P],
                                  ZV[:, tb, g * HD:(g + 1) * HD], WS[:, layer, g, :], start=True, stop=True,
                                  skip_group_check=True)
                    last.then_inc(sem("g_mm"), 1)

            def rope_stage(st):
                for n, (b, s) in enumerate(st["items"]):
                    pe.wait_ge(sem("r_sq"), st["r_sq"] + n + 1)
                    if n >= 4:
                        pe.wait_ge(sem("r_rs"), st["r_rs"] + n - 3)
                    mm(head_bank[n % 4][:, 0:S], cst("halves"), SQ[:, n, :], start=True,
                       stop=True, skip_group_check=True).then_inc(sem("r_ss"), 1)
                for n in range(4):
                    pe.wait_ge(sem("r_y"), st["r_y"] + n + 1)
                    mm(acc[n][:, 0:S], cst("swap"), SC[:, n * S:(n + 1) * S],
                       start=True, stop=True, skip_group_check=True).then_inc(sem("r_rot"), 1)

            def mod_stage(st):
                pe.wait_ge(sem("mod_read"), 16)
                for n in range(4):
                    last = nc.tensor.transpose(acc[0][:, n * 48:(n + 1) * 48], MROW[:, n, :], ident[0:48, 0:48])
                last.then_inc(sem("mod_t"), 1)

            pe.wait_ge(sem("load_oh"), 32)
            mm(stat[1][0:16, 0:384], TB, OH, start=True, stop=True).then_inc(sem("rows"), 1)
            pe.wait_ge(sem("rows_sb"), 1)
            run = dict(norm=norm_stage, ffn=ffn_stage, proj=proj_stage, index=index_stage, attn=attn_stage,
                       gate=gate_stage, rope=rope_stage, mod=mod_stage)
            for st in stages:
                run[st["kind"]](st)

        @block.scalar
        def _(act):
            fn = nc.scalar.activation
            steps = [0]

            def link(ins):
                steps[0] += 1
                ins.then_inc(sem("act_step"), 1)
                act.wait_ge(sem("act_step"), steps[0])

            def norm_stage(st):
                wait_all(act, st["ready"])
                n = 0
                for g, blocks in enumerate(st["groups"]):
                    for b in blocks:
                        if st["ln"]:
                            act.wait_ge(sem("cen"), st["cen"] + n + 1)
                            src = st["centred"](b)
                        else:
                            src = st["src"](b)
                        fn(SQ[:, n, :], src, ACT.Square).then_inc(sem("sq"), 1)
                        n += 1
                if "next_ffn" in st:
                    ffn_ahead(st["next_ffn"])
                for g, blocks in enumerate(st["groups"]):
                    act.wait_ge(sem("ss"), st["ss"] + g + 1)
                    if g == 0 and st["rstd_free"] > 0:
                        act.wait_ge(sem("rms_out"), st["rstd_free"])
                    link(fn(RS[:, g, :], sum_bank[g][:, 0:S], ACT.Ln,
                            bias=eps, scale=1.0 / (len(blocks) * P)))
                    fn(RS[:, g, :], RS[:, g, :], ACT.Exp, scale=-0.5).then_inc(sem("rstd"), 1)
                if st["ln"]:
                    for b in range(st["nb"]):
                        act.wait_ge(sem("scaled"), st["scaled"] + b + 1)
                        fn(st["dst"](b), st["centred"](b), ACT.Identity,
                           bias=st["shift"](b)).then_inc(sem("ln_out"), 1)

            def fixed(value, per):
                return value

            def round_chunk(st, at, u, third, wait):
                n = st["unit"] + u
                act.wait_ge(landed[n % RING], wait(16 * (n // RING + 1), 16 / RING))
                if at >= SPLIT:
                    act.wait_ge(sem("chunk_used"), wait(st["chunk"] + at - SPLIT + 1, 3))
                fn(WHI[at % SPLIT][:, :], unit_slot(n)[:, third * D:(third + 1) * D], ACT.Copy).then_inc(
                    sem("w_hi"), 1)

            def ffn_ahead(st):
                round_chunk(st, 0, 0, 0, fixed)
                round_chunk(st, 1, 0, 1, fixed)

            def ffn_stage(st):
                for k in range(KT):
                    act.wait_ge(sem(st["ready"][0][0]), st["ready"][0][1] - KT + k + 1)
                    fn(NHI[:, k, :], N[:, k, st["tok"]:st["tok"] + S], ACT.Copy).then_inc(sem("n_hi"), 1)
                round_chunk(st, at_up(1, 0), 1, 0, fixed)
                round_chunk(st, at_up(1, 1), 1, 1, fixed)

                def hidden(d, ahead, wait):
                    act.wait_ge(sem("chunk_used"), wait(st["chunk"] + at_up(d, 1) + 1, 3))
                    if d >= 2:
                        act.wait_ge(sem("gated"), wait(st["gated"] + d - 1, 1))
                    fn(fE[d % 2][:, :], up[d % 2][:, 0:S], ACT.Exp, scale=-1.0).then_inc(sem("ffn_exp"), 1)
                    round_chunk(st, at_down(d), d, 2, wait)
                    act.wait_ge(sem("hidden"), wait(st["act"] + d + 1, 1))
                    if d >= 2:
                        act.wait_ge(sem("chunk_used"), wait(st["chunk"] + at_down(d - 2) + 1, 3))
                    fn(GHI[d % 2][:, :], fG[d % 2][:, :], ACT.Copy).then_inc(sem("hidden_hi"), 1)
                    if ahead:
                        round_chunk(st, at_up(d + 2, 0), d + 2, 0, wait)
                        round_chunk(st, at_up(d + 2, 1), d + 2, 1, wait)

                for d in range(4):
                    hidden(d, True, fixed)
                with act.Fori(0, (FB - 6) // RING) as i:
                    def turning(value, per):
                        return i * int(RING * per) + value

                    for d in range(4, 4 + RING):
                        hidden(d, True, turning)
                for d in (FB - 2, FB - 1):
                    hidden(d, False, fixed)

            def proj_stage(st):
                for j, job in enumerate(st["jobs"]):
                    if job["eng"] == "act":
                        act.wait_ge(sem(job["done"][0]), job["done"][1])
                        evacuate(act, j, job, lambda d, s, f: fn(d, s, ACT.Copy, scale=f)).then_inc(
                            sem("evac_act"), 1)

            def index_stage(st):
                for n in range(16):
                    i = n // 8
                    act.wait_ge(sem("ix_s"), st["ix_s"] + n + 1)
                    if n >= 2:
                        act.wait_ge(sem("ix_a"), st["ix_a"] + n - 1)
                    fn(RELU[n % 2][:, 0:(i + 1) * P], acc[n % 2][:, 0:(i + 1) * P], ACT.Relu).then_inc(
                        sem("ix_r"), 1)

            def attn_stage(st):
                pairs, tiles = st["pairs"], st["tiles"]

                def exps(t):
                    n, h, i = tiles[t]
                    pr = pairs[n]
                    w = pr["keys"](i) * P
                    act.wait_ge(sem("att_m"), st["att_m"] + t + 1)
                    if t >= 3:
                        act.wait_ge(sem("att_t"), st["att_t"] + t - 2)
                    m = ATT[:, t % 3]
                    nm = m[:, 0:1]
                    if pr["bias"] is None:
                        last = fn(aP[t % 3][:, 0:w], acc[t % 3][:, 0:w], ACT.Exp, bias=nm, accum_out=m[:, 2:3])
                    else:
                        wb = min(w, 256)
                        last = fn(aP[t % 3][:, 0:wb], aS[t % 3][:, 0:wb], ACT.Exp, bias=nm, scale=-1.0,
                                  accum_out=m[:, 2:3])
                        if w > wb:
                            last = fn(aP[t % 3][:, wb:w], acc[t % 3][:, wb:w], ACT.Exp, bias=nm,
                                      accum_out=m[:, 3:4])
                    if pr["sink"] is not None:
                        last = fn(m[:, 3:4], pr["sink"](h), ACT.Exp, bias=nm)
                    last.then_inc(sem("att_e"), 1)

                def copies(t):
                    n, h, i = tiles[t]
                    ks = pairs[n]["keys"](i)
                    b = 2 * n + h
                    act.wait_ge(sem("att_t"), st["att_t"] + t + 1)
                    if b >= 2 and i == 0:
                        act.wait_ge(sem("att_o"), st["att_o"] + b - 1)
                    fn(aT[b % 2][:, 0:ks, i * P:(i + 1) * P][:, :, ::-1],
                       up[t % 2][:, 0:ks * P].rearrange("p (s t) -> p s t", t=P), ACT.Copy).then_inc(sem("att_c"), 1)

                def modulation(u):
                    act.wait_ge(sem("unit_used"), st["mod_used"] + u + 1)
                    if st["mod_row"] + u >= 2:
                        act.wait_ge(sem(f"mod_stored{u % 2}"), 16 * ((st["mod_row"] + u) // 2))
                    fn(ROWS[:, u % 2, :], acc[3][0:2, 0:UC], ACT.Copy).then_inc(sem("mod_row"), 1)

                nt = len(tiles)
                for t in range(nt + 2):
                    if t < nt:
                        exps(t)
                    if 0 <= t - 2 < nt:
                        copies(t - 2)
                    if st["mods"] is not None and t % 2 == 0 and t >= 2:
                        modulation(t // 2 - 1)

            def gate_stage(st):
                T = st["T"]
                wait_all(act, st["ready"])
                chunks = gate_chunks(st)
                for c, z in enumerate(chunks):
                    if c >= 2:
                        act.wait_ge(sem("g_z"), st["g_z"] + c - 1)
                    fn(gate_tmp(c), z, ACT.Square).then_inc(sem("g_sq"), 1)
                    act.wait_ge(sem("g_w"), st["g_w"] + c + 1)
                    fn(gate_tmp(c), gate_tmp(c), ACT.Exp, scale=-GELU_C).then_inc(sem("g_e"), 1)
                for tb in range(T // P):
                    act.wait_ge(sem("zc"), st["zc"] + tb + 1)
                    link(fn(SC[:, 2048 + tb * 256:2304 + tb * 256], ZV[:, tb, :], ACT.Square, accum_out=LNS[:, tb, 2:3]))
                    link(fn(LNS[:, tb, 3:4], LNS[:, tb, 2:3], ACT.Ln, bias=eps, scale=1.0 / 256))
                    fn(LNS[:, tb, 4:5], LNS[:, tb, 3:4], ACT.Exp, scale=-0.5).then_inc(sem("zr"), 1)

            def rope_stage(st):
                for n, (b, s) in enumerate(st["items"]):
                    fn(SQ[:, n, :], PJ[:, b, s * S:(s + 1) * S], ACT.Square).then_inc(sem("r_sq"), 1)
                for n, (b, s) in enumerate(st["items"]):
                    act.wait_ge(sem("r_ss"), st["r_ss"] + n + 1)
                    link(fn(SQ[:, n, :], head_bank[n % 4][:, 0:S], ACT.Ln, bias=eps,
                            scale=1.0 / HD))
                    fn(SQ[:, n, :], SQ[:, n, :], ACT.Exp, scale=-0.5).then_inc(sem("r_rs"), 1)

            def mod_stage(st):
                pass

            nc.scalar.preload_act_table_set("natural_log_exp_and_others")
            act.wait_ge(sem("setup"), 1)
            act.wait_ge(sem("load_con"), 32)
            fn(CTMP, vec[:, VEC["cond"]:VEC["cond"] + 16], ACT.Exp, scale=-1.0).then_inc(sem("cond_exp"), 1)
            run = dict(norm=norm_stage, ffn=ffn_stage, proj=proj_stage, index=index_stage, attn=attn_stage,
                       gate=gate_stage, rope=rope_stage, mod=mod_stage)
            for st in stages:
                run[st["kind"]](st)

        @block.vector
        def _(dve):
            ve = nc.vector
            steps = [0]

            def link(ins):
                steps[0] += 1
                ins.then_inc(sem("dve_step"), 1)
                dve.wait_ge(sem("dve_step"), steps[0])

            def norm_stage(st):
                if st["ln"]:
                    wait_all(dve, st["ready"])
                    dve.wait_ge(sem("mean"), st["mean"] + 1)
                    for b in range(st["nb"]):
                        ve.scalar_tensor_tensor(out=st["centred"](b), in0=mean_bank[:, 0:S], scalar=-1.0 / (st["nb"] * P),
                                                in1=st["src"](b), op0=ALU.mult, op1=ALU.add).then_inc(sem("cen"), 1)
                if "next_ffn" in st:
                    ffn_ahead(st["next_ffn"])
                n = 0
                for g, blocks in enumerate(st["groups"]):
                    dve.wait_ge(sem("rstd"), st["rstd"] + g + 1)
                    for b in blocks:
                        src = st["centred"](b) if st["ln"] else st["src"](b)
                        dst = st["centred"](b) if st["ln"] else st["dst"](b)
                        ve.scalar_tensor_tensor(out=dst, in0=src, scalar=st["gain"](b), in1=RS[:, g, :],
                                                op0=ALU.mult, op1=ALU.mult).then_inc(
                            sem("scaled" if st["ln"] else "rms_out"), 1)
                        n += 1

            def fixed(value, per):
                return value

            def rest_chunk(st, at, u, third, wait, last):
                n = st["unit"] + u
                dve.wait_ge(sem("w_hi"), wait(st["hi"] + at + 1, 3))
                ve.tensor_tensor(WLO[at % SPLIT][:, :], unit_slot(n)[:, third * D:(third + 1) * D],
                                 WHI[at % SPLIT][:, :].bitcast(F32), ALU.subtract).then_inc(sem("w_split"), 1)

            def ffn_ahead(st):
                rest_chunk(st, 0, 0, 0, fixed, False)
                rest_chunk(st, 1, 0, 1, fixed, False)

            def ffn_stage(st):
                tok = st["tok"]
                for k in range(KT):
                    dve.wait_ge(sem("n_hi"), st["n_hi"] + k + 1)
                    ve.tensor_tensor(NLO[:, k, :], N[:, k, tok:tok + S], NHI[:, k, :].bitcast(F32),
                                     ALU.subtract).then_inc(sem("n_split"), 1)
                rest_chunk(st, at_up(1, 0), 1, 0, fixed, False)
                rest_chunk(st, at_up(1, 1), 1, 1, fixed, False)
                base = steps[0]

                def hidden(d, ahead, wait):
                    e, g, u = fE[d % 2][:, :], fG[d % 2][:, :], up[d % 2]
                    dve.wait_ge(sem("ffn_exp"), wait(st["exp"] + d + 1, 1))
                    ve.tensor_scalar(e, e, 1.0, None, ALU.add).then_inc(sem("dve_step"), 1)
                    dve.wait_ge(sem("dve_step"), wait(base + 3 * d + 1, 3))
                    ve.reciprocal(e, e).then_inc(sem("dve_step"), 1)
                    dve.wait_ge(sem("dve_step"), wait(base + 3 * d + 2, 3))
                    ve.tensor_tensor(e, e, u[:, 0:S], ALU.mult).then_inc(sem("dve_step"), 1)
                    dve.wait_ge(sem("dve_step"), wait(base + 3 * d + 3, 3))
                    ve.tensor_tensor(g, e, u[:, S:2 * S], ALU.mult).then_inc(sem("hidden"), 1)
                    rest_chunk(st, at_down(d), d, 2, wait, True)
                    dve.wait_ge(sem("hidden_hi"), wait(st["g_hi"] + d + 1, 1))
                    ve.tensor_tensor(GLO[d % 2][:, :], g, GHI[d % 2][:, :].bitcast(F32), ALU.subtract).then_inc(
                        sem("gated"), 1)
                    if ahead:
                        rest_chunk(st, at_up(d + 2, 0), d + 2, 0, wait, False)
                        rest_chunk(st, at_up(d + 2, 1), d + 2, 1, wait, False)

                for d in range(4):
                    hidden(d, True, fixed)
                with dve.Fori(0, (FB - 6) // RING) as i:
                    def turning(value, per):
                        return i * (RING * per) + value

                    for d in range(4, 4 + RING):
                        hidden(d, True, turning)
                for d in (FB - 2, FB - 1):
                    hidden(d, False, fixed)
                steps[0] += 3 * FB
                dve.wait_ge(sem("chunk_used"), st["chunk"] + CHUNKS)
                for b in range(KT):
                    x = X[:, b, tok:tok + S]
                    residual(x, acc[b // 2][:, (b % 2) * S:(b % 2 + 1) * S],
                             st["resid"](b) if st["resid"] else 0.5, st["resid"] is not None, st["scaled"] + b + 1)

            def residual(x, y, gain, post, value):
                if post:
                    ve.tensor_scalar(x, x, ALPHA, None, ALU.mult).then_inc(sem("alpha"), 1)
                    dve.wait_ge(sem("alpha"), value)
                ve.scalar_tensor_tensor(out=x, in0=y, scalar=gain, in1=x, op0=ALU.mult, op1=ALU.add).then_inc(
                    sem("resid"), 1)

            def proj_stage(st):
                for j, job in enumerate(st["jobs"]):
                    if job["eng"] != "dve":
                        continue
                    dve.wait_ge(sem(job["done"][0]), job["done"][1])
                    if job["evac"][0] == "resid":
                        gain = job["evac"][1]
                        residual(job["dst"], acc[j % 4][:, 0:S], 1.0 if gain is None else gain, gain is not None,
                                 job.get("scaled"))
                    else:
                        evacuate(dve, j, job, lambda d, s, f: ve.tensor_scalar(d, s, f, None, ALU.mult)).then_inc(
                            sem("evac_dve"), 1)

            def index_stage(st):
                wait_all(dve, st["ready"])
                for i in range(2):
                    dve.wait_ge(sem("wx_t"), st["wx_t"] + i + 1)
                    ve.tensor_copy(WX[:, i, :], acc[2 + i][:, 0:8]).then_inc(sem("wx"), 1)
                    dve.wait_ge(sem("wx"), st["wx"] + i + 1)
                for n in range(16):
                    i, h = n // 8, n % 8
                    w = (i + 1) * P
                    dve.wait_ge(sem("ix_r"), st["ix_r"] + n + 1)
                    if h > 0:
                        dve.wait_ge(sem("ix_a"), st["ix_a"] + n)
                    before = SCORE[:, i, 0:w] if h else cst("mask_causal")[:, (1 - i) * P:2 * P]
                    ve.scalar_tensor_tensor(out=SCORE[:, i, 0:w], in0=RELU[n % 2][:, 0:w], scalar=WX[:, i, h:h + 1],
                                            in1=before, op0=ALU.mult, op1=ALU.add).then_inc(sem("ix_a"), 1)
                dve.wait_ge(sem("ix_a"), st["ix_a"] + 16)
                for i in range(2):
                    w = (i + 1) * P
                    for r_ in range(TOPK // 8):
                        top8 = small[:, 160 + 8 * i:168 + 8 * i]
                        link(ve.max(top8, SCORE[:, i, 0:w]))
                        link(ve.match_replace(SCORE[:, i, 0:w], top8, SCORE[:, i, 0:w], TAKEN))
                for i in range(2):
                    w = (i + 1) * P
                    last = ve.tensor_scalar(SEL[:, i, 0:w], SCORE[:, i, 0:w], TAKEN / 2, NEG, ALU.is_gt, ALU.mult)
                last.then_inc(sem("top"), 1)

            def attn_stage(st):
                pairs, tiles = st["pairs"], st["tiles"]
                wait_all(dve, st["ready"])
                dve.wait_ge(sem(st["bias_ready"][0]), st["bias_ready"][1])

                def maxima(t):
                    n, h, i = tiles[t]
                    pr = pairs[n]
                    w = pr["keys"](i) * P
                    m = ATT[:, t % 3]
                    s = acc[t % 3]
                    dve.wait_ge(sem("att_s"), st["att_s"] + t + 1)
                    if t >= 3:
                        dve.wait_ge(sem("att_n"), st["att_n"] + t - 2)
                    if pr["bias"] is None:
                        ve.tensor_reduce(m[:, 0:1], s[:, 0:w], AX.X, ALU.max, negate=True).then_inc(sem("att_m"), 1)
                        return
                    wb = min(w, 256)
                    bias = pr["bias"](h, i)
                    src = s[:, 0:wb]
                    if pr["sel"]:
                        link(ve.tensor_tensor(aS[t % 3][:, 0:wb], src, bias, ALU.add))
                        src, bias = aS[t % 3][:, 0:wb], SEL[:, i, 0:wb]
                    if w == wb:
                        ve.tensor_tensor_reduce(aS[t % 3][:, 0:wb], src, bias, -1.0, -NEG, ALU.add, ALU.min,
                                                m[:, 0:1]).then_inc(sem("att_m"), 1)
                        return
                    ve.tensor_tensor_reduce(aS[t % 3][:, 0:wb], src, bias, -1.0, -NEG, ALU.add, ALU.min, m[:, 4:5])
                    link(ve.tensor_reduce(m[:, 5:6], s[:, wb:w], AX.X, ALU.max, negate=True))
                    ve.tensor_tensor(m[:, 0:1], m[:, 4:5], m[:, 5:6], ALU.min).then_inc(sem("att_m"), 1)

                def scale(t):
                    n, h, i = tiles[t]
                    pr = pairs[n]
                    w = pr["keys"](i) * P
                    m = ATT[:, t % 3]
                    dve.wait_ge(sem("att_e"), st["att_e"] + t + 1)
                    den = m[:, 2:3]
                    if pr["sink"] is not None or (pr["bias"] is not None and w > 256):
                        link(ve.tensor_tensor(m[:, 6:7], m[:, 2:3], m[:, 3:4], ALU.add))
                        den = m[:, 6:7]
                    link(ve.reciprocal(m[:, 7:8], den))
                    ve.tensor_scalar(aP[t % 3][:, 0:w], aP[t % 3][:, 0:w], m[:, 7:8], None, ALU.mult).then_inc(
                        sem("att_n"), 1)

                def outputs(n):
                    dve.wait_ge(sem("att_o"), st["att_o"] + 2 * n + 2)
                    ve.tensor_copy(pairs[n]["dst"], stat[n % 2][:, 0:S]).then_inc(sem("att_out"), 1)

                nt = len(tiles)
                for t in range(nt + 5):
                    if t < nt:
                        maxima(t)
                    if 0 <= t - 1 < nt:
                        scale(t - 1)
                    if t >= 8 and t % 4 == 0 and t // 4 - 2 < len(pairs):
                        outputs(t // 4 - 2)

            def gate_stage(st):
                T, layer = st["T"], st["layer"]
                wait_all(dve, st["ready"])
                dve.wait_ge(sem("load_misc"), 16 * 6)
                for c, z in enumerate(gate_chunks(st)):
                    t = gate_tmp(c)
                    dve.wait_ge(sem("g_sq"), st["g_sq"] + c + 1)
                    link(ve.tensor_scalar(t, t, 0.044715, 1.0, ALU.mult, ALU.add))
                    ve.tensor_tensor(t, t, z, ALU.mult).then_inc(sem("g_w"), 1)
                    dve.wait_ge(sem("g_e"), st["g_e"] + c + 1)
                    link(ve.tensor_scalar(t, t, 1.0, None, ALU.add))
                    link(ve.reciprocal(t, t))
                    ve.tensor_tensor(z, z, t, ALU.mult).then_inc(sem("g_z"), 1)
                    dve.wait_ge(sem("g_z"), st["g_z"] + c + 1)
                for tb in range(T // P):
                    z = ZV[:, tb, :]
                    link(ve.tensor_reduce(LNS[:, tb, 0:1], z, AX.X, ALU.add))
                    link(ve.tensor_scalar(LNS[:, tb, 1:2], LNS[:, tb, 0:1], -1.0 / 256, None, ALU.mult))
                    ve.tensor_scalar(z, z, LNS[:, tb, 1:2], None, ALU.add).then_inc(sem("zc"), 1)
                for tb in range(T // P):
                    dve.wait_ge(sem("zr"), st["zr"] + tb + 1)
                    ve.tensor_scalar(ZV[:, tb, :], ZV[:, tb, :], LNS[:, tb, 4:5], None, ALU.mult).then_inc(
                        sem("zn"), 1)
                for tb in range(T // P):
                    dve.wait_ge(sem("g_mm"), st["g_mm"] + tb + 1)
                    for j in range(2):
                        t = SC[:, 3072 + (2 * tb + j) * P:3072 + (2 * tb + j + 1) * P]
                        link(ve.scalar_tensor_tensor(out=t, in0=acc[tb][:, j * P:(j + 1) * P],
                                                     scalar=v("g_sgu", layer * 2 + j), in1=BS[:, layer, j, :],
                                                     op0=ALU.mult, op1=ALU.add))
                        ve.tensor_tensor(N[:, 3 + j, tb * P:(tb + 1) * P], t, PJ[:, 6 + j, tb * P:(tb + 1) * P],
                                         ALU.mult).then_inc(sem("g_out"), 1)

            def rope_stage(st):
                layer = st["layer"]

                def tiles3(ap):
                    return ap.rearrange("p (i t) -> p i t", t=P)

                for n, (b, s) in enumerate(st["items"]):
                    g = GQ[:, layer:layer + 1] if b < 11 else v("g_k", layer)
                    z = PJ[:, b, s * S:(s + 1) * S]
                    dve.wait_ge(sem("r_rs"), st["r_rs"] + n + 1)
                    if s == 0:
                        ve.scalar_tensor_tensor(out=SC[:, n * S:(n + 1) * S], in0=z, scalar=g, in1=SQ[:, n, :],
                                                op0=ALU.mult, op1=ALU.mult).then_inc(sem("r_y"), 1)
                    elif b == 11:
                        ve.scalar_tensor_tensor(out=z, in0=z, scalar=g, in1=SQ[:, n, :], op0=ALU.mult,
                                                op1=ALU.mult).then_inc(sem("r_out"), 1)
                    else:
                        ve.scalar_tensor_tensor(out=SQ[:, n, :], in0=z, scalar=g, in1=SQ[:, n, :], op0=ALU.mult,
                                                op1=ALU.mult).then_inc(sem("r_y"), 1)
                for n, (b, s) in enumerate(st["items"][:-1]):
                    z = PJ[:, b, s * S:(s + 1) * S]
                    dve.wait_ge(sem("r_y"), st["r_y"] + n + 1)
                    if s == 0:
                        dve.wait_ge(sem("r_rot"), st["r_rot"] + n + 1)
                        y, r_ = SC[:, n * S:(n + 1) * S], SC[:, (4 + n) * S:(5 + n) * S]
                        ve.tensor_tensor(SQ[:, n, :], y, cst("cos"), ALU.mult)
                        link(ve.tensor_tensor(r_, acc[n][:, 0:S], cst("sin"), ALU.mult))
                        out = z if b == 11 else tiles3(z)[:, :, ::-1]
                        p, q = (SQ[:, n, :], r_) if b == 11 else (tiles3(SQ[:, n, :]), tiles3(r_))
                        ve.tensor_tensor(out, p, q, ALU.add).then_inc(sem("r_out"), 1)
                    else:
                        ve.tensor_copy(tiles3(z)[:, :, ::-1], tiles3(SQ[:, n, :])).then_inc(sem("r_out"), 1)

            def mod_stage(st):
                dve.wait_ge(sem("mod_t"), 1)
                for layer in range(2):
                    m = MOD[:, layer, :, :]
                    b = vec[:, VEC["b_mod"] + layer * 48:VEC["b_mod"] + (layer + 1) * 48]
                    rows = acc[0][:, layer * 96:(layer + 1) * 96].rearrange("p (s n) -> p s n", s=2)
                    link(ve.tensor_tensor(m, rows, b.unsqueeze(1).to_broadcast([P, 2, 48]), ALU.add))
                    link(ve.tensor_scalar(m[:, :, 8:16], m[:, :, 8:16], 1.0, None, ALU.add))
                    ve.tensor_scalar(m[:, :, 32:40], m[:, :, 32:40], 1.0, None, ALU.add).then_inc(sem("mod"), 1)

            ve.memset(eps, EPS).then_inc(sem("setup"), 1)
            dve.wait_ge(sem("load_con"), 32)
            ve.tensor_scalar(GQ, vec[:, VEC["g_q"]:VEC["g_q"] + 2], QSCALE, None, ALU.mult)
            dve.wait_ge(sem("cond_exp"), 1)
            link(ve.tensor_scalar(CTMP, CTMP, 1.0, None, ALU.add))
            link(ve.reciprocal(CTMP, CTMP))
            ve.tensor_tensor(small[:, 64:80], CTMP, vec[:, VEC["cond"]:VEC["cond"] + 16], ALU.mult).then_inc(
                sem("cond"), 1)
            dve.wait_ge(sem("rows"), 1)
            ve.tensor_copy(ROW, stat[1][0:16, 0:384]).then_inc(sem("rows_sb"), 1)
            dve.wait_ge(sem("rows_dram"), 16)
            run = dict(norm=norm_stage, ffn=ffn_stage, proj=proj_stage, index=index_stage, attn=attn_stage,
                       gate=gate_stage, rope=rope_stage, mod=mod_stage)
            for st in stages:
                run[st["kind"]](st)


def column_units(w):
    n = w.shape[1]
    u = tiles_cols(n)
    w = np.pad(w, ((0, 0), (0, u * UC - n)))
    return w.reshape(KT, P, u, UC).transpose(2, 1, 0, 3).reshape(u, P, UNIT)


def hidden_units(w1, w3, w2):
    def cols(w):
        return w.reshape(KT, P, FB, P).transpose(2, 1, 0, 3).reshape(FB, P, D)

    return np.concatenate([cols(w1), cols(w3), w2.reshape(FB, P, D)], axis=2)


def columns(v):
    return np.asarray(v).reshape(-1, P).T


def kernel(x, norm_g, final_g, rel_bias_table, ffn_w1, ffn_w3, ffn_w2, hyb_w_in, hyb_cq_g, hyb_wq_b, hyb_wq_idx,
           hyb_w_out, swa_w_in, swa_sinks, swa_w_out, c_2, ctx_2, c_ctx_2, w_mod_2, b_mod_2, w_in_2, rpb_2, w_s_2,
           b_s_2, g_sgu_2, g_q_2, g_k_2, g_out_2, w_o_2, ln1_g_2, ln1_b_2, w_ffn_in_2, w_ffn_out_2, ln2_g_2,
           ln2_b_2):
    import concourse.bacc as bacc
    from concourse.bass_utils import run_bass_kernel_spmd

    swa_cols = np.concatenate([np.r_[j * HD:(j + 1) * HD, (8 + j) * HD:(9 + j) * HD] for j in range(8)])
    gqa_cols = np.concatenate([np.r_[j * HD:(j + 1) * HD, (3 + j) * HD:(4 + j) * HD] for j in range(3)])
    swa_in = np.concatenate([swa_w_in[0][:, swa_cols], swa_w_in[0][:, 1024:]], axis=1)
    in2_cols = np.r_[0:1664, 1664 + gqa_cols, 2048:2304]
    out2_rows = np.r_[0:640, 640 + gqa_cols]

    def feature_major(t):
        return t[0].T.reshape(KT, P, S).transpose(1, 0, 2)

    cq_unit = np.zeros((1, P, UNIT), np.float32)
    cq_unit[0, :, 0:1024] = hyb_wq_b[0].reshape(2, P, 512).transpose(1, 0, 2).reshape(P, 1024)
    cq_unit[0, :, 1024:1536] = hyb_wq_idx[0].reshape(2, P, 256).transpose(1, 0, 2).reshape(P, 512)
    arrays = {
        "x": feature_major(x), "ctx": feature_major(ctx_2),
        "con": constants(), "onehot": bucket_rows(), "table": rel_bias_table,
        "vec": np.concatenate([columns(norm_g), columns(final_g), columns(hyb_cq_g), columns(b_mod_2),
                               columns(g_sgu_2), columns(np.tile(g_q_2, (1, 2))), columns(np.tile(g_k_2, (1, 2))),
                               columns(g_out_2[:, out2_rows]), columns(ln1_g_2), columns(ln1_b_2),
                               columns(ln2_g_2), columns(ln2_b_2), columns(c_2), columns(c_ctx_2)], axis=1),
        "sinks": swa_sinks, "b_s": b_s_2, "w_s": w_s_2.transpose(3, 0, 1, 2),
        "rpb": np.pad(rpb_2[:, :, 4:11, :], ((0, 0), (0, 0), (0, 0), (48, 49))),
        "ffn_units": np.concatenate([hidden_units(ffn_w1[l, f], ffn_w3[l, f], ffn_w2[l, f])
                                     for l in range(2) for f in range(2)]),
        "even_units": np.concatenate([column_units(hyb_w_in[0]), cq_unit, column_units(hyb_w_out[0])]),
        "swa_units": np.concatenate([column_units(swa_in), column_units(swa_w_out[0][swa_cols])]),
        "mod_units": np.concatenate([column_units(w_mod_2[l]) for l in range(2)]),
        "mix2_units": np.concatenate([column_units(w) for l in range(2)
                                      for w in (w_in_2[l][:, in2_cols], w_o_2[l][out2_rows])]),
        "ffn2_units": np.concatenate([hidden_units(w_ffn_in_2[l][:, :FF], w_ffn_in_2[l][:, FF:], w_ffn_out_2[l])
                                      for l in range(2)]),
    }
    nc = bacc.Bacc("TRN2", target_bir_lowering=False, num_devices=1)
    inputs, aps = {}, {}
    for name, value in arrays.items():
        value = np.ascontiguousarray(value)
        inputs[f"in_{name}"] = value
        aps[name] = nc.dram_tensor(f"in_{name}", value.shape, mybir.dt.from_np(value.dtype),
                                   kind="ExternalInput").ap()
    aps["out"] = nc.dram_tensor("out_x", (P, KT, S), F32, kind="ExternalOutput").ap()
    build_program(nc, aps)
    r = run_bass_kernel_spmd(nc, [inputs], core_ids=[0])
    out = r.results[0]["out_x"]
    return out.transpose(1, 0, 2).reshape(1, D, S).transpose(0, 2, 1)
```

```python
import math
from contextlib import ExitStack

import numpy as np

import concourse.bass as bass
from concourse import mybir

F32 = mybir.dt.float32
F32R = mybir.dt.float32r
ALU = mybir.AluOpType
ACT = mybir.ActivationFunctionType
AX = mybir.AxisListType

P = 128
D = 1024
KT = D // P
S = 256
FF = 2816
FB = FF // P
HD = 64
EPS = 1e-6
ALPHA = 4.0 ** 0.25
QSCALE = HD ** -0.5
NEG = -1.0e30
TAKEN = -3.0e38
TOPK = 64
UC = 384
UNIT = KT * UC
RING = 4
SPLIT = 4
CHUNKS = 3 * FB
IDX_SCALE = (32 ** -0.5) * (8 ** -0.5)
GELU_C = 2.0 * math.sqrt(2.0 / math.pi)

VEC_PARTS = [("norm_g", 48), ("final_g", 8), ("cq_g", 2), ("b_mod", 96), ("g_sgu", 4), ("g_q", 2), ("g_k", 2),
             ("g_out", 16), ("ln1_g", 16), ("ln1_b", 16), ("ln2_g", 16), ("ln2_b", 16), ("cond", 16)]
VEC = {}
_at = 0
for _name, _n in VEC_PARTS:
    VEC[_name] = _at
    _at += _n
NVEC = _at
CONST_PARTS = [("ident", 128), ("ones", 128), ("halves", 128), ("swap", 128), ("mask_mix", 256),
               ("mask_causal", 256), ("mask_swa", 256), ("mask_na", 64), ("cos", 256), ("sin", 256),
               ("pick", 2)]
CONST = {}
_at = 0
for _name, _n in CONST_PARTS:
    CONST[_name] = _at
    _at += _n
NCONST = _at


def constants():
    c = np.zeros((P, NCONST), np.float32)

    def put(name, a):
        c[:, CONST[name]:CONST[name] + a.shape[1]] = a

    put("ident", np.eye(P, dtype=np.float32))
    put("ones", np.ones((P, P), np.float32))
    half = np.arange(P) // HD
    put("halves", (half[:, None] == half[None, :]).astype(np.float32))
    swap = np.zeros((P, P), np.float32)
    for m in range(P):
        if m % 32 < 16:
            swap[m + 16, m] = -1.0
        else:
            swap[m - 16, m] = 1.0
    put("swap", swap)
    dist = 255 - np.arange(P)[:, None] - np.arange(S)[None, :]
    count = (dist <= 128).astype(int) + (dist % 4 == 0) + (dist % 16 == 0)
    ok = (dist >= 0) & (count > 0)
    put("mask_mix", np.where(ok, np.log(np.maximum(count, 1).astype(np.float64)), NEG).astype(np.float32))
    put("mask_causal", np.where(dist >= 0, 0.0, NEG).astype(np.float32))
    put("mask_swa", np.where((dist >= 0) & (dist <= 127), 0.0, NEG).astype(np.float32))
    col = 63 - np.arange(P) % 64
    start = np.clip(col - 8, 0, 48)
    key = np.arange(64)[None, :]
    put("mask_na", np.where((key >= start[:, None]) & (key < start[:, None] + 16), 0.0, NEG).astype(np.float32))
    put("pick", (np.arange(P)[:, None] % 32 == np.arange(2)[None, :]).astype(np.float32))
    t = np.arange(S)
    inv = (1.0 / (np.float32(10000.0) ** (np.arange(16, dtype=np.float32) / np.float32(16)))).astype(np.float32)
    pos = np.stack([t // 64, t % 64]).astype(np.float32)
    feature = np.arange(P) % HD
    ang = pos[feature // 32] * inv[feature % 16][:, None]
    put("cos", np.cos(ang.astype(np.float32)).astype(np.float32))
    put("sin", np.sin(ang.astype(np.float32)).astype(np.float32))
    return c


def bucket_rows():
    d = np.maximum(255 - np.arange(384), 0)
    f = np.maximum(d, 1).astype(np.float32)
    large = 16 + (np.log(f / np.float32(16)) / np.float32(math.log(2048 / 16)) * np.float32(16)).astype(np.int32)
    b = np.where(d < 16, d, np.minimum(large, 31))
    return (np.arange(32)[:, None] == b[None, :]).astype(np.float32)


class Count:

    def __init__(self):
        self.n = {}

    def take(self, name, n):
        base = self.n.get(name, 0)
        self.n[name] = base + n
        return base


def tiles_cols(n):
    return -(-n // UC)


def build_program(nc, a):
    with ExitStack() as ctx:
        def sb(name, shape):
            return ctx.enter_context(nc.sbuf_tensor(name, shape, F32))

        def sb_r(name, shape):
            return ctx.enter_context(nc.sbuf_tensor(name, shape, F32R))

        def bank(name):
            return ctx.enter_context(nc.psum_tensor(name, [P, 512], F32))

        sems = {}

        def sem(name):
            if name not in sems:
                sems[name] = ctx.enter_context(nc.semaphore(name))
            return sems[name]

        fixed_buffers = [("resid", [P, KT, 2 * S])] + [("normed", [P, KT, 2 * S])] + [
            (f"unit{i}", [P, UNIT]) for i in range(RING)] + [
            ("rstd", [P, 3, S]), ("bias", [P, 16, 256]), ("spare_hi", [P, D]), ("squares", [P, KT * S]),
            ("vec", [P, NVEC]), ("con", [P, NCONST]), ("gate_w", [P, 2, 4, P]), ("gate_b", [P, 2, 2, P]),
            ("mod", [P, 2, 48, 2]), ("mod_rows", [P, UC]), ("cond_silu", [P, KT, 32]), ("small", [P, 256])]
        mixer_buffers = [("scratch", [P, 6144]), ("proj", [P, 12, 2 * S]), ("values", [P, 4, 512]),
                         ("gate_v", [P, 4, 256])]
        with ExitStack() as second_names:
            R = {}
            for name, shape in fixed_buffers + mixer_buffers:
                if name == "bias":
                    second_names.enter_context(nc.sbuf_tensor("bias_head", [P, 12 * 256], F32))
                    name, shape = "window", [P, 4, D]
                elif name in ("spare_hi", "squares"):
                    continue
                R[name] = second_names.enter_context(nc.sbuf_tensor(name + "_short", shape, F32R))
        B = {name: sb(name, shape) for name, shape in fixed_buffers}
        X = B["resid"]
        N = B["normed"]
        ring = [B[f"unit{i}"] for i in range(RING)]
        ring_short = [R[f"unit{i}"] for i in range(RING)]
        SQ = B["squares"][:, :].rearrange("p (k s) -> p k s", k=KT)
        RS = B["rstd"]
        BT = B["bias"]
        vec, con, small = B["vec"], B["con"], B["small"]
        WS, BS = B["gate_w"], B["gate_b"]
        MOD = B["mod"]
        ROWS = B["mod_rows"]
        CS = B["cond_silu"]
        with ExitStack() as mixers:
            B.update((name, mixers.enter_context(nc.sbuf_tensor(name, shape, F32))) for name, shape in mixer_buffers)
            SC = B["scratch"]
            PJ = B["proj"]
            VT = B["values"]
            ZV = B["gate_v"]
        WHI = [sb_r(f"w_hi{i}", [P, D]) for i in range(SPLIT)]
        WLO = [sb_r(f"w_lo{i}", [P, D]) for i in range(SPLIT)]
        NHI = sb_r("normed_hi", [P, KT, S])
        NLO = sb_r("normed_lo", [P, KT, S])
        GHI = [sb_r(f"hidden_hi{i}", [P, S]) for i in range(2)]
        GLO = [sb_r(f"hidden_lo{i}", [P, S]) for i in range(2)]
        fE = [sb(f"silu{i}", [P, S]) for i in range(2)]
        fA = [sb(f"scaled{i}", [P, S]) for i in range(2)]
        fG = [sb(f"hidden{i}", [P, S]) for i in range(2)]
        flat = BT[:, :, :].rearrange("p h s -> p (h s)")
        OH = flat[0:32, 0:384]
        TB = flat[0:32, 384:400]
        ROW = flat[0:16, 512:896]

        acc = [bank(f"acc{i}") for i in range(4)]
        up = [bank(f"up{i}") for i in range(2)]
        stat = [bank(f"stat{i}") for i in range(2)]

        def chunk_of(ap):
            return ap.rearrange("p (k c) -> p k c", k=KT)

        def chunks_at(ap):
            return ap.rearrange("p b (k c) -> p b k c", k=KT)

        def place(weights, c):
            return weights[c % 4] if isinstance(weights, list) else weights[:, c % 4]

        sc_short = R["scratch"]
        w_first = chunks_at(sc_short[:, 0:4 * D].rearrange("p (b f) -> p b f", b=4))
        n_in_x = sc_short[:, 4 * D:6 * D].rearrange("p (k t) -> p k t", k=KT)
        w_second = chunks_at(R["window"][:, :, :])
        n_in = sc_short[:, 2 * D:6 * D].rearrange("p (k t) -> p k t", k=KT)
        w_out = [chunk_of(ap) for ap in (sc_short[:, 2 * D:3 * D], sc_short[:, 3 * D:4 * D],
                                         R["proj"][:, 0:2, :].rearrange("p b t -> p (b t)"),
                                         R["proj"][:, 2:4, :].rearrange("p b t -> p (b t)"))]
        n_out = R["proj"][:, 4:12, :]
        w_out_x = [R["window"][:, i, :].rearrange("p (k c) -> p k c", k=KT) for i in (1, 2, 3)] + w_out[1:2]
        n_out_x = R["values"][:, :, :].rearrange("p i (u t) -> p (i u) t", u=2)
        N_LO = R["normed"][:, :, :]

        mean_bank = up[0]
        sum_bank = [stat[0], stat[1], up[1]]
        head_bank = [up[0], up[1], stat[0], stat[1]]

        def cst(name, n=None):
            return con[:, CONST[name]:CONST[name] + (n or dict(CONST_PARTS)[name])]

        def v(name, i):
            return vec[:, VEC[name] + i:VEC[name] + i + 1]

        ident, ones = cst("ident"), cst("ones")
        eps = small[:, 0:1]
        sinks = small[:, 16:32]
        GQ = small[:, 32:34]
        WX = small[:, 40:56].rearrange("p (i h) -> p i h", i=2)
        CTMP = small[:, 80:96]
        ATT = small[:, 96:96 + 24].rearrange("p (b n) -> p b n", b=3)
        LNS = small[:, 128:160].rearrange("p (t n) -> p t n", t=4)

        aS = [SC[:, i * 512:(i + 1) * 512] for i in range(3)]
        aP = [SC[:, 1536 + i * 512:2048 + i * 512] for i in range(3)]
        aT = [SC[:, 3072 + i * 1024:4096 + i * 1024].rearrange("p (s t) -> p s t", s=4) for i in range(2)]
        SEL = SC[:, 5120:5632].rearrange("p (i s) -> p i s", i=2)
        SCORE = SC[:, 5632:6144].rearrange("p (i s) -> p i s", i=2)
        RELU = [SC[:, i * 256:(i + 1) * 256] for i in range(2)]
        QI = SQ
        PJE = PJ[:, :, :].rearrange("p b (u t) -> p (b u) t", u=2)
        VTE = VT[:, :, :].rearrange("p (i u) n -> p i (u n)", u=2)
        NAB = BT[:, 0:12, :].rearrange("p (i h) s -> p i h s", i=2)

        scratch_rows = nc.dram_tensor("bias_rows", (16, 384), F32).ap()

        def rev(ap):
            return ap[:, ::-1]

        def at_up(u, half):
            return half if u == 0 else 3 * u - 1 + half

        def at_down(d):
            return min(4 + 3 * d, CHUNKS - 1)

        cnt = Count()
        stages = []
        loads = []
        free = []

        def add_units(name, start, n):
            loads.append((a[name], start, n))
            return cnt.take("unit", n)

        def by_tensor(n):
            base = cnt.take("unit_used", n)
            free.extend(("unit_used", base + j + 1) for j in range(n))
            return base

        def norm(kind, groups, src, dst, gain, shift, ready, centred=None, each=None, low=None):
            nb = sum(len(g) for g in groups)
            st = dict(kind="norm", ln=kind == "ln", groups=groups, src=src, dst=dst, gain=gain, shift=shift,
                      ready=ready, each=each, centred=centred, nb=nb, sq=cnt.take("sq", nb), ss=cnt.take("ss", len(groups)),
                      rstd=cnt.take("rstd", len(groups)))
            if st["ln"]:
                st["mean"] = cnt.take("mean", 1)
                st["cen"] = cnt.take("cen", nb)
                st["scaled"] = cnt.take("scaled", nb)
            st["low"] = low
            if low:
                st["n_low"] = cnt.take("n_low", nb)
            st["out_sem"] = "ln_out" if st["ln"] else "rms_out"
            st["out"] = cnt.take(st["out_sem"], nb)
            st["rstd_free"] = cnt.n["rms_out"] - (0 if st["ln"] else nb) if "rms_out" in cnt.n else 0
            stages.append(st)
            if low:
                return ("n_low", st["n_low"] + nb)
            return (st["out_sem"], st["out"] + nb)

        def blocks_of(r):
            return [(r[0], r[1] - KT + b + 1) for b in range(KT)]

        def ffn(units, tok, ready, resid, rms=None, each=None, ahead=None):
            st = dict(kind="ffn", tok=tok, ready=ready, resid=resid, rms=rms, each=each, ahead=ahead, unit=add_units(*units, FB),
                      chunk=cnt.take("chunk_used", CHUNKS), hi=cnt.take("w_hi", CHUNKS),
                      split=cnt.take("w_split", CHUNKS), n_hi=cnt.take("n_hi", KT if rms else 0), n_split=cnt.take("n_split", KT if rms else 0),
                      act=cnt.take("hidden", FB), g_hi=cnt.take("hidden_hi", FB), exp=cnt.take("ffn_exp", FB), gated=cnt.take("gated", FB),
                      scaled=cnt.take("alpha", KT if resid else 0), res=cnt.take("resid", 8))
            free.extend(("w_split", st["split"] + at_down(d) + 1) for d in range(FB))
            if rms:
                st.update(sq=cnt.take("sq", KT), ss=cnt.take("ss", 1), rstd=cnt.take("rstd", 1),
                          scaled_a=cnt.take("scaled_a", FB))
            if ahead:
                ahead["early"] = st
            elif not rms:
                stages[-1]["next_ffn"] = st
            stages.append(st)
            return ("resid", st["res"] + 8)

        def proj(jobs, units, ready, weights=None, n_hi=None, split=(), low=None):
            base = add_units(*units)
            used = by_tensor(units[2])
            last = {}
            for j, job in enumerate(jobs):
                last[job["unit"]] = j
            for j, job in enumerate(jobs):
                job["slot"] = base + job["unit"]
                job["last"] = last[job["unit"]] == j
                job["done"] = ("unit_used", used + job["unit"] + 1) if job["last"] else \
                    ("proj", cnt.take("proj", 1) + 1)
                e = job["evac"]
                name = "resid" if e[0] == "resid" else {"act": "evac_act", "dve": "evac_dve"}[job["eng"]]
                job["out"] = (name, cnt.take(name, 1) + 1)
                if e[0] == "resid" and e[1] is not None:
                    job["scaled"] = cnt.take("alpha", 1) + 1
            st = dict(kind="proj", jobs=jobs, ready=ready, weights=weights, n_hi=n_hi)
            if weights is not None:
                st["chunks"], turn_of, reader, next_turn = [], {}, {}, 0
                for j, job in enumerate(jobs):
                    first = job["unit"] * 3 + job["off"] // P
                    n = job["n"] // P if job["tm"] else 1
                    if first not in turn_of:
                        if next_turn % 4 + n > 4:
                            next_turn += 1
                        for c in range(first, first + n):
                            turn_of[c] = next_turn
                            st["chunks"].append((job["slot"], c % 3, next_turn))
                            next_turn += 1
                    for c in range(first, first + n):
                        reader[turn_of[c]] = j
                    job["turn"] = turn_of[first]
                    job["split"] = [t for _, _, t in st["chunks"]].index(turn_of[first]) + n
                st["after"] = []
                for i, (slot, third, turn) in enumerate(st["chunks"]):
                    before = [t for t in reader if t < turn and t % 4 == turn % 4]
                    st["after"].append(reader[max(before)] if before else -1)
                for i in range(1, len(st["after"])):
                    st["after"][i] = max(st["after"][i], st["after"][i - 1])
                st["first"] = sum(j < 0 for j in st["after"])
                st["w_cols_hi"] = cnt.take("w_cols_hi", len(st["chunks"]))
                st["w_cols"] = cnt.take("w_cols", len(st["chunks"]))
                st["blocks"], st["n_low"] = [], {}
                for tok, each in split:
                    for k in range(KT):
                        st["blocks"].append((tok, k, each[k] if each else None))
                st["n_high_base"] = cnt.take("n_high", len(st["blocks"]))
                st["n_low_base"] = cnt.take("n_low", len(st["blocks"]))
                for n, (tok, k, _) in enumerate(st["blocks"]):
                    st["n_low"][tok, k] = st["n_low_base"] + n + 1
                for tok, r_ in (low or {}).items():
                    for k in range(KT):
                        st["n_low"][tok, k] = r_[1] - KT + k + 1
                st["begun"] = stages[-1]["kind"] in ("norm", "attn")
                if st["begun"]:
                    stages[-1]["next_proj"] = st
            stages.append(st)
            return [(n, max(j["out"][1] for j in jobs if j["out"][0] == n)) for n in {j["out"][0] for j in jobs}]

        def other(kind, sizes, **kw):
            st = dict(kind=kind, **kw)
            for name, n in sizes.items():
                st[name] = cnt.take(name, n)
            stages.append(st)
            return st

        def alternate(jobs):
            for j, job in enumerate(jobs):
                job.setdefault("eng", "act" if j % 2 == 0 else "dve")
            return jobs

        def xs(tok):
            return lambda b: X[:, b, tok:tok + S]

        def ns(tok):
            return lambda b: N[:, b, tok:tok + S]

        def feature_job(unit, off, m, dst, q, n=S, tok=0, src=None, kts=KT, kstep=UC):
            return dict(unit=unit, off=off, m=m, kts=kts, kstep=kstep, tm=False, n=n, dst=dst,
                        src=src, span=(tok, n), evac=("q" if q else "copy",))

        def token_job(unit, off, n, tile, dst):
            return dict(unit=unit, off=off, m=P, kts=KT, kstep=UC, tm=True, n=n, dst=dst,
                        span=(tile * P, P), evac=("copy",))

        def out_jobs(toks, gain):
            jobs = []
            for b in range(KT):
                for t in toks:
                    jobs.append(dict(unit=b // 3, off=(b % 3) * P, m=P, kts=KT, kstep=UC, tm=False, n=S,
                                     dst=X[:, b, t:t + S], span=(t, S),
                                     evac=("resid", gain(b, t)), eng="dve", tok=t))
            return jobs

        def attention(pairs, mods=None, **kw):
            if mods is not None:
                first, count, lead = mods
                kw.update(mods=mods, mod_unit=add_units("mod_units", first, count),
                          mod_used=by_tensor(count), mod_row=cnt.take("mod_row", count),
                          mod_sum=cnt.take("mod_sum", 1), mod=cnt.take("mod", 1), period=4 * len(pairs) // (count - lead))
            else:
                kw.update(mods=None)
            tiles = []
            for n, pr in enumerate(pairs):
                for h in range(2):
                    for i in range(2):
                        tiles.append((n, h, i))
            return other("attn", dict(att_s=len(tiles), att_m=len(tiles), att_e=len(tiles), att_n=len(tiles),
                                      att_t=len(tiles), att_c=len(tiles), att_o=2 * len(pairs),
                                      att_out=len(pairs), att_add=len(tiles)),
                         pairs=pairs, tiles=tiles, **kw)

        x_ready = [("load_x", 16), ("load_vec", 16)]
        for layer in range(2):
            ng = lambda j, layer=layer: (lambda b: v("norm_g", (layer * 3 + j) * 8 + b))
            if layer == 0:
                r = ffn(("ffn_units", 0), 0, x_ready, None, rms=ng(0))
            else:
                r = ffn(("ffn_units", 2 * FB), 0, [], None, rms=ng(0), each=blocks_of(r))
            r = norm("rms", [range(KT)], xs(0), ns(0), ng(1), None, [], each=blocks_of(r))
            if layer == 0:
                jobs = []
                for b in range(8):
                    jobs.append(feature_job(b // 3, (b % 3) * P, P, PJE[:, b, :], b < 4))
                for b in range(2):
                    jobs.append(feature_job(2 + b, 2 * P if b == 0 else 0, P, PJE[:, 16 + b, :], False))
                for half in range(2):
                    for i in range(2):
                        jobs.append(token_job(3 + half, P if half == 0 else 0, 256, i,
                                              VTE[:, i, half * 256:(half + 1) * 256]))
                for b in range(4):
                    jobs.append(feature_job(4 + (b + 2) // 3, ((b + 2) % 3) * P, P, PJE[:, 8 + b, :], False))
                for i in range(2):
                    jobs.append(token_job(6, 0, 256, i, VTE[:, i, 512:768]))
                jobs.append(feature_job(6, 256, 32, PJE[0:32, 20, :], False))
                wx = feature_job(6, 288, 8, PJE[0:8, 21, :], False)
                wx["evac"] = ("reverse", IDX_SCALE)
                jobs.append(wx)
                for i in range(2):
                    jobs.append(token_job(7, 0, 256, i, VTE[:, i, 768:1024]))
                w = proj(alternate(jobs), ("even_units", 0, 8), [], w_first, n_in_x, [(0, blocks_of(r))])
                r = norm("rms", [range(2)], lambda b: PJE[:, 16 + b, :], lambda b: PJE[:, 18 + b, :],
                         lambda b: v("cq_g", b), None, w)
                cq = lambda k: PJE[:, 18 + k, :]
                jobs = [feature_job(0, b * P, P, PJE[:, 12 + b, :], True, src=cq, kts=2, kstep=512)
                        for b in range(4)]
                for h in range(8):
                    j = feature_job(0, 1024 + h * 32, 32, QI[0:32, h, :], False, src=cq, kts=2, kstep=256)
                    j["evac"] = ("reverse", 1.0)
                    jobs.append(j)
                w = proj(alternate(jobs), ("even_units", 8, 1), [r])
                st = other("index", dict(wx_t=2, wx=2, ix_s=16, ix_r=16, ix_a=16, top=1), ready=w)
                pairs = []
                for j in range(8):
                    mix = j < 4
                    pairs.append(dict(q=(lambda i, j=j: PJE[:, (j if j < 4 else 8 + j), i * P:(i + 1) * P]),
                                      k=(lambda h, i, j=j: PJE[:, 4 + j, 0:(i + 1) * P]),
                                      v=(lambda h, s, j=j: VTE[:, s, (2 * j + h) * HD:(2 * j + h + 1) * HD]),
                                      bias=(lambda h, i, j=j: BT[:, 2 * j + h, (1 - i) * P:2 * P]),
                                      keys=lambda i: i + 1, sel=not mix, sink=None, dst=N[:, j, 0:S]))
                at = attention(pairs, mods=(0, 12, 4), bank_free=("wx", st["wx"] + 2), ready=[("top", st["top"] + 1)] + w, bias_ready=("bias0", 2))
                r = proj(out_jobs([0], lambda b, t: None), ("even_units", 9, 3),
                         [("att_out", at["att_out"] + 8), ("mod", at["mod"] + 1)], w_out_x, n_out_x, [(0, None)])[0]
                early = stages[-1]
            else:
                jobs = []
                for b in range(8):
                    jobs.append(feature_job(b // 3, (b % 3) * P, P, PJE[:, b, :], True))
                jobs.append(feature_job(2, 256, P, PJE[:, 8, :], False))
                for i in range(2):
                    jobs.append(token_job(3, 0, 128, i, VTE[:, i, 0:128]))
                w = proj(alternate(jobs), ("swa_units", 0, 4), [], w_first, n_in_x, [(0, blocks_of(r))])
                pairs = []
                for j in range(8):
                    pairs.append(dict(q=(lambda i, j=j: PJE[:, j, i * P:(i + 1) * P]),
                                      k=(lambda h, i: PJE[:, 8, 0:(i + 1) * P]),
                                      v=(lambda h, s: VTE[:, s, h * HD:(h + 1) * HD]),
                                      bias=(lambda h, i, j=j: BT[:, 8 * h + j, (1 - i) * P:2 * P]),
                                      keys=lambda i: i + 1, sel=False,
                                      sink=(lambda h, j=j: sinks[:, 8 * h + j:8 * h + j + 1]), dst=N[:, j, 0:S]))
                at = attention(pairs, mods=(12, 8, 0), ready=w, bias_ready=("bias1", 1))
                r = proj(out_jobs([0], lambda b, t: None), ("swa_units", 4, 3),
                         [("att_out", at["att_out"] + 8), ("mod", at["mod"] + 1)], w_out_x, n_out_x, [(0, None)])[0]
                early = stages[-1]
            first_att = at if layer == 0 else first_att
            second_att = at
            r = ffn(("ffn_units", (2 * layer + 1) * FB), 0, [], None, rms=ng(2), each=blocks_of(r), ahead=early)
        r = norm("rms", [range(KT)], xs(0), xs(0), lambda b: v("final_g", b), None, [],
                 each=blocks_of(r))

        x_now, c_now = r, ("load_ctx", 16)

        def modv(layer, which, stream):
            return lambda b: MOD[:, layer, which * 8 + b, stream:stream + 1]

        na_att = []
        for layer in range(2):
            both = layer == 0
            toks = [0, S] if both else [0]
            T = len(toks) * S
            def n_hi(tok):
                return lambda b: n_in[:, b, tok:tok + S]

            def n_lo(tok):
                return lambda b: N_LO[:, b, tok:tok + S]

            rx = norm("ln", [range(KT)], xs(0), n_hi(0), modv(layer, 1, 0), modv(layer, 0, 0),
                      [x_now, ("mod", 2 + layer)], ns(0), each=blocks_of(x_now), low=n_lo(0))
            rc = norm("ln", [range(KT)], xs(S), n_hi(S), modv(layer, 1, 1), modv(layer, 0, 1), [c_now], ns(S),
                      each=[c_now] * KT, low=n_lo(S))
            jobs = []

            def feats(unit, off, blk, q, streams):
                n = len(streams) * S
                tok = streams[0] * S
                jobs.append(feature_job(unit, off, P, PJ[:, blk, tok:tok + n], q, n=n, tok=tok))

            mine, all_ = (([0, 1], [0, 1]) if both else ([0], [0, 1]))
            feats(0, 0, 6, False, mine)
            for i in range(T // P):
                jobs.append(token_job(0, P, 256, i, ZV[:, i, :]))
            feats(1, 0, 7, False, mine)
            gate_in = len(jobs)
            for b in range(2):
                feats(1, (1 + b) * P, 8 + b, False, mine)
            feats(2, 0, 10, False, mine)
            feats(2, P, 11, False, all_)
            for b in range(3):
                feats(2 + (b + 2) // 3, (b + 2) % 3 * P, b, True, mine)
            feats(3, 2 * P, 3, False, all_)
            feats(4, 0, 4, False, all_)
            for i in range(4):
                jobs.append(token_job(4, P, 256, i, VT[:, i, 0:256]))
            for i in range(4):
                jobs.append(token_job(5, 0, 256, i, VT[:, i, 256:512]))
            feats(5, 2 * P, 5, False, all_)
            w = proj(alternate(jobs), ("mix2_units", layer * 9, 6), [], w_second, n_in, low={0: rx, S: rc})
            nchunk = T // S * 2
            beside = stages[-1]
            gt = other("gate", dict(g_sq=nchunk, g_w=nchunk, g_e=nchunk, g_z=nchunk, zc=T // P, zr=T // P, zn=T // P,
                                    g_mm=T // P, g_out=2 * (T // P)), layer=layer, T=T, ready=w)
            beside["gate"] = gt
            beside["gate_in"] = [max(j["out"] for j in jobs[:gate_in] if j["out"][0] == n)
                                 for n in ("evac_act", "evac_dve")]
            beside["pieces"] = {gate_in + 1 + 2 * c: c for c in range(nchunk + 1)}
            items = [(8 + b, 0) for b in range(4)] + ([(8 + b, 1) for b in range(4)] if both else [(11, 1)])
            rp = other("rope", dict(r_sq=len(items), r_ss=len(items), r_rs=len(items), r_y=len(items) - 1, r_rot=4,
                                    r_out=len(items)), layer=layer, items=items, ready=w)
            pairs = []
            for j in range(3):
                pairs.append(dict(q=(lambda i, j=j: PJ[:, j, i * P:(i + 1) * P]),
                                  k=(lambda h, i, j=j: PJ[:, 3 + j, 0:512]),
                                  v=(lambda h, s, j=j: VT[:, s, (2 * j + h) * HD:(2 * j + h + 1) * HD]),
                                  bias=(lambda h, i, j=j: NAB[:, i, 2 * j + h, :]),
                                  keys=lambda i: 4, sel=False, sink=None, dst=N[:, j, 0:S]))
            for j in range(3):
                pairs.append(dict(q=(lambda i, j=j: PJ[:, 8 + j, i * P:(i + 1) * P]),
                                  k=(lambda h, i: PJ[:, 11, 0:512]),
                                  v=(lambda h, s: VT[:, s, 384 + h * HD:384 + (h + 1) * HD]),
                                  bias=None, keys=lambda i: 4, sel=False, sink=None, dst=N[:, 5 + j, 0:S]))
            if both:
                for j in range(3):
                    pairs.append(dict(q=(lambda i, j=j: PJ[:, j, S + i * P:S + (i + 1) * P]),
                                      k=(lambda h, i, j=j: PJ[:, 3 + j, S:2 * S]),
                                      v=(lambda h, s, j=j: VT[:, 2 + s, (2 * j + h) * HD:(2 * j + h + 1) * HD]),
                                      bias=None, keys=lambda i: 2, sel=False, sink=None, dst=N[:, j, S:2 * S]))
                for j in range(3):
                    pairs.append(dict(q=(lambda i, j=j: PJ[:, 8 + j, S + i * P:S + (i + 1) * P]),
                                      k=(lambda h, i: PJ[:, 11, S:2 * S]),
                                      v=(lambda h, s: VT[:, 2 + s, 384 + h * HD:384 + (h + 1) * HD]),
                                      bias=None, keys=lambda i: 2, sel=False, sink=None, dst=N[:, 5 + j, S:2 * S]))
            at = attention(pairs, mods=(20, 12, 0) if both else None, ready=[("r_out", rp["r_out"] + len(items))], bias_ready=(f"bias{2 + layer}", 1))
            na_att.append(at)
            done = [("att_out", at["att_out"] + len(pairs)), ("g_out", gt["g_out"] + 2 * (T // P))]
            merged = []
            for t in toks:
                merged.append(norm("rms", [range(3), range(3, 5), range(5, 8)], ns(t), ns(t),
                                   lambda b, layer=layer: v("g_out", layer * 8 + b), None, done))
            jobs = out_jobs(toks, lambda b, t, layer=layer: modv(layer, 2, t // S)(b))
            r = proj(jobs, ("mix2_units", layer * 9 + 6, 3), [("mod", at["mod"] + 1)] if both else [], w_out, n_out,
                     [(t, blocks_of(m)) for t, m in zip(toks, merged)])[0]
            early = stages[-1]
            for which, t in enumerate(toks):
                ln = lambda name, layer=layer: (lambda b: v(name, layer * 8 + b))
                each = [j["out"] for j in jobs if j["tok"] == t]
                q = norm("ln", [range(KT)], xs(t), xs(t), ln("ln1_g"), ln("ln1_b"), [r], ns(t), each=each)
                q = norm("ln", [range(KT)], xs(t), lambda b: NHI[:, b, :], modv(layer, 4, which),
                         modv(layer, 3, which), [], ns(t), each=blocks_of(q), low=lambda b: NLO[:, b, :])
                q = ffn(("ffn2_units", layer * FB), t, [q], modv(layer, 5, which),
                        ahead=early if which == 0 else None)
                q = norm("ln", [range(KT)], xs(t), xs(t), ln("ln2_g"), ln("ln2_b"), [], ns(t), each=blocks_of(q))
                if which == 0:
                    x_now = q
                else:
                    c_now = q
        total_units = cnt.n["unit"]
        landed = [sem(f"unit_landed{i}") for i in range(RING)]

        def unit_slot(n):
            return ring[n % RING]

        def wait_all(eng, pairs):
            for name, value in pairs:
                eng.wait_ge(sem(name), value)

        for name in list(cnt.n) + ["load_x", "load_vec", "load_con", "load_ctx", "load_oh", "load_misc", "rows", "rows_sb",
                                   "rows_dram", "bt0", "bt1", "nab0", "nab1", "bias0", "bias1", "bias2",
                                   "bias3", "store", "dve_step", "act_step", "unit_used", "setup", "cond_exp", "cond"]:
            sem(name)

        def evacuate(eng, j, job, copy):
            bank_ = acc[j % 4]
            m, n = job["m"], job["n"]
            kind = job["evac"][0]
            if kind == "copy":
                return copy(job["dst"], bank_[0:m, 0:n], 1.0)
            factor = QSCALE if kind == "q" else job["evac"][1]
            return copy(job["dst"].rearrange("p (i t) -> p i t", t=P)[:, :, ::-1],
                        bank_[0:m, 0:n].rearrange("p (i t) -> p i t", t=P), factor)

        def gate_chunks(st):
            if st["T"] == 2 * S:
                return [PJ[:, b, :].rearrange("p (i t) -> p i t", i=2) for b in (6, 7)] + [
                    ZV[:, 0:2, :], ZV[:, 2:4, :]]
            return [PJ[:, 6:8, 0:S], ZV[:, 0:2, :]]

        def gate_tmp(c):
            t = SC[:, (c % 2) * 512:(c % 2 + 1) * 512]
            return t.rearrange("p (i t) -> p i t", i=2)

        block = ctx.enter_context(nc.Block())

        @block.sync
        def _(sp):
            sp.dma_start(X[:, :, 0:S], a["x"]).then_inc(sem("load_x"), 16)

            def steady(n, trips):
                if n < RING:
                    return False
                step = free[n][1] - free[n - RING][1]
                return all(free[n - RING + RING * t + j] == (free[n - RING][0], free[n - RING + j][1] + step * t)
                           for t in range(trips) for j in range(RING))

            n = 0
            for src, start, count in loads:
                at = 0
                while at < count:
                    m = n + at
                    trips = (count - at) // RING
                    while trips > 1 and not steady(m, trips):
                        trips -= 1
                    if trips > 1:
                        name = free[m - RING][0]
                        step = free[m][1] - free[m - RING][1]
                        with sp.Fori(0, trips) as i:
                            for j in range(RING):
                                sp.wait_ge(sem(name), i * step + free[m - RING + j][1])
                                sp.dma_start(ring[(m + j) % RING][:, :],
                                             src[bass.ds(i * RING + (start + at + j), 1), :, :].rearrange(
                                                 "o p c -> (o p) c")).then_inc(landed[(m + j) % RING], 16)
                        at += trips * RING
                    else:
                        if m >= RING:
                            sp.wait_ge(sem(free[m - RING][0]), free[m - RING][1])
                        sp.dma_start(ring[m % RING][:, :], src[start + at]).then_inc(landed[m % RING], 16)
                        at += 1
                n += count
            sp.wait_ge(sem(x_now[0]), x_now[1])
            sp.dma_start(a["out"], X[:, :, 0:S]).then_inc(sem("store"), 16)
            sp.wait_ge(sem("store"), 16)

        @block.gpsimd
        def _(pool):
            pool.dma_start(OH, a["onehot"]).then_inc(sem("load_oh"), 16)
            pool.dma_start(TB, a["table"]).then_inc(sem("load_oh"), 16)
            pool.dma_start(X[:, :, S:2 * S], a["ctx"]).then_inc(sem("load_ctx"), 16)
            pool.dma_start(sinks, bass.AP(a["sinks"].tensor, 0, [[0, P], [1, 16]])).then_inc(sem("load_misc"), 16)
            pool.dma_start(WS[:, :, :, :], a["w_s"]).then_inc(sem("load_misc"), 16)
            for half in range(2):
                for layer in range(2):
                    src = bass.AP(a["b_s"].tensor, layer * 4 * P + half * P, [[0, HD], [2 * P, 2], [1, P]])
                    pool.dma_start(BS[half * HD:(half + 1) * HD, layer, :, :], src).then_inc(sem("load_misc"), 16)
            pool.wait_ge(sem("rows_sb"), 1)
            pool.dma_start(scratch_rows, ROW).then_inc(sem("rows_dram"), 16)
            pool.wait_ge(sem("rows_dram"), 16)
            diagonal = bass.AP(scratch_rows.tensor, 0, [[1, P], [384, 16], [1, 256]])

            def add_mask(region, mask, done):
                for h in range(region.shape[1]):
                    last = pool.tensor_tensor(region[:, h], region[:, h],
                                              mask if len(region.shape) == 3 else
                                              mask.unsqueeze(1).to_broadcast([P, region.shape[2], region.shape[3]]),
                                              ALU.add)
                last.then_inc(sem(done), 1)

            pool.dma_start(BT[:, :, :], diagonal).then_inc(sem("bt0"), 16)
            pool.wait_ge(sem("bt0"), 16)
            pool.wait_ge(sem("load_con"), 16)
            add_mask(BT[:, 0:8, :], cst("mask_mix"), "bias0")
            add_mask(BT[:, 8:16, :], cst("mask_causal"), "bias0")
            pool.wait_ge(sem("att_m"), first_att["att_m"] + len(first_att["tiles"]))
            pool.dma_start(BT[:, :, :], diagonal).then_inc(sem("bt1"), 16)
            pool.wait_ge(sem("bt1"), 16)
            add_mask(BT[:, :, :], cst("mask_swa"), "bias1")
            for layer in range(2):
                before = second_att if layer == 0 else na_att[0]
                pool.wait_ge(sem("att_m"), before["att_m"] + len(before["tiles"]))
                nd = 0
                for r_ in range(4):
                    part = 0 if r_ % 2 else HD
                    for h in range(6):
                        src = bass.AP(a["rpb"].tensor, ((layer * 6 + h) * 7 + 3 - r_) * 128,
                                      [[1, HD], [128, 4], [1, 64]])
                        dst = NAB[part:part + HD, r_ // 2, h, :].rearrange("p (k c) -> p k c", k=4)
                        pool.dma_start(dst, src).then_inc(sem(f"nab{layer}"), 16)
                        nd += 16
                pool.wait_ge(sem(f"nab{layer}"), nd)
                add_mask(BT[:, 0:12, :].rearrange("p h (k c) -> p h k c", c=64), cst("mask_na"), f"bias{2 + layer}")

        @block.tensor
        def _(pe):
            mm = nc.tensor.matmul

            def norm_stage(st):
                if st["ln"]:
                    for j in range(st["nb"]):
                        wait_all(pe, st["each"][j:j + 1])
                        last = mm(mean_bank[:, 0:S], ones, st["src"](j), start=j == 0, stop=j == st["nb"] - 1)
                    last.then_inc(sem("mean"), 1)
                n = 0
                for g, blocks in enumerate(st["groups"]):
                    for j, b in enumerate(blocks):
                        pe.wait_ge(sem("sq"), st["sq"] + n + 1)
                        last = mm(sum_bank[g][:, 0:S], ones, SQ[:, n, :],
                                  start=j == 0, stop=j == len(blocks) - 1, skip_group_check=True)
                        n += 1
                    last.then_inc(sem("ss"), 1)

            def ffn_stage(st):
                def parts(out, w, k, hi, lo, first, last):
                    cols = slice(k * P, (k + 1) * P)
                    mm(out, WHI[w][:, cols], hi, start=first, stop=False, skip_group_check=True)
                    mm(out, WHI[w][:, cols], lo, start=False, stop=False, skip_group_check=True)
                    return mm(out, WLO[w][:, cols], hi, start=False, stop=last, skip_group_check=True)

                def ffn_up(at, u, half, wait):
                    pe.wait_ge(sem("w_split"), wait(st["split"] + at + 1, 3))
                    for k in range(KT):
                        if u == 0 and half == 0:
                            if st["rms"]:
                                pe.wait_ge(sem("n_split"), st["n_split"] + k + 1)
                            else:
                                pe.wait_ge(sem("n_low"), st["ready"][0][1] - KT + k + 1)
                        last = parts((up, stat)[half][u % 2][:, 0:S], at % SPLIT, k, NHI[:, k, :],
                                     NLO[:, k, :], k == 0, k == KT - 1)
                    last.then_inc(sem("chunk_used"), 1)

                def ffn_down(at, d, first, wait):
                    pe.wait_ge(sem("w_split"), wait(st["split"] + at + 1, 3))
                    pe.wait_ge(sem("gated"), wait(st["gated"] + d + 1, 1))
                    for b in range(KT):
                        last = parts(acc[b // 2][:, (b % 2) * S:(b % 2 + 1) * S], at % SPLIT, b, GHI[d % 2][:, :],
                                     GLO[d % 2][:, :], first and b % 2 == 0, True)
                    last.then_inc(sem("chunk_used"), 1)

                def both(u, wait):
                    if u >= 2:
                        pe.wait_ge(sem("hidden"), wait(st["act"] + u - 1, 1))
                    ffn_up(at_up(u, 0), u, 0, wait)
                    ffn_up(at_up(u, 1), u, 1, wait)

                def fixed(value, per):
                    return value

                both(0, fixed)
                if st["rms"]:
                    pe.wait_ge(sem("load_con"), 16)
                    for b in range(KT):
                        pe.wait_ge(sem("sq"), st["sq"] + b + 1)
                        last = mm(acc[3][:, 0:S], ones, SQ[:, b, :], start=b == 0, stop=b == KT - 1)
                    last.then_inc(sem("ss"), 1)
                both(1, fixed)
                ffn_down(at_down(0), 0, True, fixed)
                trips = (FB - 2) // RING
                with pe.Fori(0, trips) as i:
                    def turning(value, per):
                        return i * (RING * per) + value

                    for j in range(RING):
                        both(2 + j, turning)
                        ffn_down(at_down(1 + j), 1 + j, False, turning)
                ffn_down(at_down(FB - 1), FB - 1, False, fixed)

            def short_job(st, j, job, done_blocks):
                start, length = job["span"]
                pe.wait_ge(sem("w_cols"), st["w_cols"] + job["split"])
                w = chunk_of(ring_short[job["slot"] % RING][:, :])
                off, turn = job["off"], job["turn"]
                for k in range(KT):
                    for tok in (0, S):
                        if start < tok + S and start + length > tok and (tok, k) not in done_blocks:
                            done_blocks.add((tok, k))
                            pe.wait_ge(sem("n_low"), st["n_low"][tok, k])
                    n_hi, n_lo = st["n_hi"][:, k, start:start + length], N_LO[:, k, start:start + length]
                    if job["tm"]:
                        out = acc[j % 4][:, 0:job["n"]]
                        w_hi, w_lo = st["weights"][:, turn % 4, k, :], w[:, k, off:off + job["n"]]
                        if job["n"] > P:
                            chunks = job["n"] // P
                            out, w_lo = [ap.rearrange("p (b c) -> p b c", b=chunks) for ap in (out, w_lo)]
                            w_hi = st["weights"][:, turn % 4:turn % 4 + chunks, k, :]
                    else:
                        out = acc[j % 4][0:job["m"], 0:job["n"]]
                        w_hi = place(st["weights"], turn)[:, k, off % P:off % P + job["m"]]
                        w_lo = w[:, k, off:off + job["m"]]
                    for p, (w_, n_) in enumerate(((w_hi, n_hi), (w_hi, n_lo), (w_lo, n_hi))):
                        lhs, rhs = (n_, w_) if job["tm"] else (w_, n_)
                        last = mm(out, lhs, rhs, start=k == 0 and p == 0, stop=k == KT - 1 and p == 2,
                                  skip_group_check=True)
                return last

            def proj_stage(st):
                wait_all(pe, st["ready"])
                jobs = st["jobs"]
                seen, done_blocks = set(), set()
                for j, job in enumerate(jobs):
                    if st["weights"] is None and job["slot"] not in seen:
                        seen.add(job["slot"])
                        pe.wait_ge(landed[job["slot"] % RING], 16 * (job["slot"] // RING + 1))
                    if j >= 4:
                        pe.wait_ge(sem(jobs[j - 4]["out"][0]), jobs[j - 4]["out"][1])
                    w = unit_slot(job["slot"])
                    if st["weights"] is not None:
                        short_job(st, j, job, done_blocks).then_inc(sem("unit_used" if job["last"] else "proj"), 1)
                        continue
                    for k in range(job["kts"]):
                        cols = w[:, k * job["kstep"] + job["off"]:k * job["kstep"] + job["off"] +
                                 (job["n"] if job["tm"] else job["m"])] if job["off"] < 1024 or job["kts"] == KT \
                            else w[:, 1024 + k * 256 + job["off"] - 1024:1024 + k * 256 + job["off"] - 1024 + job["m"]]
                        lhs, rhs = (job["src"](k), cols) if job["tm"] else (cols, job["src"](k))
                        last = mm(acc[j % 4][0:job["m"], 0:job["n"]], lhs, rhs, start=k == 0,
                                  stop=k == job["kts"] - 1, skip_group_check=True)
                    last.then_inc(sem("unit_used" if job["last"] else "proj"), 1)

            def index_stage(st):
                wait_all(pe, st["ready"])
                for i in range(2):
                    nc.tensor.transpose(acc[2 + i][:, 0:8], PJE[0:8, 21, i * P:(i + 1) * P],
                                        ident[0:8, 0:8]).then_inc(sem("wx_t"), 1)
                for n in range(16):
                    i, h = n // 8, n % 8
                    if n >= 2:
                        pe.wait_ge(sem("ix_r"), st["ix_r"] + n - 1)
                    mm(acc[n % 2][:, 0:(i + 1) * P], QI[0:32, h, i * P:(i + 1) * P], PJE[0:32, 20, 0:(i + 1) * P],
                       start=True, stop=True).then_inc(sem("ix_s"), 1)

            def attn_stage(st):
                pairs, tiles = st["pairs"], st["tiles"]
                nt = len(tiles)

                def scores(t):
                    n, h, i = tiles[t]
                    pr = pairs[n]
                    if t >= 3:
                        pe.wait_ge(sem("att_e"), st["att_e"] + t - 2)
                    lo = h * HD
                    mm(acc[t % 3][:, 0:pr["keys"](i) * P], pr["q"](i)[lo:lo + HD], pr["k"](h, i)[lo:lo + HD],
                       start=True, stop=True).then_inc(sem("att_s"), 1)

                def turn(t):
                    n, h, i = tiles[t]
                    pe.wait_ge(sem("att_n"), st["att_n"] + t + 1)
                    if t >= 2:
                        pe.wait_ge(sem("att_c"), st["att_c"] + t - 1)
                    for s in range(pairs[n]["keys"](i)):
                        last = nc.tensor.transpose(up[t % 2][:, s * P:(s + 1) * P], aP[t % 3][:, s * P:(s + 1) * P],
                                                   ident)
                    last.then_inc(sem("att_t"), 1)

                def values(t):
                    n, h, i = tiles[t]
                    pr = pairs[n]
                    pe.wait_ge(sem("att_c"), st["att_c"] + t + 1)
                    if h == 0 and n >= 2:
                        pe.wait_ge(sem("att_out"), st["att_out"] + n - 1)
                    o = stat[n % 2][h * HD:(h + 1) * HD]
                    pT = aT[(2 * n + h) % 2]
                    ks = pr["keys"](1)
                    for s in range(ks):
                        t0 = P if s >= pr["keys"](0) else 0
                        last = mm(o[:, t0:S], pr["v"](h, s), pT[:, s, t0:S], start=s == 0, stop=s == ks - 1,
                                  skip_group_check=True)
                    last.then_inc(sem("att_o"), 1)

                def pick(u):
                    pe.wait_ge(sem("mod_row"), st["mod_row"] + u + 1)
                    for b in range(3):
                        col = UC + (u * 3 + b) * 2
                        last = mm(acc[3][:, col:col + 2], ROWS[:, b * P:(b + 1) * P], cst("pick"), start=True,
                                  stop=True, skip_group_check=True)
                    return last

                def modulation(u, half):
                    n = st["mod_unit"] + u
                    if half == 0:
                        if u:
                            pick(u - 1)
                        pe.wait_ge(landed[n % RING], 16 * (n // RING + 1))
                    for j in range(4):
                        k = 4 * half + j
                        last = mm(acc[3][32 * j:32 * j + 32, 0:UC], CS[:, k, :],
                                  unit_slot(n)[:, k * UC:(k + 1) * UC], start=half == 0, stop=half == 1,
                                  skip_group_check=True)
                    if half:
                        last.then_inc(sem("unit_used"), 1)

                lead = 0
                if st["mods"] is not None:
                    pe.wait_ge(sem("cond"), 1)
                    lead = st["mods"][2]
                    if lead:
                        pe.wait_ge(sem(st["bank_free"][0]), st["bank_free"][1])
                    for u in range(lead):
                        modulation(u, 0)
                        modulation(u, 1)
                wait_all(pe, st["ready"])
                for t in range(nt + 4):
                    if st["mods"] is not None and t < nt and (t + 1) % st["period"] == 0:
                        modulation(lead + t // st["period"], 1)
                    if t < nt:
                        scores(t)
                    if 0 <= t - 3 < nt:
                        turn(t - 3)
                    if 0 <= t - 4 < nt and tiles[t - 4][2] == 1:
                        values(t - 4)
                    if st["mods"] is not None and t < nt and t % st["period"] == 0:
                        modulation(lead + t // st["period"], 0)
                if st["mods"] is not None:
                    pick(st["mods"][1] - 1).then_inc(sem("mod_sum"), 1)

            def gate_stage(st):
                T, layer = st["T"], st["layer"]
                wait_all(pe, st["ready"])
                pe.wait_ge(sem("load_misc"), 16 * 6)
                for tb in range(T // P):
                    pe.wait_ge(sem("zn"), st["zn"] + tb + 1)
                    for g in range(4):
                        h = g % 2
                        last = mm(acc[tb][h * HD:(h + 1) * HD, (g // 2) * P:(g // 2 + 1) * P],
                                  ZV[:, tb, g * HD:(g + 1) * HD], WS[:, layer, g, :], start=True, stop=True,
                                  skip_group_check=True)
                    last.then_inc(sem("g_mm"), 1)

            def rope_stage(st):
                for n, (b, s) in enumerate(st["items"]):
                    pe.wait_ge(sem("r_sq"), st["r_sq"] + n + 1)
                    if n >= 4:
                        pe.wait_ge(sem("r_rs"), st["r_rs"] + n - 3)
                    mm(head_bank[n % 4][:, 0:S], cst("halves"), SQ[:, n, :], start=True,
                       stop=True, skip_group_check=True).then_inc(sem("r_ss"), 1)
                for n in range(4):
                    pe.wait_ge(sem("r_y"), st["r_y"] + n + 1)
                    mm(acc[n][:, 0:S], cst("swap"), SC[:, n * S:(n + 1) * S],
                       start=True, stop=True, skip_group_check=True).then_inc(sem("r_rot"), 1)

            def bias_rows():
                pe.wait_ge(sem("load_oh"), 32)
                mm(stat[1][0:16, 0:384], TB, OH, start=True, stop=True).then_inc(sem("rows"), 1)

            run = dict(norm=norm_stage, ffn=ffn_stage, proj=proj_stage, index=index_stage, attn=attn_stage,
                       gate=gate_stage, rope=rope_stage)
            for n, st in enumerate(stages):
                run[st["kind"]](st)
                if n == 0:
                    bias_rows()

        @block.scalar
        def _(act):
            fn = nc.scalar.activation
            steps = [0]

            def link(ins):
                steps[0] += 1
                ins.then_inc(sem("act_step"), 1)
                act.wait_ge(sem("act_step"), steps[0])

            def norm_stage(st):
                wait_all(act, st["ready"])
                n = 0
                for g, blocks in enumerate(st["groups"]):
                    for b in blocks:
                        if st["each"] and not st["ln"]:
                            wait_all(act, st["each"][n:n + 1])
                        if st["ln"]:
                            act.wait_ge(sem("cen"), st["cen"] + n + 1)
                            src = st["centred"](b)
                        else:
                            src = st["src"](b)
                        fn(SQ[:, n, :], src, ACT.Square).then_inc(sem("sq"), 1)
                        n += 1
                if "next_ffn" in st:
                    ffn_ahead(st["next_ffn"])
                if "next_proj" in st:
                    for c in range(2):
                        round_cols(st["next_proj"], c)
                for g, blocks in enumerate(st["groups"]):
                    act.wait_ge(sem("ss"), st["ss"] + g + 1)
                    if g == 0 and st["rstd_free"] > 0:
                        act.wait_ge(sem("rms_out"), st["rstd_free"])
                    link(fn(RS[:, g, :], sum_bank[g][:, 0:S], ACT.Ln,
                            bias=eps, scale=1.0 / (len(blocks) * P)))
                    fn(RS[:, g, :], RS[:, g, :], ACT.Exp, scale=-0.5).then_inc(sem("rstd"), 1)
                if st["ln"]:
                    for b in range(st["nb"]):
                        act.wait_ge(sem("scaled"), st["scaled"] + b + 1)
                        fn(st["dst"](b), st["centred"](b), ACT.Identity, bias=st["shift"](b)).then_inc(sem("ln_out"), 1)

            def fixed(value, per):
                return value

            def round_chunk(st, at, u, third, wait):
                n = st["unit"] + u
                act.wait_ge(landed[n % RING], wait(16 * (n // RING + 1), 16 / RING))
                if at >= SPLIT:
                    act.wait_ge(sem("chunk_used"), wait(st["chunk"] + at - SPLIT + 1, 3))
                fn(WHI[at % SPLIT][:, :], unit_slot(n)[:, third * D:(third + 1) * D], ACT.Copy).then_inc(
                    sem("w_hi"), 1)

            def ffn_ahead(st):
                round_chunk(st, 0, 0, 0, fixed)
                round_chunk(st, 1, 0, 1, fixed)

            def round_cols(st, c):
                slot, third, turn = st["chunks"][c]
                act.wait_ge(landed[slot % RING], 16 * (slot // RING + 1))
                if st["after"][c] >= 0:
                    done = st["jobs"][st["after"][c]]["done"]
                    act.wait_ge(sem(done[0]), done[1])
                fn(place(st["weights"], turn),
                   chunk_of(unit_slot(slot)[:, :])[:, :, third * P:(third + 1) * P], ACT.Copy).then_inc(
                    sem("w_cols_hi"), 1)

            def ffn_stage(st):
                tok = st["tok"]
                if st["rms"]:
                    wait_all(act, st["ready"])
                    if st["each"]:
                        wait_all(act, st["each"][0:1])
                    if st["each"] and not st["ahead"]:
                        ffn_ahead(st)
                    for k in range(KT):
                        if st["each"]:
                            wait_all(act, st["each"][k:k + 1])
                        fn(NHI[:, k, :], X[:, k, tok:tok + S], ACT.Identity, scale=st["rms"](k)).then_inc(
                            sem("n_hi"), 1)
                    if not st["each"]:
                        ffn_ahead(st)
                    for k in range(KT):
                        fn(SQ[:, k, :], X[:, k, tok:tok + S], ACT.Square).then_inc(sem("sq"), 1)
                round_chunk(st, at_up(1, 0), 1, 0, fixed)
                round_chunk(st, at_up(1, 1), 1, 1, fixed)
                if st["rms"]:
                    act.wait_ge(sem("ss"), st["ss"] + 1)
                    link(fn(RS[:, 0, :], acc[3][:, 0:S], ACT.Ln, bias=eps, scale=1.0 / D))
                    fn(RS[:, 0, :], RS[:, 0, :], ACT.Exp, scale=-0.5).then_inc(sem("rstd"), 1)

                def hidden(d, ahead, wait):
                    act.wait_ge(sem("chunk_used"), wait(st["chunk"] + at_up(d, 0) + 1, 3))
                    if d >= 2:
                        act.wait_ge(sem("gated"), wait(st["gated"] + d - 1, 1))
                    a_ = up[d % 2][:, 0:S]
                    if st["rms"]:
                        act.wait_ge(sem("scaled_a"), wait(st["scaled_a"] + d + 1, 1))
                        a_ = fA[d % 2][:, :]
                    fn(fE[d % 2][:, :], a_, ACT.Exp, scale=-1.0).then_inc(sem("ffn_exp"), 1)
                    round_chunk(st, at_down(d), d, 2, wait)
                    act.wait_ge(sem("hidden"), wait(st["act"] + d + 1, 1))
                    if d >= 2:
                        act.wait_ge(sem("chunk_used"), wait(st["chunk"] + at_down(d - 2) + 1, 3))
                    fn(GHI[d % 2][:, :], fG[d % 2][:, :], ACT.Copy).then_inc(sem("hidden_hi"), 1)
                    if ahead:
                        round_chunk(st, at_up(d + 2, 0), d + 2, 0, wait)
                        round_chunk(st, at_up(d + 2, 1), d + 2, 1, wait)

                for d in range(4):
                    hidden(d, True, fixed)
                with act.Fori(0, (FB - 6) // RING) as i:
                    def turning(value, per):
                        return i * int(RING * per) + value

                    for d in range(4, 4 + RING):
                        hidden(d, True, turning)
                for d in (FB - 2, FB - 1):
                    hidden(d, False, fixed)

            def proj_stage(st):
                chunks = st["first"] if st["weights"] is not None else 0
                if chunks:
                    wait_all(act, st["ready"])
                    for c in range(2 if st["begun"] else 0, 2):
                        round_cols(st, c)
                    for tok, k, written in st["blocks"]:
                        if written:
                            act.wait_ge(sem(written[0]), written[1])
                        fn(st["n_hi"][:, k, tok:tok + S], N[:, k, tok:tok + S], ACT.Copy).then_inc(
                            sem("n_high"), 1)
                    for c in range(2, chunks):
                        round_cols(st, c)
                    if "early" in st:
                        ffn_ahead(st["early"])
                for j, job in enumerate(st["jobs"]):
                    if job["eng"] == "act":
                        act.wait_ge(sem(job["done"][0]), job["done"][1])
                        evacuate(act, j, job, lambda d, s, f: fn(d, s, ACT.Copy, scale=f)).then_inc(
                            sem("evac_act"), 1)
                    if chunks:
                        for c, after in enumerate(st["after"]):
                            if after == j:
                                round_cols(st, c)
                    if j in st.get("pieces", ()):
                        gate_piece(st, st["pieces"][j])

            def index_stage(st):
                for n in range(16):
                    i = n // 8
                    act.wait_ge(sem("ix_s"), st["ix_s"] + n + 1)
                    if n >= 2:
                        act.wait_ge(sem("ix_a"), st["ix_a"] + n - 1)
                    fn(RELU[n % 2][:, 0:(i + 1) * P], acc[n % 2][:, 0:(i + 1) * P], ACT.Relu).then_inc(
                        sem("ix_r"), 1)

            def attn_stage(st):
                pairs, tiles = st["pairs"], st["tiles"]

                def exps(t):
                    n, h, i = tiles[t]
                    pr = pairs[n]
                    w = pr["keys"](i) * P
                    act.wait_ge(sem("att_m"), st["att_m"] + t + 1)
                    if t >= 3:
                        act.wait_ge(sem("att_t"), st["att_t"] + t - 2)
                    m = ATT[:, t % 3]
                    nm = m[:, 0:1]
                    if pr["bias"] is None:
                        last = fn(aP[t % 3][:, 0:w], acc[t % 3][:, 0:w], ACT.Exp, bias=nm, accum_out=m[:, 2:3])
                    else:
                        wb = min(w, 256)
                        last = fn(aP[t % 3][:, 0:wb], aS[t % 3][:, 0:wb], ACT.Exp, bias=nm, scale=-1.0,
                                  accum_out=m[:, 2:3])
                        if w > wb:
                            last = fn(aP[t % 3][:, wb:w], acc[t % 3][:, wb:w], ACT.Exp, bias=nm,
                                      accum_out=m[:, 3:4])
                    if pr["sink"] is not None:
                        last = fn(m[:, 3:4], pr["sink"](h), ACT.Exp, bias=nm)
                    last.then_inc(sem("att_e"), 1)

                def copies(t):
                    n, h, i = tiles[t]
                    ks = pairs[n]["keys"](i)
                    b = 2 * n + h
                    act.wait_ge(sem("att_t"), st["att_t"] + t + 1)
                    if b >= 2 and i == 0:
                        act.wait_ge(sem("att_o"), st["att_o"] + b - 1)
                    fn(aT[b % 2][:, 0:ks, i * P:(i + 1) * P][:, :, ::-1],
                       up[t % 2][:, 0:ks * P].rearrange("p (s t) -> p s t", t=P), ACT.Copy).then_inc(sem("att_c"), 1)

                def modulation(u):
                    act.wait_ge(sem("unit_used"), st["mod_used"] + u + 1)
                    fn(ROWS[:, :], acc[3][:, 0:UC], ACT.Copy).then_inc(sem("mod_row"), 1)

                nt = len(tiles)
                lead = st["mods"][2] if st["mods"] is not None else 0
                for u in range(lead):
                    modulation(u)
                for t in range(nt + 3):
                    if st["mods"] is not None and t < nt and (t + 1) % st["period"] == 0:
                        modulation(lead + t // st["period"])
                    if t < nt:
                        exps(t)
                    if 0 <= t - 3 < nt:
                        copies(t - 3)
                if "next_proj" in st:
                    for c in range(2):
                        round_cols(st["next_proj"], c)

            def gate_stage(st):
                pass

            def gate_piece(proj_st, c):
                st = proj_st["gate"]
                chunks = gate_chunks(st)
                if c == 0:
                    wait_all(act, proj_st["gate_in"])
                if c < len(chunks):
                    if c >= 2:
                        act.wait_ge(sem("g_z"), st["g_z"] + c - 1)
                    fn(gate_tmp(c), chunks[c], ACT.Square).then_inc(sem("g_sq"), 1)
                    act.wait_ge(sem("g_w"), st["g_w"] + c + 1)
                    fn(gate_tmp(c), gate_tmp(c), ACT.Exp, scale=-GELU_C).then_inc(sem("g_e"), 1)
                    return
                for tb in range(st["T"] // P):
                    act.wait_ge(sem("zc"), st["zc"] + tb + 1)
                    link(fn(SC[:, 1024 + tb * 256:1280 + tb * 256], ZV[:, tb, :], ACT.Square, accum_out=LNS[:, tb, 2:3]))
                    link(fn(LNS[:, tb, 3:4], LNS[:, tb, 2:3], ACT.Ln, bias=eps, scale=1.0 / 256))
                    fn(LNS[:, tb, 4:5], LNS[:, tb, 3:4], ACT.Exp, scale=-0.5).then_inc(sem("zr"), 1)

            def rope_stage(st):
                wait_all(act, st["ready"])
                for n, (b, s) in enumerate(st["items"]):
                    fn(SQ[:, n, :], PJ[:, b, s * S:(s + 1) * S], ACT.Square).then_inc(sem("r_sq"), 1)
                for n, (b, s) in enumerate(st["items"]):
                    act.wait_ge(sem("r_ss"), st["r_ss"] + n + 1)
                    link(fn(SQ[:, n, :], head_bank[n % 4][:, 0:S], ACT.Ln, bias=eps,
                            scale=1.0 / HD))
                    fn(SQ[:, n, :], SQ[:, n, :], ACT.Exp, scale=-0.5).then_inc(sem("r_rs"), 1)

            act.dma_start(vec[:, :], a["vec"]).then_inc(sem("load_vec"), 16)
            act.dma_start(con[:, :], a["con"]).then_inc(sem("load_con"), 16)
            nc.scalar.preload_act_table_set("natural_log_exp_and_others")
            act.wait_ge(sem("setup"), 1)
            act.wait_ge(sem("load_vec"), 16)
            fn(CTMP, vec[:, VEC["cond"]:VEC["cond"] + 16], ACT.Exp, scale=-1.0).then_inc(sem("cond_exp"), 1)
            run = dict(norm=norm_stage, ffn=ffn_stage, proj=proj_stage, index=index_stage, attn=attn_stage,
                       gate=gate_stage, rope=rope_stage)
            for st in stages:
                run[st["kind"]](st)

        @block.vector
        def _(dve):
            ve = nc.vector
            steps = [0]

            def link(ins):
                steps[0] += 1
                ins.then_inc(sem("dve_step"), 1)
                dve.wait_ge(sem("dve_step"), steps[0])

            def mark(ins):
                steps[0] += 1
                ins.then_inc(sem("dve_step"), 1)
                return steps[0]

            def need(value):
                dve.wait_ge(sem("dve_step"), value)

            def norm_stage(st):
                if st["ln"]:
                    wait_all(dve, st["ready"])
                    dve.wait_ge(sem("mean"), st["mean"] + 1)
                    for b in range(st["nb"]):
                        ve.scalar_tensor_tensor(out=st["centred"](b), in0=mean_bank[:, 0:S], scalar=-1.0 / (st["nb"] * P),
                                                in1=st["src"](b), op0=ALU.mult, op1=ALU.add).then_inc(sem("cen"), 1)
                if "next_ffn" in st:
                    ffn_ahead(st["next_ffn"])
                if "next_proj" in st:
                    for c in range(2):
                        rest_cols(st["next_proj"], c)
                n = 0
                for g, blocks in enumerate(st["groups"]):
                    dve.wait_ge(sem("rstd"), st["rstd"] + g + 1)
                    for b in blocks:
                        src = st["centred"](b) if st["ln"] else st["src"](b)
                        dst = st["centred"](b) if st["ln"] else st["dst"](b)
                        ve.scalar_tensor_tensor(out=dst, in0=src, scalar=st["gain"](b), in1=RS[:, g, :],
                                                op0=ALU.mult, op1=ALU.mult).then_inc(
                            sem("scaled" if st["ln"] else "rms_out"), 1)
                        n += 1
                if st["low"]:
                    for b in range(st["nb"]):
                        dve.wait_ge(sem("ln_out"), st["out"] + b + 1)
                        ve.scalar_tensor_tensor(out=st["low"](b), in0=st["centred"](b), scalar=st["shift"](b),
                                                in1=st["dst"](b).bitcast(F32), op0=ALU.add, op1=ALU.subtract).then_inc(
                            sem("n_low"), 1)

            def rest_cols(st, c):
                slot, third, turn = st["chunks"][c]
                raw = chunk_of(unit_slot(slot)[:, :])[:, :, third * P:(third + 1) * P]
                dve.wait_ge(sem("w_cols_hi"), st["w_cols_hi"] + c + 1)
                low = chunk_of(ring_short[slot % RING][:, :])[:, :, third * P:(third + 1) * P]
                ve.tensor_tensor(low, raw, place(st["weights"], turn).bitcast(F32), ALU.subtract).then_inc(
                    sem("w_cols"), 1)

            def fixed(value, per):
                return value

            def rest_chunk(st, at, u, third, wait):
                n = st["unit"] + u
                dve.wait_ge(sem("w_hi"), wait(st["hi"] + at + 1, 3))
                ve.tensor_tensor(WLO[at % SPLIT][:, :], unit_slot(n)[:, third * D:(third + 1) * D],
                                 WHI[at % SPLIT][:, :].bitcast(F32), ALU.subtract).then_inc(sem("w_split"), 1)

            def ffn_ahead(st):
                rest_chunk(st, 0, 0, 0, fixed)
                rest_chunk(st, 1, 0, 1, fixed)

            def ffn_stage(st):
                tok = st["tok"]
                if st["rms"] and st["each"] and not st["ahead"]:
                    ffn_ahead(st)
                if st["rms"]:
                    for k in range(KT):
                        dve.wait_ge(sem("n_hi"), st["n_hi"] + k + 1)
                        ve.scalar_tensor_tensor(out=NLO[:, k, :], in0=X[:, k, tok:tok + S], scalar=st["rms"](k),
                                                in1=NHI[:, k, :].bitcast(F32), op0=ALU.mult,
                                                op1=ALU.subtract).then_inc(sem("n_split"), 1)
                    if not st["each"]:
                        ffn_ahead(st)
                rest_chunk(st, at_up(1, 0), 1, 0, fixed)
                rest_chunk(st, at_up(1, 1), 1, 1, fixed)
                base = steps[0]
                ns_ = 3
                if st["rms"]:
                    dve.wait_ge(sem("rstd"), st["rstd"] + 1)

                def hidden(d, ahead, wait):
                    e, g = fE[d % 2][:, :], fG[d % 2][:, :]
                    a_, b_ = up[d % 2][:, 0:S], stat[d % 2][:, 0:S]
                    if st["rms"]:
                        dve.wait_ge(sem("chunk_used"), wait(st["chunk"] + at_up(d, 0) + 1, 3))
                        a_ = fA[d % 2][:, :]
                        ve.tensor_tensor(a_, up[d % 2][:, 0:S], RS[:, 0, :], ALU.mult).then_inc(sem("scaled_a"), 1)
                    dve.wait_ge(sem("ffn_exp"), wait(st["exp"] + d + 1, 1))
                    step = [0]

                    def next_step(ins):
                        step[0] += 1
                        ins.then_inc(sem("dve_step"), 1)
                        dve.wait_ge(sem("dve_step"), wait(base + ns_ * d + step[0], ns_))

                    next_step(ve.tensor_scalar(e, e, 1.0, None, ALU.add))
                    next_step(ve.reciprocal(e, e))
                    next_step(ve.tensor_tensor(e, e, a_, ALU.mult))
                    dve.wait_ge(sem("chunk_used"), wait(st["chunk"] + at_up(d, 1) + 1, 3))
                    ve.tensor_tensor(g, e, b_, ALU.mult).then_inc(sem("hidden"), 1)
                    rest_chunk(st, at_down(d), d, 2, wait)
                    dve.wait_ge(sem("hidden_hi"), wait(st["g_hi"] + d + 1, 1))
                    ve.tensor_tensor(GLO[d % 2][:, :], g, GHI[d % 2][:, :].bitcast(F32), ALU.subtract).then_inc(
                        sem("gated"), 1)
                    if ahead:
                        rest_chunk(st, at_up(d + 2, 0), d + 2, 0, wait)
                        rest_chunk(st, at_up(d + 2, 1), d + 2, 1, wait)

                for d in range(4):
                    hidden(d, True, fixed)
                with dve.Fori(0, (FB - 6) // RING) as i:
                    def turning(value, per):
                        return i * (RING * per) + value

                    for d in range(4, 4 + RING):
                        hidden(d, True, turning)
                for d in (FB - 2, FB - 1):
                    hidden(d, False, fixed)
                steps[0] += ns_ * FB
                dve.wait_ge(sem("chunk_used"), st["chunk"] + CHUNKS)
                if st["rms"]:
                    def factored(b):
                        return mark(ve.tensor_tensor(SQ[:, b, :], acc[b // 2][:, (b % 2) * S:(b % 2 + 1) * S],
                                                     RS[:, 0, :], ALU.mult))

                    ready = [factored(0)]
                    for b in range(KT):
                        if b + 1 < KT:
                            ready.append(factored(b + 1))
                        need(ready[b])
                        residual(X[:, b, tok:tok + S], SQ[:, b, :], 0.5, False, None)
                    return
                for b in range(KT):
                    x = X[:, b, tok:tok + S]
                    residual(x, acc[b // 2][:, (b % 2) * S:(b % 2 + 1) * S],
                             st["resid"](b) if st["resid"] else 0.5, st["resid"] is not None, st["scaled"] + b + 1)

            def residual(x, y, gain, post, value):
                if post:
                    ve.tensor_scalar(x, x, ALPHA, None, ALU.mult).then_inc(sem("alpha"), 1)
                    dve.wait_ge(sem("alpha"), value)
                ve.scalar_tensor_tensor(out=x, in0=y, scalar=gain, in1=x, op0=ALU.mult, op1=ALU.add).then_inc(
                    sem("resid"), 1)

            def proj_stage(st):
                chunks = st["first"] if st["weights"] is not None else 0
                if chunks:
                    for c in range(2 if st["begun"] else 0, 2):
                        rest_cols(st, c)
                    for n, (tok, k, _) in enumerate(st["blocks"]):
                        dve.wait_ge(sem("n_high"), st["n_high_base"] + n + 1)
                        ve.tensor_tensor(N_LO[:, k, tok:tok + S], N[:, k, tok:tok + S],
                                         st["n_hi"][:, k, tok:tok + S].bitcast(F32), ALU.subtract).then_inc(sem("n_low"), 1)
                    for c in range(2, chunks):
                        rest_cols(st, c)
                    if "early" in st:
                        ffn_ahead(st["early"])
                for j, job in enumerate(st["jobs"]):
                    if job["eng"] == "dve":
                        take_out(j, job)
                    if chunks:
                        for c, after in enumerate(st["after"]):
                            if after == j:
                                rest_cols(st, c)
                    if j in st.get("pieces", ()):
                        gate_piece(st, st["pieces"][j])

            def take_out(j, job):
                dve.wait_ge(sem(job["done"][0]), job["done"][1])
                if job["evac"][0] == "resid":
                    gain = job["evac"][1]
                    residual(job["dst"], acc[j % 4][:, 0:S], 1.0 if gain is None else gain, gain is not None,
                             job.get("scaled"))
                else:
                    evacuate(dve, j, job, lambda d, s, f: ve.tensor_scalar(d, s, f, None, ALU.mult)).then_inc(
                        sem("evac_dve"), 1)

            def index_stage(st):
                wait_all(dve, st["ready"])
                for i in range(2):
                    dve.wait_ge(sem("wx_t"), st["wx_t"] + i + 1)
                    ve.tensor_copy(WX[:, i, :], acc[2 + i][:, 0:8]).then_inc(sem("wx"), 1)
                    dve.wait_ge(sem("wx"), st["wx"] + i + 1)
                for n in range(16):
                    i, h = n // 8, n % 8
                    w = (i + 1) * P
                    dve.wait_ge(sem("ix_r"), st["ix_r"] + n + 1)
                    if h > 0:
                        dve.wait_ge(sem("ix_a"), st["ix_a"] + n)
                    before = SCORE[:, i, 0:w] if h else cst("mask_causal")[:, (1 - i) * P:2 * P]
                    ve.scalar_tensor_tensor(out=SCORE[:, i, 0:w], in0=RELU[n % 2][:, 0:w], scalar=WX[:, i, h:h + 1],
                                            in1=before, op0=ALU.mult, op1=ALU.add).then_inc(sem("ix_a"), 1)
                dve.wait_ge(sem("ix_a"), st["ix_a"] + 16)
                for i in range(2):
                    w = (i + 1) * P
                    for r_ in range(TOPK // 8):
                        top8 = small[:, 160 + 8 * i:168 + 8 * i]
                        link(ve.max(top8, SCORE[:, i, 0:w]))
                        link(ve.match_replace(SCORE[:, i, 0:w], top8, SCORE[:, i, 0:w], TAKEN))
                for i in range(2):
                    w = (i + 1) * P
                    last = ve.tensor_scalar(SEL[:, i, 0:w], SCORE[:, i, 0:w], TAKEN / 2, NEG, ALU.is_gt, ALU.mult)
                last.then_inc(sem("top"), 1)

            def attn_stage(st):
                pairs, tiles = st["pairs"], st["tiles"]
                wait_all(dve, st["ready"])
                dve.wait_ge(sem(st["bias_ready"][0]), st["bias_ready"][1])

                def maxima(t):
                    n, h, i = tiles[t]
                    pr = pairs[n]
                    w = pr["keys"](i) * P
                    m = ATT[:, t % 3]
                    s = acc[t % 3]
                    dve.wait_ge(sem("att_s"), st["att_s"] + t + 1)
                    if t >= 3:
                        dve.wait_ge(sem("att_n"), st["att_n"] + t - 2)
                    if pr["bias"] is None:
                        ve.tensor_reduce(m[:, 0:1], s[:, 0:w], AX.X, ALU.max, negate=True).then_inc(sem("att_m"), 1)
                        return
                    wb = min(w, 256)
                    bias = pr["bias"](h, i)
                    src = s[:, 0:wb]
                    if pr["sel"]:
                        added = mark(ve.tensor_tensor(aS[t % 3][:, 0:wb], src, bias, ALU.add))
                        src, bias = aS[t % 3][:, 0:wb], SEL[:, i, 0:wb]
                        yield
                        need(added)
                    if w == wb:
                        ve.tensor_tensor_reduce(aS[t % 3][:, 0:wb], src, bias, -1.0, -NEG, ALU.add, ALU.min,
                                                m[:, 0:1]).then_inc(sem("att_m"), 1)
                        return
                    ve.tensor_tensor_reduce(aS[t % 3][:, 0:wb], src, bias, -1.0, -NEG, ALU.add, ALU.min, m[:, 4:5])
                    yield
                    rest = mark(ve.tensor_reduce(m[:, 5:6], s[:, wb:w], AX.X, ALU.max, negate=True))
                    yield
                    need(rest)
                    ve.tensor_tensor(m[:, 0:1], m[:, 4:5], m[:, 5:6], ALU.min).then_inc(sem("att_m"), 1)

                def scale(t):
                    n, h, i = tiles[t]
                    pr = pairs[n]
                    w = pr["keys"](i) * P
                    m = ATT[:, t % 3]
                    dve.wait_ge(sem("att_e"), st["att_e"] + t + 1)
                    den = m[:, 2:3]
                    if pr["sink"] is not None or (pr["bias"] is not None and w > 256):
                        den = m[:, 6:7]
                        total = mark(ve.tensor_tensor(den, m[:, 2:3], m[:, 3:4], ALU.add))
                        yield
                        need(total)
                    inverse = mark(ve.reciprocal(m[:, 7:8], den))
                    yield
                    need(inverse)
                    ve.tensor_scalar(aP[t % 3][:, 0:w], aP[t % 3][:, 0:w], m[:, 7:8], None, ALU.mult).then_inc(
                        sem("att_n"), 1)

                def outputs(n):
                    dve.wait_ge(sem("att_o"), st["att_o"] + 2 * n + 2)
                    ve.tensor_copy(pairs[n]["dst"], stat[n % 2][:, 0:S]).then_inc(sem("att_out"), 1)

                nt = len(tiles)
                for t in range(nt + 5):
                    a_ = maxima(t) if t < nt else iter(())
                    b_ = scale(t - 1) if 0 <= t - 1 < nt else iter(())
                    for _ in range(3):
                        next(a_, None)
                        next(b_, None)
                    if t >= 8 and t % 4 == 0 and t // 4 - 2 < len(pairs):
                        outputs(t // 4 - 2)
                    if "next_proj" in st and t == nt:
                        for c in range(2):
                            rest_cols(st["next_proj"], c)
                if st["mods"] is not None:
                    first, count, _ = st["mods"]
                    lo, hi = 3 * first, 3 * (first + count)
                    flat_mod = MOD[:, :, :, :].rearrange("p l n s -> p (l n) s")
                    b = vec[:, VEC["b_mod"] + lo:VEC["b_mod"] + hi]
                    dve.wait_ge(sem("mod_sum"), st["mod_sum"] + 1)
                    last = ve.tensor_tensor(flat_mod[:, lo:hi, :],
                                            acc[3][:, UC:UC + 2 * (hi - lo)].rearrange("p (n s) -> p n s", s=2),
                                            b.unsqueeze(2).to_broadcast([P, hi - lo, 2]), ALU.add)
                    for scales in (8, 32, 48 + 8, 48 + 32):
                        begin, end = max(lo, scales), min(hi, scales + 8)
                        if begin < end:
                            link(last)
                            m = flat_mod[:, begin:end, :]
                            last = ve.tensor_scalar(m, m, 1.0, None, ALU.add)
                    last.then_inc(sem("mod"), 1)

            def gate_piece(proj_st, c):
                st = proj_st["gate"]
                T = st["T"]
                chunks = gate_chunks(st)
                if c == 0:
                    wait_all(dve, proj_st["gate_in"])
                if c < len(chunks):
                    z, t = chunks[c], gate_tmp(c)
                    dve.wait_ge(sem("g_sq"), st["g_sq"] + c + 1)
                    link(ve.tensor_scalar(t, t, 0.044715, 1.0, ALU.mult, ALU.add))
                    ve.tensor_tensor(t, t, z, ALU.mult).then_inc(sem("g_w"), 1)
                    dve.wait_ge(sem("g_e"), st["g_e"] + c + 1)
                    link(ve.tensor_scalar(t, t, 1.0, None, ALU.add))
                    link(ve.reciprocal(t, t))
                    ve.tensor_tensor(z, z, t, ALU.mult).then_inc(sem("g_z"), 1)
                    dve.wait_ge(sem("g_z"), st["g_z"] + c + 1)
                    return
                for tb in range(T // P):
                    z = ZV[:, tb, :]
                    link(ve.tensor_reduce(LNS[:, tb, 0:1], z, AX.X, ALU.add))
                    link(ve.tensor_scalar(LNS[:, tb, 1:2], LNS[:, tb, 0:1], -1.0 / 256, None, ALU.mult))
                    ve.tensor_scalar(z, z, LNS[:, tb, 1:2], None, ALU.add).then_inc(sem("zc"), 1)
                for tb in range(T // P):
                    dve.wait_ge(sem("zr"), st["zr"] + tb + 1)
                    ve.tensor_scalar(ZV[:, tb, :], ZV[:, tb, :], LNS[:, tb, 4:5], None, ALU.mult).then_inc(
                        sem("zn"), 1)

            def gate_stage(st):
                T, layer = st["T"], st["layer"]
                wait_all(dve, st["ready"])
                dve.wait_ge(sem("load_misc"), 16 * 6)
                for tb in range(T // P):
                    dve.wait_ge(sem("g_mm"), st["g_mm"] + tb + 1)
                    for j in range(2):
                        t = SC[:, 3072 + (2 * tb + j) * P:3072 + (2 * tb + j + 1) * P]
                        link(ve.scalar_tensor_tensor(out=t, in0=acc[tb][:, j * P:(j + 1) * P],
                                                     scalar=v("g_sgu", layer * 2 + j), in1=BS[:, layer, j, :],
                                                     op0=ALU.mult, op1=ALU.add))
                        ve.tensor_tensor(N[:, 3 + j, tb * P:(tb + 1) * P], t, PJ[:, 6 + j, tb * P:(tb + 1) * P],
                                         ALU.mult).then_inc(sem("g_out"), 1)

            def rope_stage(st):
                layer = st["layer"]

                def tiles3(ap):
                    return ap.rearrange("p (i t) -> p i t", t=P)

                for n, (b, s) in enumerate(st["items"]):
                    g = GQ[:, layer:layer + 1] if b < 11 else v("g_k", layer)
                    z = PJ[:, b, s * S:(s + 1) * S]
                    dve.wait_ge(sem("r_rs"), st["r_rs"] + n + 1)
                    if s == 0:
                        ve.scalar_tensor_tensor(out=SC[:, n * S:(n + 1) * S], in0=z, scalar=g, in1=SQ[:, n, :],
                                                op0=ALU.mult, op1=ALU.mult).then_inc(sem("r_y"), 1)
                    elif b == 11:
                        ve.scalar_tensor_tensor(out=z, in0=z, scalar=g, in1=SQ[:, n, :], op0=ALU.mult,
                                                op1=ALU.mult).then_inc(sem("r_out"), 1)
                    else:
                        ve.scalar_tensor_tensor(out=SQ[:, n, :], in0=z, scalar=g, in1=SQ[:, n, :], op0=ALU.mult,
                                                op1=ALU.mult).then_inc(sem("r_y"), 1)
                for n, (b, s) in enumerate(st["items"][:-1]):
                    z = PJ[:, b, s * S:(s + 1) * S]
                    dve.wait_ge(sem("r_y"), st["r_y"] + n + 1)
                    if s == 0:
                        dve.wait_ge(sem("r_rot"), st["r_rot"] + n + 1)
                        y, r_ = SC[:, n * S:(n + 1) * S], SC[:, (4 + n) * S:(5 + n) * S]
                        ve.tensor_tensor(SQ[:, n, :], y, cst("cos"), ALU.mult)
                        link(ve.tensor_tensor(r_, acc[n][:, 0:S], cst("sin"), ALU.mult))
                        out = z if b == 11 else tiles3(z)[:, :, ::-1]
                        p, q = (SQ[:, n, :], r_) if b == 11 else (tiles3(SQ[:, n, :]), tiles3(r_))
                        ve.tensor_tensor(out, p, q, ALU.add).then_inc(sem("r_out"), 1)
                    else:
                        ve.tensor_copy(tiles3(z)[:, :, ::-1], tiles3(SQ[:, n, :])).then_inc(sem("r_out"), 1)

            ve.memset(eps, EPS).then_inc(sem("setup"), 1)
            dve.wait_ge(sem("load_vec"), 16)
            ve.tensor_scalar(GQ, vec[:, VEC["g_q"]:VEC["g_q"] + 2], QSCALE, None, ALU.mult)

            def bias_rows():
                dve.wait_ge(sem("rows"), 1)
                ve.tensor_copy(ROW, stat[1][0:16, 0:384]).then_inc(sem("rows_sb"), 1)

            dve.wait_ge(sem("cond_exp"), 1)
            link(ve.tensor_scalar(CTMP, CTMP, 1.0, None, ALU.add))
            link(ve.reciprocal(CTMP, CTMP))
            link(ve.memset(CS[:, :, :], 0.0))
            ve.tensor_tensor(CS[:, :, 0:2], CTMP.rearrange("p (s k) -> p k s", s=2),
                             vec[:, VEC["cond"]:VEC["cond"] + 16].rearrange("p (s k) -> p k s", s=2),
                             ALU.mult).then_inc(sem("cond"), 1)
            run = dict(norm=norm_stage, ffn=ffn_stage, proj=proj_stage, index=index_stage, attn=attn_stage,
                       gate=gate_stage, rope=rope_stage)
            for n, st in enumerate(stages):
                run[st["kind"]](st)
                if n == 0:
                    bias_rows()


def column_units(w):
    n = w.shape[1]
    u = tiles_cols(n)
    w = np.pad(w, ((0, 0), (0, u * UC - n)))
    return w.reshape(KT, P, u, UC).transpose(2, 1, 0, 3).reshape(u, P, UNIT)


def hidden_units(w1, w3, w2):
    def cols(w):
        return w.reshape(KT, P, FB, P).transpose(2, 1, 0, 3).reshape(FB, P, D)

    return np.concatenate([cols(w1), cols(w3), w2.reshape(FB, P, D)], axis=2)


def columns(v):
    return np.asarray(v).reshape(-1, P).T


def kernel(x, norm_g, final_g, rel_bias_table, ffn_w1, ffn_w3, ffn_w2, hyb_w_in, hyb_cq_g, hyb_wq_b, hyb_wq_idx,
           hyb_w_out, swa_w_in, swa_sinks, swa_w_out, c_2, ctx_2, c_ctx_2, w_mod_2, b_mod_2, w_in_2, rpb_2, w_s_2,
           b_s_2, g_sgu_2, g_q_2, g_k_2, g_out_2, w_o_2, ln1_g_2, ln1_b_2, w_ffn_in_2, w_ffn_out_2, ln2_g_2,
           ln2_b_2):
    import concourse.bacc as bacc
    from concourse.bass_utils import run_bass_kernel_spmd

    swa_cols = np.concatenate([np.r_[j * HD:(j + 1) * HD, (8 + j) * HD:(9 + j) * HD] for j in range(8)])
    gqa_cols = np.concatenate([np.r_[j * HD:(j + 1) * HD, (3 + j) * HD:(4 + j) * HD] for j in range(3)])
    swa_in = np.concatenate([swa_w_in[0][:, swa_cols], swa_w_in[0][:, 1024:]], axis=1)
    even_cols = np.r_[0:1024, 1536:1664, 1664:1792, 1024:1536, 1792:2560, 2816:2944, 2560:2816]
    even_in = np.pad(hyb_w_in[0], ((0, 0), (0, 88)))[:, even_cols]
    in2_cols = np.r_[1152:1280, 1408:1664, 1280:1408, 1664 + gqa_cols, 2048:2176, 0:384, 384:640,
                     768:1152, 2176:2304, 640:768]
    out2_rows = np.r_[0:640, 640 + gqa_cols]

    def feature_major(t):
        return t[0].T.reshape(KT, P, S).transpose(1, 0, 2)

    cq_unit = np.zeros((1, P, UNIT), np.float32)
    cq_unit[0, :, 0:1024] = hyb_wq_b[0].reshape(2, P, 512).transpose(1, 0, 2).reshape(P, 1024)
    cq_unit[0, :, 1024:1536] = hyb_wq_idx[0].reshape(2, P, 256).transpose(1, 0, 2).reshape(P, 512)
    arrays = {
        "x": feature_major(x), "ctx": feature_major(ctx_2),
        "con": constants(), "onehot": bucket_rows(), "table": rel_bias_table,
        "vec": np.concatenate([columns(norm_g), columns(final_g), columns(hyb_cq_g), columns(b_mod_2),
                               columns(g_sgu_2), columns(np.tile(g_q_2, (1, 2))), columns(np.tile(g_k_2, (1, 2))),
                               columns(g_out_2[:, out2_rows]), columns(ln1_g_2), columns(ln1_b_2),
                               columns(ln2_g_2), columns(ln2_b_2), columns(c_2), columns(c_ctx_2)], axis=1),
        "sinks": swa_sinks, "b_s": b_s_2, "w_s": w_s_2.transpose(3, 0, 1, 2),
        "rpb": np.pad(rpb_2[:, :, 4:11, :], ((0, 0), (0, 0), (0, 0), (48, 49))),
        "ffn_units": np.concatenate([hidden_units(ffn_w1[l, f], ffn_w3[l, f], ffn_w2[l, f])
                                     for l in range(2) for f in range(2)]),
        "even_units": np.concatenate([column_units(even_in), cq_unit, column_units(hyb_w_out[0])]),
        "swa_units": np.concatenate([column_units(swa_in), column_units(swa_w_out[0][swa_cols])]),
        "mod_units": np.concatenate([column_units(w_mod_2[l]) for l in range(2)]),
        "mix2_units": np.concatenate([column_units(w) for l in range(2)
                                      for w in (w_in_2[l][:, in2_cols], w_o_2[l][out2_rows])]),
        "ffn2_units": np.concatenate([hidden_units(w_ffn_in_2[l][:, :FF], w_ffn_in_2[l][:, FF:], w_ffn_out_2[l])
                                      for l in range(2)]),
    }
    nc = bacc.Bacc("TRN2", target_bir_lowering=False, num_devices=1)
    inputs, aps = {}, {}
    for name, value in arrays.items():
        value = np.ascontiguousarray(value)
        inputs[f"in_{name}"] = value
        aps[name] = nc.dram_tensor(f"in_{name}", value.shape, mybir.dt.from_np(value.dtype),
                                   kind="ExternalInput").ap()
    aps["out"] = nc.dram_tensor("out_x", (P, KT, S), F32, kind="ExternalOutput").ap()
    build_program(nc, aps)
    r = run_bass_kernel_spmd(nc, [inputs], core_ids=[0])
    out = r.results[0]["out_x"]
    return out.transpose(1, 0, 2).reshape(1, D, S).transpose(0, 2, 1)
```
